# Optimizing a Trainium2 kernel written in Bass

```python
import math
import jax
import jax.numpy as jnp
from jax import lax
import numpy as np
import jax, jax.numpy as jnp

D_MODEL = 1024
BATCH = 1
SEQ = 512
DEPTH = 2

N_EVEN = (DEPTH + 1) // 2
N_ODD = DEPTH // 2
NORM_EPS = 1e-6

SSD_HEAD_DIM = 64
SSD_HEADS = 16
SSD_GROUPS = 2
SSD_HEADS_PER_GROUP = SSD_HEADS // SSD_GROUPS
SSD_STATE = 128
SSD_CHUNK = 128
CONV_WIDTH = 4
D_SSM = SSD_HEADS * SSD_HEAD_DIM
CONV_DIM = D_SSM + 2 * SSD_GROUPS * SSD_STATE

GLA_HEADS = 4
GLA_KEY_DIM = D_MODEL // 2
GLA_VAL_DIM = D_MODEL
GLA_HEAD_K = GLA_KEY_DIM // GLA_HEADS
GLA_HEAD_V = GLA_VAL_DIM // GLA_HEADS
GLA_GATE_RANK = 16
GLA_GATE_NORM = 16.0
GLA_CHUNK = 64

IN_SIZES = (D_SSM, CONV_DIM, SSD_HEADS, GLA_KEY_DIM, GLA_KEY_DIM, GLA_VAL_DIM, GLA_VAL_DIM, GLA_GATE_RANK)
IN_COLS = sum(IN_SIZES)
MIX_WIDTH = D_SSM + GLA_VAL_DIM

MLA_HEADS = 16
MLA_NOPE = 64
MLA_ROPE = 32
MLA_V = 64
MLA_Q_RANK = 384
MLA_KV_RANK = 256
ROPE_THETA = 10000.0
ATTN_BLOCK = 128

FFN_HIDDEN = -(-(8 * D_MODEL) // (3 * 256)) * 256


def _offsets(sizes):
    out, acc = [], 0
    for s in sizes[:-1]:
        acc += s
        out.append(acc)
    return out

def rms_norm(x, w):
    xf = x.astype(jnp.float32)
    y = xf * lax.rsqrt(jnp.mean(xf * xf, axis=-1, keepdims=True) + NORM_EPS)
    return (y * w.astype(jnp.float32)).astype(x.dtype)

def causal_depthwise_conv(x, w, b):
    c = x.shape[-1]
    y = lax.conv_general_dilated(x, w[:, None, :].astype(x.dtype), window_strides=(1,),
                                 padding=[(CONV_WIDTH - 1, 0)],
                                 dimension_numbers=('NWC', 'WIO', 'NWC'),
                                 feature_group_count=c)
    return y + b

def ssd_mixer(z, xbc, dt_raw, conv_w, conv_b, dt_bias, a_log, d_skip, norm_w):
    bsz, seqlen, _ = z.shape
    G, K, P, N, Q = SSD_GROUPS, SSD_HEADS_PER_GROUP, SSD_HEAD_DIM, SSD_STATE, SSD_CHUNK
    nc = seqlen // Q
    xbc = jax.nn.silu(causal_depthwise_conv(xbc, conv_w, conv_b))
    xs, bm, cm = jnp.split(xbc, [D_SSM, D_SSM + G * N], axis=-1)
    xs = xs.reshape(bsz, nc, Q, G, K, P)
    bm = bm.reshape(bsz, nc, Q, G, N)
    cm = cm.reshape(bsz, nc, Q, G, N)
    dt = jax.nn.softplus(dt_raw + dt_bias).reshape(bsz, nc, Q, G, K)
    a = dt * (-jnp.exp(a_log)).reshape(G, K)
    a_cum = jnp.cumsum(a, axis=2)
    xdt = xs * dt[..., None]
    causal = jnp.tril(jnp.ones((Q, Q), dtype=bool))
    seg = a_cum[:, :, :, None] - a_cum[:, :, None, :]
    decay = jnp.exp(jnp.where(causal[:, :, None, None], seg, -jnp.inf))
    cb = jnp.einsum('bclgn,bcsgn->bclsg', cm, bm)
    y_diag = jnp.einsum('bclsg,bclsgk,bcsgkp->bclgkp', cb, decay, xdt)
    to_end = jnp.exp(a_cum[:, :, -1:] - a_cum)
    states = jnp.einsum('bcsgn,bcsgk,bcsgkp->bcgkpn', bm, to_end, xdt)
    chunk_decay = jnp.exp(a_cum[:, :, -1])

    def step(h, inp):
        s_c, d_c = inp
        return h * d_c[..., None, None] + s_c, h

    h0 = jnp.zeros((bsz, G, K, P, N), states.dtype)
    _, prev = lax.scan(step, h0, (jnp.moveaxis(states, 1, 0), jnp.moveaxis(chunk_decay, 1, 0)))
    prev = jnp.moveaxis(prev, 0, 1)
    y_off = jnp.einsum('bclgn,bcgkpn,bclgk->bclgkp', cm, prev, jnp.exp(a_cum))
    y = y_diag + y_off + xs * d_skip.reshape(G, K)[:, :, None]
    y = y.reshape(bsz, seqlen, D_SSM) * jax.nn.silu(z)
    gsz = D_SSM // G
    y = rms_norm(y.reshape(bsz, seqlen, G, gsz), norm_w.reshape(G, gsz))
    return y.reshape(bsz, seqlen, D_SSM)

def gla_mixer(q, k, v, g, gk_low, gk_w2, gk_b, norm_w):
    bsz, seqlen, _ = q.shape
    H, DK, DV, Q = GLA_HEADS, GLA_HEAD_K, GLA_HEAD_V, GLA_CHUNK
    nc = seqlen // Q
    dtype = q.dtype
    gk = jax.nn.log_sigmoid((gk_low @ gk_w2 + gk_b).astype(jnp.float32)) / GLA_GATE_NORM
    gcum = jnp.cumsum(gk.reshape(bsz, nc, Q, H, DK), axis=2)
    g_last = gcum[:, :, -1]
    q = q.reshape(bsz, nc, Q, H, DK) * (DK ** -0.5)
    k = k.reshape(bsz, nc, Q, H, DK)
    v = v.reshape(bsz, nc, Q, H, DV)
    q_dec = q * jnp.exp(gcum).astype(dtype)
    k_inv = k * jnp.exp(-gcum).astype(dtype)
    k_end = k * jnp.exp(g_last[:, :, None] - gcum).astype(dtype)
    causal = jnp.tril(jnp.ones((Q, Q), dtype=bool))
    scores = jnp.where(causal, jnp.einsum('bcihd,bcjhd->bchij', q_dec, k_inv), 0)
    o_intra = jnp.einsum('bchij,bcjhv->bcihv', scores, v)
    chunk_kv = jnp.einsum('bcjhd,bcjhv->bchdv', k_end, v)
    chunk_decay = jnp.exp(g_last).astype(dtype)

    def step(s, inp):
        kv_c, d_c = inp
        return s * d_c[..., None] + kv_c, s

    s0 = jnp.zeros((bsz, H, DK, DV), chunk_kv.dtype)
    _, prev = lax.scan(step, s0, (jnp.moveaxis(chunk_kv, 1, 0), jnp.moveaxis(chunk_decay, 1, 0)))
    prev = jnp.moveaxis(prev, 0, 1)
    o_inter = jnp.einsum('bcihd,bchdv->bcihv', q_dec, prev)
    o = (o_intra + o_inter).reshape(bsz, seqlen, H, DV)
    o = rms_norm(o, norm_w) * jax.nn.silu(g.reshape(bsz, seqlen, H, DV))
    return o.reshape(bsz, seqlen, GLA_VAL_DIM)

def ssd_gla_layer(h, w_in, conv_w, conv_b, dt_bias, a_log, d_skip, ssd_norm,
                  gla_gk_w2, gla_gk_b, gla_norm, w_out):
    bsz, seqlen, _ = h.shape
    proj = h @ w_in
    z, xbc, dt_raw, q, k, v, g, gk_low = jnp.split(proj, _offsets(IN_SIZES), axis=-1)
    y_ssd = ssd_mixer(z, xbc, dt_raw, conv_w, conv_b, dt_bias, a_log, d_skip, ssd_norm)
    y_gla = gla_mixer(q, k, v, g, gk_low, gla_gk_w2, gla_gk_b, gla_norm)
    return jnp.concatenate([y_ssd, y_gla], axis=-1) @ w_out

def rope_tables(seqlen):
    pos = jnp.arange(seqlen, dtype=jnp.float32)
    inv = 1.0 / (ROPE_THETA ** (jnp.arange(0, MLA_ROPE, 2, dtype=jnp.float32) / MLA_ROPE))
    ang = pos[:, None] * inv[None, :]
    return jnp.cos(ang), jnp.sin(ang)

def apply_rope(x, cos, sin):
    x1, x2 = jnp.split(x, 2, axis=-1)
    cos = cos.astype(x.dtype)
    sin = sin.astype(x.dtype)
    return jnp.concatenate([x1 * cos - x2 * sin, x2 * cos + x1 * sin], axis=-1)

def mla_layer(h, w_dqkv, q_lora_norm, w_uq, kv_lora_norm, w_ukv,
              q_nope_norm, q_rope_norm, k_nope_norm, k_rope_norm, w_o):
    bsz, seqlen, _ = h.shape
    H = MLA_HEADS
    cq, ckv, k_rope = jnp.split(h @ w_dqkv, [MLA_Q_RANK, MLA_Q_RANK + MLA_KV_RANK], axis=-1)
    q = (rms_norm(cq, q_lora_norm) @ w_uq).reshape(bsz, seqlen, H, MLA_NOPE + MLA_ROPE)
    q_nope, q_rope = jnp.split(q, [MLA_NOPE], axis=-1)
    kv = (rms_norm(ckv, kv_lora_norm) @ w_ukv).reshape(bsz, seqlen, H, MLA_NOPE + MLA_V)
    k_nope, v = jnp.split(kv, [MLA_NOPE], axis=-1)
    cos, sin = rope_tables(seqlen)
    q_nope = rms_norm(q_nope, q_nope_norm)
    q_rope = apply_rope(rms_norm(q_rope, q_rope_norm), cos[:, None, :], sin[:, None, :])
    k_nope = rms_norm(k_nope, k_nope_norm)
    k_rope = apply_rope(rms_norm(k_rope, k_rope_norm), cos, sin)
    scale = (MLA_NOPE + MLA_ROPE) ** -0.5
    kpos = jnp.arange(seqlen)

    def block(i):
        start = i * ATTN_BLOCK
        qn = lax.dynamic_slice_in_dim(q_nope, start, ATTN_BLOCK, axis=1)
        qr = lax.dynamic_slice_in_dim(q_rope, start, ATTN_BLOCK, axis=1)
        s = jnp.einsum('bqhd,bkhd->bhqk', qn, k_nope) + jnp.einsum('bqhr,bkr->bhqk', qr, k_rope)
        s = s.astype(jnp.float32) * scale
        qpos = start + jnp.arange(ATTN_BLOCK)
        mask = kpos[None, :] <= qpos[:, None]
        p = jax.nn.softmax(jnp.where(mask, s, -jnp.inf), axis=-1).astype(v.dtype)
        return jnp.einsum('bhqk,bkhv->bqhv', p, v)

    o = lax.map(block, jnp.arange(seqlen // ATTN_BLOCK))
    o = jnp.moveaxis(o, 0, 1).reshape(bsz, seqlen, H * MLA_V)
    return o @ w_o

def swiglu(h, w_gate, w_up, w_down):
    return (jax.nn.silu(h @ w_gate) * (h @ w_up)) @ w_down

def first_inputs(seed: int = 0) -> dict:
    key = jax.random.key(seed)
    keys = iter(jax.random.split(key, 40))

    def nrm(shape, scale):
        return jax.random.normal(next(keys), shape, jnp.float32) * scale

    def gain(shape):
        return 1.0 + nrm(shape, 0.02)

    NE, NO = N_EVEN, N_ODD
    x = nrm((BATCH, SEQ, D_MODEL), 1.0)
    u = jax.random.uniform(next(keys), (NE, SSD_HEADS), jnp.float32)
    dt0 = jnp.exp(u * (math.log(0.1) - math.log(0.001)) + math.log(0.001))
    dt_bias = dt0 + jnp.log(-jnp.expm1(-dt0))
    a_log = jnp.log(jax.random.uniform(next(keys), (NE, SSD_HEADS), jnp.float32, 1.0, 16.0))
    return {
        'x': x,
        'mix_norm_even': gain((NE, D_MODEL)),
        'w_in_even': nrm((NE, D_MODEL, IN_COLS), D_MODEL ** -0.5),
        'conv_w': nrm((NE, CONV_WIDTH, CONV_DIM), CONV_WIDTH ** -0.5),
        'conv_b': nrm((NE, CONV_DIM), 0.02),
        'dt_bias': dt_bias,
        'a_log': a_log,
        'd_skip': 1.0 + nrm((NE, SSD_HEADS), 0.1),
        'ssd_norm': gain((NE, D_SSM)),
        'gla_gk_w2': nrm((NE, GLA_GATE_RANK, GLA_KEY_DIM), GLA_GATE_RANK ** -0.5),
        'gla_gk_b': nrm((NE, GLA_KEY_DIM), 0.1),
        'gla_norm': gain((NE, GLA_HEAD_V)),
        'w_out_even': nrm((NE, MIX_WIDTH, D_MODEL), MIX_WIDTH ** -0.5),
        'mix_norm_odd': gain((NO, D_MODEL)),
        'w_dqkv': nrm((NO, D_MODEL, MLA_Q_RANK + MLA_KV_RANK + MLA_ROPE), D_MODEL ** -0.5),
        'q_lora_norm': gain((NO, MLA_Q_RANK)),
        'w_uq': nrm((NO, MLA_Q_RANK, MLA_HEADS * (MLA_NOPE + MLA_ROPE)), MLA_Q_RANK ** -0.5),
        'kv_lora_norm': gain((NO, MLA_KV_RANK)),
        'w_ukv': nrm((NO, MLA_KV_RANK, MLA_HEADS * (MLA_NOPE + MLA_V)), MLA_KV_RANK ** -0.5),
        'q_nope_norm': gain((NO, MLA_NOPE)),
        'q_rope_norm': gain((NO, MLA_ROPE)),
        'k_nope_norm': gain((NO, MLA_NOPE)),
        'k_rope_norm': gain((NO, MLA_ROPE)),
        'w_o_mla': nrm((NO, MLA_HEADS * MLA_V, D_MODEL), (MLA_HEADS * MLA_V) ** -0.5),
        'ffn_norm': gain((DEPTH, D_MODEL)),
        'w_gate': nrm((DEPTH, D_MODEL, FFN_HIDDEN), D_MODEL ** -0.5),
        'w_up': nrm((DEPTH, D_MODEL, FFN_HIDDEN), D_MODEL ** -0.5),
        'w_down': nrm((DEPTH, FFN_HIDDEN, D_MODEL), FFN_HIDDEN ** -0.5),
    }

def first_block(x, mix_norm_even, w_in_even, conv_w, conv_b, dt_bias, a_log, d_skip, ssd_norm,
              gla_gk_w2, gla_gk_b, gla_norm, w_out_even,
              mix_norm_odd, w_dqkv, q_lora_norm, w_uq, kv_lora_norm, w_ukv,
              q_nope_norm, q_rope_norm, k_nope_norm, k_rope_norm, w_o_mla,
              ffn_norm, w_gate, w_up, w_down):
    for i in range(DEPTH):
        j = i // 2
        if i % 2 == 0:
            h = rms_norm(x, mix_norm_even[j])
            x = x + ssd_gla_layer(h, w_in_even[j], conv_w[j], conv_b[j], dt_bias[j], a_log[j],
                                  d_skip[j], ssd_norm[j], gla_gk_w2[j], gla_gk_b[j], gla_norm[j],
                                  w_out_even[j])
        else:
            h = rms_norm(x, mix_norm_odd[j])
            x = x + mla_layer(h, w_dqkv[j], q_lora_norm[j], w_uq[j], kv_lora_norm[j], w_ukv[j],
                              q_nope_norm[j], q_rope_norm[j], k_nope_norm[j], k_rope_norm[j],
                              w_o_mla[j])
        x = x + swiglu(rms_norm(x, ffn_norm[i]), w_gate[i], w_up[i], w_down[i])
    return x


DEPTH_2 = 1

HG_HEADS = 8
HG_DK = 128
HG_DV = 128
HG_CHUNK = 64
RET_HEADS = 4
RET_DK = 256
RET_DV = 512
RET_CHUNK = 128
ROPE_BASE = 10000.0
PEER_HEADS = 8
PEER_NKEYS = 128
PEER_N_EXPERTS = PEER_NKEYS * PEER_NKEYS
PEER_QDIM = 256
PEER_HALF = PEER_QDIM // 2
PEER_TOPK = 16
PEER_BLOCK = 128

IN_SIZES_2 = (HG_HEADS * HG_DK, HG_HEADS * HG_DK, HG_HEADS * HG_DV, HG_HEADS * HG_DV,
            RET_HEADS * RET_DK, RET_HEADS * RET_DK, RET_HEADS * RET_DV, RET_HEADS * RET_DV,
            D_MODEL, D_MODEL)
IN_WIDTH = (2 * HG_HEADS * HG_DK + 2 * HG_HEADS * HG_DV + 2 * RET_HEADS * RET_DK
            + 2 * RET_HEADS * RET_DV + 2 * D_MODEL)


def rmsnorm(x, w):
    xf = x.astype(jnp.float32)
    y = xf * lax.rsqrt(jnp.mean(xf * xf, axis=-1, keepdims=True) + NORM_EPS)
    return (y * w.astype(jnp.float32)).astype(x.dtype)

def head_rms(x):
    return x * lax.rsqrt(jnp.mean(x * x, axis=-1, keepdims=True) + NORM_EPS)

def split_cols(t, sizes):
    outs, start = [], 0
    for n in sizes:
        outs.append(t[..., start:start + n])
        start += n
    return outs

def to_chunks(t, chunk):
    B, S, H, d = t.shape
    return t.reshape(B, S // chunk, chunk, H, d).transpose(1, 0, 3, 2, 4)

def from_chunks(t):
    nc, B, H, C, d = t.shape
    return t.transpose(1, 0, 3, 2, 4).reshape(B, nc * C, H, d)

def hgrn2_mix(q, f_logit, i, lb):
    B, S, _ = q.shape
    f = lb + (1.0 - lb) * jax.nn.sigmoid(f_logit)
    k = 1.0 - f
    logf = jnp.log(f)
    qc = to_chunks((q * HG_DK ** -0.5).reshape(B, S, HG_HEADS, HG_DK), HG_CHUNK)
    kc = to_chunks(k.reshape(B, S, HG_HEADS, HG_DK), HG_CHUNK)
    gc = to_chunks(logf.reshape(B, S, HG_HEADS, HG_DK), HG_CHUNK)
    vc = to_chunks(i.reshape(B, S, HG_HEADS, HG_DV), HG_CHUNK)
    causal = jnp.tril(jnp.ones((HG_CHUNK, HG_CHUNK), dtype=bool))

    def step(state, inp):
        qb, kb, gb, vb = inp
        b = jnp.cumsum(gb, axis=2)
        diff = b[:, :, :, None, :] - b[:, :, None, :, :]
        decay = jnp.exp(jnp.where(causal[:, :, None], diff, -jnp.inf))
        a = jnp.einsum('bhtd,bhsd,bhtsd->bhts', qb, kb, decay)
        o = (jnp.einsum('bhts,bhsv->bhtv', a, vb)
             + jnp.einsum('bhtd,bhdv->bhtv', qb * jnp.exp(b), state))
        b_last = b[:, :, -1:, :]
        state = (jnp.exp(b_last[:, :, 0, :])[..., None] * state
                 + jnp.einsum('bhsd,bhsv->bhdv', kb * jnp.exp(b_last - b), vb))
        return state, o

    s0 = jnp.zeros((B, HG_HEADS, HG_DK, HG_DV), jnp.float32)
    _, o = lax.scan(step, s0, (qc, kc, gc, vc))
    return from_chunks(o)

def rotary(x, pos):
    half = x.shape[-1] // 2
    inv = ROPE_BASE ** (-jnp.arange(half, dtype=jnp.float32) / half)
    ang = pos[:, None] * inv[None, :]
    cos = jnp.cos(ang)[None, :, None, :]
    sin = jnp.sin(ang)[None, :, None, :]
    x1, x2 = x[..., :half], x[..., half:]
    return jnp.concatenate([x1 * cos - x2 * sin, x1 * sin + x2 * cos], axis=-1)

def retention_mix(q, k, v):
    C = RET_CHUNK
    log_g = jnp.log(1.0 - jnp.exp2(-5.0 - jnp.arange(RET_HEADS, dtype=jnp.float32)))
    idx = jnp.arange(C, dtype=jnp.float32)
    rel = idx[:, None] - idx[None, :]
    dmask = jnp.where(rel >= 0, jnp.exp(log_g[:, None, None] * jnp.maximum(rel, 0.0)), 0.0)
    q_decay = jnp.exp(log_g[:, None] * (idx + 1.0))[None, :, :, None]
    k_decay = jnp.exp(log_g[:, None] * (C - 1.0 - idx))[None, :, :, None]
    chunk_decay = jnp.exp(log_g * C)[None, :, None, None]
    qc, kc, vc = to_chunks(q, C), to_chunks(k, C), to_chunks(v, C)

    def step(state, inp):
        qb, kb, vb = inp
        a = jnp.einsum('bhtd,bhsd->bhts', qb, kb) * dmask[None]
        o = (jnp.einsum('bhts,bhsv->bhtv', a, vb)
             + jnp.einsum('bhtd,bhdv->bhtv', qb * q_decay, state))
        state = chunk_decay * state + jnp.einsum('bhsd,bhsv->bhdv', kb * k_decay, vb)
        return state, o

    B = q.shape[0]
    s0 = jnp.zeros((B, RET_HEADS, RET_DK, RET_DV), jnp.float32)
    _, o = lax.scan(step, s0, (qc, kc, vc))
    return from_chunks(o)

def peer_ffn(h, w_q, sub_keys, expert_u, expert_v):
    B, S, D = h.shape
    T = B * S
    ht = h.reshape(T, D)
    q = (ht @ w_q).astype(jnp.float32).reshape(T, PEER_HEADS, 2, PEER_HALF)
    s = jnp.einsum('thpd,hpkd->thpk', q, sub_keys.astype(jnp.float32))
    top_s, top_i = lax.top_k(s, PEER_TOPK)
    cand = top_s[:, :, 0, :, None] + top_s[:, :, 1, None, :]
    cand_idx = top_i[:, :, 0, :, None] * PEER_NKEYS + top_i[:, :, 1, None, :]
    best_s, best_c = lax.top_k(cand.reshape(T, PEER_HEADS, PEER_TOPK * PEER_TOPK), PEER_TOPK)
    expert_idx = jnp.take_along_axis(
        cand_idx.reshape(T, PEER_HEADS, PEER_TOPK * PEER_TOPK), best_c, axis=-1)
    gates = jax.nn.softmax(best_s, axis=-1)
    nb = T // PEER_BLOCK

    def block_fn(args):
        xb, ib, gb = args
        u = jnp.take(expert_u, ib, axis=0)
        act = jax.nn.gelu(jnp.einsum('td,thkd->thk', xb, u).astype(jnp.float32))
        w = (gb * act).astype(xb.dtype)
        v = jnp.take(expert_v, ib, axis=0)
        return jnp.einsum('thk,thkd->td', w, v)

    out = lax.map(block_fn, (ht.reshape(nb, PEER_BLOCK, D),
                             expert_idx.reshape(nb, PEER_BLOCK, PEER_HEADS, PEER_TOPK),
                             gates.reshape(nb, PEER_BLOCK, PEER_HEADS, PEER_TOPK)))
    return out.reshape(B, S, D)

def second_inputs(seed: int = 0) -> dict:
    key = jax.random.key(seed)
    ks = jax.random.split(key, 14)
    f32 = jnp.float32

    def nrm(k, shape, scale):
        return jax.random.normal(k, shape, f32) * scale

    return {
        "x": nrm(ks[0], (BATCH, SEQ, D_MODEL), 1.0),
        "norm_mix_w": 1.0 + nrm(ks[1], (DEPTH_2, D_MODEL), 0.02),
        "w_in": nrm(ks[2], (DEPTH_2, D_MODEL, IN_WIDTH), D_MODEL ** -0.5),
        "hg_lower_bounds": nrm(ks[3], (DEPTH_2 + 1, HG_HEADS * HG_DK), 0.1),
        "hg_norm_w": 1.0 + nrm(ks[4], (DEPTH_2, HG_HEADS * HG_DV), 0.02),
        "w_branch_hg": nrm(ks[5], (DEPTH_2, HG_HEADS * HG_DV, D_MODEL), (HG_HEADS * HG_DV) ** -0.5),
        "w_branch_ret": nrm(ks[6], (DEPTH_2, RET_HEADS * RET_DV, D_MODEL), (RET_HEADS * RET_DV) ** -0.5),
        "w_out": nrm(ks[7], (DEPTH_2, D_MODEL, D_MODEL), D_MODEL ** -0.5),
        "norm_ffn_w": 1.0 + nrm(ks[8], (DEPTH_2, D_MODEL), 0.02),
        "peer_w_q": nrm(ks[9], (DEPTH_2, D_MODEL, PEER_HEADS * PEER_QDIM), D_MODEL ** -0.5),
        "peer_sub_keys": nrm(ks[10], (DEPTH_2, PEER_HEADS, 2, PEER_NKEYS, PEER_HALF), PEER_HALF ** -0.5),
        "expert_u": nrm(ks[11], (DEPTH_2, PEER_N_EXPERTS, D_MODEL), D_MODEL ** -0.5),
        "expert_v": nrm(ks[12], (DEPTH_2, PEER_N_EXPERTS, D_MODEL), PEER_HEADS ** -0.5),
        "final_norm_w": 1.0 + nrm(ks[13], (D_MODEL,), 0.02),
    }

def second_block(x, norm_mix_w, w_in, hg_lower_bounds, hg_norm_w, w_branch_hg, w_branch_ret,
              w_out, norm_ffn_w, peer_w_q, peer_sub_keys, expert_u, expert_v, final_norm_w):
    B, S, _ = x.shape
    f32 = jnp.float32
    lbs = jnp.cumsum(jax.nn.softmax(hg_lower_bounds.astype(f32), axis=0), axis=0)
    pos = jnp.arange(S, dtype=f32)
    for l in range(DEPTH_2):
        h = rmsnorm(x, norm_mix_w[l])
        proj = h @ w_in[l]
        hq, hf, hi, hg, rq, rk, rv, rg, gate_a, gate_b = split_cols(proj, IN_SIZES_2)

        o_hg = hgrn2_mix(hq.astype(f32), hf.astype(f32), hi.astype(f32), lbs[l])
        o_hg = (head_rms(o_hg).reshape(B, S, HG_HEADS * HG_DV) * hg_norm_w[l].astype(f32)
                * jax.nn.silu(hg.astype(f32)))

        q = rotary(rq.astype(f32).reshape(B, S, RET_HEADS, RET_DK), pos)
        k = rotary(rk.astype(f32).reshape(B, S, RET_HEADS, RET_DK), pos) * RET_DK ** -0.5
        v = rv.astype(f32).reshape(B, S, RET_HEADS, RET_DV)
        o_ret = retention_mix(q, k, v)
        o_ret = head_rms(o_ret).reshape(B, S, RET_HEADS * RET_DV) * jax.nn.silu(rg.astype(f32))

        y_hg = o_hg.astype(x.dtype) @ w_branch_hg[l]
        y_ret = o_ret.astype(x.dtype) @ w_branch_ret[l]
        merged = jax.nn.sigmoid(gate_a) * y_hg + jax.nn.sigmoid(gate_b) * y_ret
        x = x + merged @ w_out[l]

        h = rmsnorm(x, norm_ffn_w[l])
        x = x + peer_ffn(h, peer_w_q[l], peer_sub_keys[l], expert_u[l], expert_v[l])
    return rmsnorm(x, final_norm_w)


def setup_inputs(seed=0):
    out = dict(first_inputs(seed))
    for name, value in second_inputs(seed + 1).items():
        if name != "x":
            out[name + "_2"] = value
    return out


def reference(
    x, mix_norm_even, w_in_even, conv_w, conv_b, dt_bias, a_log, d_skip, ssd_norm, gla_gk_w2,
    gla_gk_b, gla_norm, w_out_even, mix_norm_odd, w_dqkv, q_lora_norm, w_uq, kv_lora_norm,
    w_ukv, q_nope_norm, q_rope_norm, k_nope_norm, k_rope_norm, w_o_mla, ffn_norm, w_gate, w_up,
    w_down, norm_mix_w_2, w_in_2, hg_lower_bounds_2, hg_norm_w_2, w_branch_hg_2, w_branch_ret_2,
    w_out_2, norm_ffn_w_2, peer_w_q_2, peer_sub_keys_2, expert_u_2, expert_v_2, final_norm_w_2,
):
    x = first_block(
        x, mix_norm_even, w_in_even, conv_w, conv_b, dt_bias, a_log, d_skip, ssd_norm,
        gla_gk_w2, gla_gk_b, gla_norm, w_out_even, mix_norm_odd, w_dqkv, q_lora_norm, w_uq,
        kv_lora_norm, w_ukv, q_nope_norm, q_rope_norm, k_nope_norm, k_rope_norm, w_o_mla,
        ffn_norm, w_gate, w_up, w_down,
    )
    return second_block(
        x, norm_mix_w_2, w_in_2, hg_lower_bounds_2, hg_norm_w_2, w_branch_hg_2, w_branch_ret_2,
        w_out_2, norm_ffn_w_2, peer_w_q_2, peer_sub_keys_2, expert_u_2, expert_v_2,
        final_norm_w_2,
    )


_drawn_inputs = setup_inputs


def setup_inputs(seed=0):
    import zlib

    import numpy as np

    out = dict(_drawn_inputs(seed))
    spreads = {}
    factors = {'ssd_norm': 2.933,
     'gla_norm': 3.985,
     'mix_norm_odd': 5.926,
     'q_lora_norm': 8.0,
     'kv_lora_norm': 6.973,
     'q_nope_norm': 8.0,
     'q_rope_norm': 8.0,
     'k_nope_norm': 8.0,
     'k_rope_norm': 8.0,
     'norm_mix_w_2': 3.226,
     'hg_norm_w_2': 24.043,
     'norm_ffn_w_2': 27.424,
     'final_norm_w_2': 7.752}
    for name, (base, spread) in spreads.items():
        noise = np.random.default_rng([zlib.crc32(name.encode()), seed]).standard_normal(out[name].shape)
        drawn = base * np.exp(spread * noise) if base else spread * noise
        out[name] = jnp.asarray(drawn.astype(out[name].dtype))
    for name, factor in factors.items():
        out[name] = (out[name] * factor).astype(out[name].dtype)
    return out
```

```python
from contextlib import ExitStack

import numpy as np
import concourse.bass as bass
from concourse import mybir

F32 = mybir.dt.float32
I32 = mybir.dt.int32
U32 = mybir.dt.uint32
ALU = mybir.AluOpType
ACT = mybir.ActivationFunctionType
AX = mybir.AxisListType

P = 128
T = 512
D = 1024
DT = D // P
NCH = T // P
EPS = 1e-6
HID = 2816
HT = HID // P
CONVT = 12
SLOT = 4096


class Tally:

    def __init__(self, nc, ctx, name):
        self.sem = ctx.enter_context(nc.semaphore(name))
        self.base = 0

    def at(self, n):
        return self.base + n

    def close(self, n):
        self.base += n


class Chain:

    def __init__(self, tally, engine):
        self.tally, self.engine, self.n = tally, engine, 0

    def link(self, ins):
        self.n += 1
        ins.then_inc(self.tally.sem, 1)
        self.engine.wait_ge(self.tally.sem, self.tally.at(self.n))

    def close(self):
        self.tally.close(self.n)


def levels():
    return [64, 32, 16, 8, 4, 2, 1]


def const_table():
    f = np.float32
    eye = np.eye(P, dtype=f)
    s = np.arange(P)
    out = {"ident": eye, "ones": np.ones((P, P), f), "tri": (s[:, None] <= s[None, :]).astype(f)}
    out["ones64"] = (s[:, None] // 64 == s[None, :] // 64).astype(f)
    out["ones32"] = (s[:, None] // 32 == s[None, :] // 32).astype(f)
    swap = np.zeros((P, P), f)
    for o in range(P):
        r = o % 32
        swap[o + 16 if r < 16 else o - 16, o] = -1.0 if r < 16 else 1.0
    out["swap"] = swap
    out["future"] = np.where(s[None, :] <= s[:, None], 0.0, -3e38).astype(f)
    keep = np.ones((P, T), f)
    keep[:, ::P] = 0.0
    out["keep"] = keep
    out["iota"] = np.broadcast_to(s.astype(f), (P, P)).copy()
    pos = np.arange(T, dtype=f)
    inv = (f(1.0) / np.power(f(10000.0), np.arange(0, 32, 2, dtype=f) / f(32))).astype(f)
    ang = pos[None, :] * inv[:, None]
    out["mla_cos"] = np.tile(np.cos(ang), (8, 1)).astype(f)
    out["mla_sin"] = np.tile(np.sin(ang), (8, 1)).astype(f)
    inv = np.power(f(10000.0), -np.arange(128, dtype=f) / f(128)).astype(f)
    ang = pos[None, :] * inv[:, None]
    out["ret_cos"] = np.cos(ang).astype(f)
    out["ret_sin"] = np.sin(ang).astype(f)
    for h in range(4):
        log_g = np.log(1.0 - np.exp2(-5.0 - h))
        rel = np.arange(T)[None, :] - s[:, None]
        out[f"ret_decay{h}"] = np.where(rel >= 0, np.exp(log_g * np.maximum(rel, 0)) / 16.0, 0.0).astype(f)
    sel = np.zeros((P, 16 * P), f)
    for h in range(16):
        sel[h, h * P:(h + 1) * P] = 1.0
    out["sel"] = sel
    return out


def level_masks():
    s, t = np.arange(P)[:, None], np.arange(P)[None, :]
    m = [((s // (2 * w) == t // (2 * w)) & (s % (2 * w) < w) & (t % (2 * w) >= w)) for w in levels()]
    return np.concatenate(m, axis=1).astype(np.int32)


CONST_AT, _at = {}, 0
for _k, _v in const_table().items():
    CONST_AT[_k] = (_at, _v.shape[1])
    _at += _v.shape[1]
CONST_W = _at

COL_AT, COL_W = {}, 0
for _k, _n in (("mix_norm_even", 8), ("conv_w", 48), ("conv_b", 12), ("dt_bias", 1), ("a_log", 1), ("d_skip", 8),
               ("ssd_norm", 8), ("gla_gk_b", 4), ("gla_norm", 2), ("mix_norm_odd", 8), ("q_lora_norm", 3),
               ("kv_lora_norm", 2), ("q_nope_norm", 1), ("q_rope_norm", 1), ("k_nope_norm", 1),
               ("k_rope_norm", 1), ("ffn_norm0", 8), ("ffn_norm1", 8), ("norm_mix_w_2", 8), ("lb0", 8),
               ("lb1", 8), ("hg_norm_w_2", 8), ("norm_ffn_w_2", 8), ("final_norm_w_2", 8)):
    COL_AT[_k] = (COL_W, _n)
    COL_W += _n


class Core:

    def __init__(self, nc, ctx, dram):
        self.nc, self.ctx, self.dram, self.n_tensors = nc, ctx, dram, 0
        self.xT = self.sb(ctx, "xT", [P, DT, T])
        self.hT = self.sb(ctx, "hT", [P, DT, T])
        self.ring = self.sb(ctx, "ring", [P, 2, SLOT])
        self.cols = self.sb(ctx, "cols_sb", [P, COL_W])
        self.basic = self.sb(ctx, "basic", [P, 3 * P])
        self.eps = self.sb(ctx, "eps", [P, 1])
        self.ident = self.basic[:, 0:P]
        self.ones = self.basic[:, P:2 * P]
        self.tri = self.basic[:, 2 * P:3 * P]
        self.ps = ctx.enter_context(nc.psum_tensor("ps", [P, 8, T], F32))
        def tally(name):
            return Tally(nc, ctx, name)

        self.loaded = tally("loaded")
        self.slot0_loaded = tally("slot0_loaded")
        self.slot1_loaded = tally("slot1_loaded")
        self.mm_done = tally("mm_done")
        self.bank_free = tally("bank_free")
        self.act_done = tally("act_done")
        self.dve_done = tally("dve_done")
        self.pool_done = tally("pool_done")
        self.stored = tally("stored")
        self.squared = tally("squared")
        self.summed = tally("summed")
        self.log_done = tally("log_done")
        self.rstd_done = tally("rstd_done")
        self.dve_chain = tally("dve_chain")
        self.act_chain = tally("act_chain")
        self.pool_chain = tally("pool_chain")
        self.a_ready = tally("a_ready")
        self.b_ready = tally("b_ready")
        self.c_ready = tally("c_ready")
        self.d_ready = tally("d_ready")
        self.e_ready = tally("e_ready")
        self.f_ready = tally("f_ready")
        self.g_ready = tally("g_ready")
        self.h_ready = tally("h_ready")

    def sb(self, ctx, name, shape, dt=F32):
        self.n_tensors += 1
        return ctx.enter_context(self.nc.sbuf_tensor(f"{name}_{self.n_tensors}", shape, dt))

    def col(self, name, k=0, parts=P):
        return self.cols[0:parts, COL_AT[name][0] + k:COL_AT[name][0] + k + 1]

    def const(self, name):
        at, n = CONST_AT[name]
        return self.dram["consts"][:, at:at + n]


def load(c, pairs):
    with c.nc.Block() as block:
        @block.sync
        def _(sp):
            for dst, src in pairs:
                sp.dma_start(dst, src).then_inc(c.loaded.sem, 16)
            sp.wait_ge(c.loaded.sem, c.loaded.at(16 * len(pairs)))
    c.loaded.close(16 * len(pairs))


def start(c, x_dram):
    at = CONST_AT["ident"][0]
    load(c, [(c.xT[:], x_dram), (c.cols[:], c.dram["cols"]), (c.basic[:], c.dram["consts"][:, at:at + 3 * P])])
    with c.nc.Block() as block:
        @block.vector
        def _(dve):
            dve.memset(c.eps[:], EPS).then_inc(c.dve_done.sem, 1)
            dve.wait_ge(c.dve_done.sem, c.dve_done.at(1))
    c.dve_done.close(1)


def norm(c, groups, tiles, src, dst, width, weight=None, gate=None, ones=None, parts=P):
    n = groups * tiles
    with ExitStack() as ctx:
        sq = c.sb(ctx, "sq", [parts, min(n, 8), T])
        rs = c.sb(ctx, "rs", [parts, groups, T])
        with c.nc.Block() as block:
            @block.scalar
            def _(act):
                for k in range(n):
                    if k >= 8:
                        act.wait_ge(c.summed.sem, c.summed.at(k - 7))
                    act.activation(sq[:, k % 8, :], src(k), ACT.Square).then_inc(c.squared.sem, 1)
                for g in range(groups):
                    act.wait_ge(c.summed.sem, c.summed.at((g + 1) * tiles))
                    act.activation(rs[:, g, :], c.ps[0:parts, g % 8, :], ACT.Ln, bias=c.eps[0:parts, :],
                                   scale=1.0 / width).then_inc(c.log_done.sem, 1)
                for g in range(groups):
                    act.wait_ge(c.log_done.sem, c.log_done.at(g + 1))
                    act.activation(rs[:, g, :], rs[:, g, :], ACT.Exp, scale=-0.5).then_inc(c.rstd_done.sem, 1)

            @block.tensor
            def _(pe):
                for k in range(n):
                    g = k // tiles
                    if g >= 8 and k % tiles == 0:
                        pe.wait_ge(c.log_done.sem, c.log_done.at(g - 7))
                    pe.wait_ge(c.squared.sem, c.squared.at(k + 1))
                    pe.matmul(c.ps[0:parts, g % 8, :], (ones if ones is not None else c.ones)[0:parts, 0:parts],
                              sq[:, k % 8, :], start=k % tiles == 0,
                              stop=k % tiles == tiles - 1).then_inc(c.summed.sem, 1)

            @block.vector
            def _(dve):
                ch = Chain(c.dve_chain, dve)
                for k in range(n):
                    g = k // tiles
                    if k % tiles == 0:
                        dve.wait_ge(c.rstd_done.sem, c.rstd_done.at(g + 1))
                    w = weight(k) if weight else 1.0
                    ch.link(dve.scalar_tensor_tensor(dst(k), src(k), w, rs[:, g, :], ALU.mult, ALU.mult))
                    if gate:
                        ch.link(dve.tensor_tensor(dst(k), dst(k), gate(k), ALU.mult))
                ch.close()
    c.squared.close(n)
    c.summed.close(n)
    c.log_done.close(groups)
    c.rstd_done.close(groups)


def linear(c, w, kt, nb, rhs, dst, add=False):
    width = kt * P

    def slot(r):
        return c.ring[:, r, 0:width]

    loaded = (c.slot0_loaded, c.slot1_loaded)
    pairs, odd = nb // 2, nb % 2
    with c.nc.Block() as block:
        @block.sync
        def _(sp):
            def one(p, r):
                sp.wait_ge(c.bank_free.sem, c.bank_free.at(1) + p * 2 + r)
                sp.dma_start(slot(r), w[bass.ds(p * 2 + r, 1), :, :].rearrange("a p n -> p (a n)")
                             ).then_inc(loaded[r].sem, 16)
            with sp.Fori(0, pairs) as p:
                for r in range(2):
                    one(p, r)
            if odd:
                one(pairs, 0)

        @block.tensor
        def _(pe):
            def one(p, r):
                pe.wait_ge(loaded[r].sem, loaded[r].at(16) + p * 16)
                pe.wait_ge(c.bank_free.sem, c.bank_free.at(1) + p * 2 + r)
                for k in range(kt):
                    mm = pe.matmul(c.ps[:, r, :], slot(r)[:, k * P:(k + 1) * P], rhs(k),
                                   start=k == 0, stop=k == kt - 1)
                mm.then_inc(c.mm_done.sem, 1)
            with pe.Fori(0, pairs) as p:
                for r in range(2):
                    one(p, r)
            if odd:
                one(pairs, 0)

        @block.vector
        def _(dve):
            dve.sem_inc(c.bank_free.sem, 2)

            def one(p, r):
                dve.wait_ge(c.mm_done.sem, c.mm_done.at(1) + p * 2 + r)
                out = dst[:, bass.ds(p * 2 + r, 1), :].rearrange("p a t -> p (a t)")
                if add:
                    ins = dve.tensor_tensor(out, out, c.ps[:, r, :], ALU.add)
                else:
                    ins = dve.tensor_copy(out, c.ps[:, r, :])
                ins.then_inc(c.bank_free.sem, 1)
            with dve.Fori(0, pairs) as p:
                for r in range(2):
                    one(p, r)
            if odd:
                one(pairs, 0)
            dve.wait_ge(c.bank_free.sem, c.bank_free.at(nb + 2))
    c.slot0_loaded.close(16 * (pairs + odd))
    c.slot1_loaded.close(16 * pairs)
    c.mm_done.close(nb)
    c.bank_free.close(nb + 2)


def linear_tokens(c, w, kt, nb, lhs, dst):
    loaded = (c.slot0_loaded, c.slot1_loaded)
    with c.nc.Block() as block:
        @block.sync
        def _(sp):
            with sp.Fori(0, nb // 2) as p:
                for r in range(2):
                    sp.wait_ge(c.bank_free.sem, c.bank_free.at(NCH) + (p * 2 + r) * NCH)
                    sp.dma_start(c.ring[:, r, 0:kt * T], w[bass.ds(p * 2 + r, 1), :, :].rearrange("a p n -> p (a n)")
                                 ).then_inc(loaded[r].sem, 16)

        @block.tensor
        def _(pe):
            with pe.Fori(0, nb // 2) as p:
                for r in range(2):
                    pe.wait_ge(loaded[r].sem, loaded[r].at(16) + p * 16)
                    for t in range(NCH):
                        pe.wait_ge(c.bank_free.sem, c.bank_free.at(1 + t) + (p * 2 + r) * NCH)
                        for k in range(kt):
                            mm = pe.matmul(c.ps[:, 4 * r + t, :], lhs(k)[:, t * P:(t + 1) * P],
                                           c.ring[:, r, k * T:(k + 1) * T], start=k == 0, stop=k == kt - 1)
                        mm.then_inc(c.mm_done.sem, 1)

        @block.vector
        def _(dve):
            dve.sem_inc(c.bank_free.sem, 2 * NCH)
            with dve.Fori(0, nb // 2) as p:
                for r in range(2):
                    for t in range(NCH):
                        dve.wait_ge(c.mm_done.sem, c.mm_done.at(1 + t) + (p * 2 + r) * NCH)
                        dve.tensor_copy(dst[:, t, bass.ds((p * 2 + r) * T, T)], c.ps[:, 4 * r + t, :]
                                        ).then_inc(c.bank_free.sem, 1)
            dve.wait_ge(c.bank_free.sem, c.bank_free.at((nb + 2) * NCH))
    c.slot0_loaded.close(8 * nb)
    c.slot1_loaded.close(8 * nb)
    c.mm_done.close(nb * NCH)
    c.bank_free.close((nb + 2) * NCH)


def conv_silu(c, x):
    with ExitStack() as ctx:
        y = c.sb(ctx, "conv_y", [P, 2, T])
        with c.nc.Block() as block:
            @block.vector
            def _(dve):
                ch = Chain(c.dve_chain, dve)
                for n in range(CONVT):
                    if n >= 2:
                        dve.wait_ge(c.act_done.sem, c.act_done.at(n - 1))
                    ch.link(dve.tensor_scalar(y[:, n % 2, :], x[:, n, :], c.col("conv_w", 4 * n + 3), None, ALU.mult))
                    for back in range(1, 4):
                        part = y[:, n % 2, back:T]
                        ch.link(dve.scalar_tensor_tensor(part, x[:, n, 0:T - back], c.col("conv_w", 4 * n + 3 - back),
                                                         part, ALU.mult, ALU.add))
                    dve.sem_inc(c.dve_done.sem, 1)
                ch.close()

            @block.scalar
            def _(act):
                for n in range(CONVT):
                    act.wait_ge(c.dve_done.sem, c.dve_done.at(n + 1))
                    act.activation(x[:, n, :], y[:, n % 2, :], ACT.Silu, bias=c.col("conv_b", n)
                                   ).then_inc(c.act_done.sem, 1)
    c.dve_done.close(CONVT)
    c.act_done.close(CONVT)


NH, NG = 16, 2
OFF = [0, 512, 896, 1152]
WID = 1280


def ssd(c, z, xbc, small, out):
    nc = c.nc
    xs = lambda k: xbc[:, k, :]
    Bf = lambda g: xbc[:, 8 + g, :]
    Cf = lambda g: xbc[:, 10 + g, :]
    with ExitStack() as ctx:
        sel = c.sb(ctx, "sel", [NH, NH * P])
        dt = c.sb(ctx, "dt", [NH, T])
        a = c.sb(ctx, "a", [NH, T])
        lin = c.sb(ctx, "dt_lin", [NH, T])
        one = c.sb(ctx, "one_row", [NH, T])
        ea = c.sb(ctx, "exp_a_log", [NH, 1])
        acum = c.sb(ctx, "acum", [NH, NCH, T])
        dtT = c.sb(ctx, "dtT", [P, NCH, NH])
        negT = c.sb(ctx, "neg_acumT", [P, NCH, NH])
        xdt = c.sb(ctx, "xdt", [P, NCH, D])
        cbm = c.sb(ctx, "cbm", [P, NG, WID])
        diag = c.sb(ctx, "seg_diag", [P, 2, P])
        E = c.sb(ctx, "decay", [P, 2, T])
        M = c.sb(ctx, "weights_st", [P, 2, T])
        load(c, [(sel[:], c.const("sel")[0:NH, :])])
        with nc.Block() as block:
            @block.scalar
            def _(act):
                ch = Chain(c.act_chain, act)
                ch.link(act.activation(dt[:], small[0:NH, :], ACT.Abs, bias=c.col("dt_bias", 0, NH)))
                ch.link(act.activation(dt[:], dt[:], ACT.Exp, scale=-1.0))
                act.activation(ea[:], c.col("a_log", 0, NH), ACT.Exp).then_inc(c.act_done.sem, 1)
                act.activation(dt[:], dt[:], ACT.Ln, bias=1.0).then_inc(c.act_done.sem, 1)
                ch.close()

            @block.gpsimd
            def _(pool):
                pool.memset(one[:], 1.0).then_inc(c.pool_done.sem, 1)

            @block.vector
            def _(dve):
                ch = Chain(c.dve_chain, dve)
                ch.link(dve.tensor_scalar(lin[:], small[0:NH, :], c.col("dt_bias", 0, NH), 0.0, ALU.add, ALU.max))
                dve.wait_ge(c.act_done.sem, c.act_done.at(2))
                ch.link(dve.tensor_tensor(dt[:], dt[:], lin[:], ALU.add))
                ch.link(dve.tensor_scalar(a[:], dt[:], ea[:], -1.0, ALU.mult, ALU.mult))
                dve.wait_ge(c.pool_done.sem, c.pool_done.at(1))
                for j in range(NCH):
                    dve.tensor_tensor_scan(acum[:, j, j * P:T], one[:, j * P:T], a[:, j * P:T], 0.0,
                                           ALU.mult, ALU.add).then_inc(c.dve_done.sem, 1)
                dve.wait_ge(c.mm_done.sem, c.mm_done.at(2 * NCH))
                for j in range(NCH):
                    ch.link(dve.tensor_copy(dtT[:, j, :], c.ps[:, 0, 32 * j:32 * j + NH]))
                    ch.link(dve.tensor_scalar(negT[:, j, :], c.ps[:, 1, 32 * j:32 * j + NH], -1.0, None, ALU.mult))
                for j in range(NCH):
                    for f in range(2):
                        n = 2 * j + f
                        dve.wait_ge(c.a_ready.sem, c.a_ready.at(n + 1))
                        dve.tensor_tensor(xdt[:, j, f * T:(f + 1) * T].rearrange("p (h d) -> p h d", d=64),
                                          c.ps[:, 2 + n % 2, :].rearrange("p (h d) -> p h d", d=64),
                                          dtT[:, j, 8 * f:8 * f + 8].unsqueeze(2).broadcast_to([P, 8, 64]),
                                          ALU.mult).then_inc(c.b_ready.sem, 1)
                for g in range(NG):
                    for j in range(NCH):
                        n = NCH * g + j
                        dve.wait_ge(c.c_ready.sem, c.c_ready.at(n + 1))
                        dve.tensor_tensor(cbm[:, g, OFF[j]:OFF[j] + P], c.ps[:, 4 + n % 2, 0:P], c.tri, ALU.mult
                                          ).then_inc(c.d_ready.sem, 1)
                        if j < 3:
                            ch.link(dve.tensor_copy(cbm[:, g, OFF[j] + P:OFF[j] + T - j * P],
                                                    c.ps[:, 4 + n % 2, P:T - j * P]))
                        dve.sem_inc(c.d_ready.sem, 1)
                dve.wait_ge(c.b_ready.sem, c.b_ready.at(8))
                dve.wait_ge(c.d_ready.sem, c.d_ready.at(16))
                ch.close()

            @block.tensor
            def _(pe):
                pe.wait_ge(c.dve_done.sem, c.dve_done.at(NCH))
                for j in range(NCH):
                    pe.transpose(c.ps[:, 0, 32 * j:32 * j + NH], dt[:, j * P:(j + 1) * P],
                                 c.ident[0:NH, 0:NH]).then_inc(c.mm_done.sem, 1)
                    pe.transpose(c.ps[:, 1, 32 * j:32 * j + NH], acum[:, j, j * P:(j + 1) * P],
                                 c.ident[0:NH, 0:NH]).then_inc(c.mm_done.sem, 1)
                for j in range(NCH):
                    for f in range(2):
                        n = 2 * j + f
                        if n >= 2:
                            pe.wait_ge(c.b_ready.sem, c.b_ready.at(n - 1))
                        for q in range(4):
                            mm = pe.transpose(c.ps[:, 2 + n % 2, q * P:(q + 1) * P],
                                              xs(4 * f + q)[:, j * P:(j + 1) * P], c.ident)
                        mm.then_inc(c.a_ready.sem, 1)
                for g in range(NG):
                    for j in range(NCH):
                        n = NCH * g + j
                        if n >= 2:
                            pe.wait_ge(c.d_ready.sem, c.d_ready.at(2 * (n - 1)))
                        pe.matmul(c.ps[:, 4 + n % 2, 0:T - j * P], Bf(g)[:, j * P:(j + 1) * P], Cf(g)[:, j * P:T],
                                  start=True, stop=True).then_inc(c.c_ready.sem, 1)
        c.act_done.close(2)
        c.pool_done.close(1)
        c.dve_done.close(NCH)
        c.mm_done.close(8)
        c.a_ready.close(8)
        c.b_ready.close(8)
        c.c_ready.close(8)
        c.d_ready.close(16)
        steps = [(h, j) for h in range(NH) for j in range(NCH)]
        with nc.Block() as block:
            @block.tensor
            def _(pe):
                def spread(n):
                    h, j = steps[n]
                    if n >= 2:
                        pe.wait_ge(c.a_ready.sem, c.a_ready.at(n - 1))
                        pe.wait_ge(c.act_done.sem, c.act_done.at(n - 1))
                    pe.matmul(c.ps[:, n % 2, 0:T - j * P], sel[:, h * P:(h + 1) * P], acum[:, j, j * P:T],
                              start=True, stop=True).then_inc(c.mm_done.sem, 1)
                spread(0)
                for n, (h, j) in enumerate(steps):
                    if n + 1 < len(steps):
                        spread(n + 1)
                    if j == 0 and h % 2 == 0 and h >= 4:
                        pe.wait_ge(c.c_ready.sem, c.c_ready.at(h // 2 - 1))
                    pe.wait_ge(c.b_ready.sem, c.b_ready.at(n + 1))
                    p0 = 64 * (h % 2)
                    mm = pe.matmul(c.ps[p0:p0 + 64, 2 + (h // 2) % 2, j * P:T], xdt[:, j, 64 * h:64 * h + 64],
                                   M[:, n % 2, 0:T - j * P], start=j == 0, stop=j == NCH - 1)
                    mm.then_inc(c.d_ready.sem, 1)

            @block.scalar
            def _(act):
                for n, (h, j) in enumerate(steps):
                    if n >= 2:
                        act.wait_ge(c.b_ready.sem, c.b_ready.at(n - 1))
                    act.wait_ge(c.mm_done.sem, c.mm_done.at(n + 1))
                    act.wait_ge(c.a_ready.sem, c.a_ready.at(n + 1))
                    if j < 3:
                        act.activation(E[:, n % 2, P:T - j * P], c.ps[:, n % 2, P:T - j * P], ACT.Exp,
                                       bias=negT[:, j, h:h + 1]).then_inc(c.e_ready.sem, 1)
                    act.activation(E[:, n % 2, 0:P], diag[:, n % 2, :], ACT.Exp).then_inc(c.act_done.sem, 1)

            @block.vector
            def _(dve):
                def seg(n):
                    h, j = steps[n]
                    dve.wait_ge(c.mm_done.sem, c.mm_done.at(n + 1))
                    if n >= 2:
                        dve.wait_ge(c.act_done.sem, c.act_done.at(n - 1))
                    dve.tensor_scalar(diag[:, n % 2, :], c.ps[:, n % 2, 0:P], negT[:, j, h:h + 1], 0.0,
                                      ALU.add, ALU.min).then_inc(c.a_ready.sem, 1)
                seg(0)
                for n, (h, j) in enumerate(steps):
                    if n + 1 < len(steps):
                        seg(n + 1)
                    dve.wait_ge(c.act_done.sem, c.act_done.at(n + 1))
                    if j < 3:
                        dve.wait_ge(c.e_ready.sem, c.e_ready.at(3 * h + j + 1))
                    if n >= 2:
                        dve.wait_ge(c.d_ready.sem, c.d_ready.at(n - 1))
                    dve.tensor_tensor(M[:, n % 2, 0:T - j * P], E[:, n % 2, 0:T - j * P],
                                      cbm[:, h // 8, OFF[j]:OFF[j] + T - j * P], ALU.mult).then_inc(c.b_ready.sem, 1)
                    if j == NCH - 1 and h % 2 == 1:
                        k = h // 2
                        dve.wait_ge(c.d_ready.sem, c.d_ready.at(n + 1))
                        dve.scalar_tensor_tensor(out[:, k, :], xs(k), c.col("d_skip", k),
                                                 c.ps[:, 2 + k % 2, :], ALU.mult, ALU.add).then_inc(c.c_ready.sem, 1)
                dve.wait_ge(c.c_ready.sem, c.c_ready.at(NH // 2))
        ns = len(steps)
        c.mm_done.close(ns)
        c.a_ready.close(ns)
        c.b_ready.close(ns)
        c.act_done.close(ns)
        c.e_ready.close(3 * NH)
        c.d_ready.close(ns)
        c.c_ready.close(NH // 2)
        with nc.Block() as block:
            @block.scalar
            def _(act):
                for k in range(DT):
                    act.activation(z[:, k, :], z[:, k, :], ACT.Silu).then_inc(c.act_done.sem, 1)

            @block.vector
            def _(dve):
                for k in range(DT):
                    dve.wait_ge(c.act_done.sem, c.act_done.at(k + 1))
                    dve.tensor_tensor(out[:, k, :], out[:, k, :], z[:, k, :], ALU.mult).then_inc(c.dve_done.sem, 1)
                dve.wait_ge(c.dve_done.sem, c.dve_done.at(DT))
        c.act_done.close(DT)
        c.dve_done.close(DT)


def silu_tiles(c, x, n):
    with c.nc.Block() as block:
        @block.scalar
        def _(act):
            for k in range(n):
                act.activation(x[:, k, :], x[:, k, :], ACT.Silu).then_inc(c.act_done.sem, 1)
            act.wait_ge(c.act_done.sem, c.act_done.at(n))
    c.act_done.close(n)


def gated_linear(c, tag, heads, vt, q, k, B, v, out):
    nc = c.nc
    lv = levels()
    NL = len(lv)
    W = vt * P
    items = [(h, l) for h in range(heads) for l in range(NL)]
    with ExitStack() as ctx:
        mask = c.sb(ctx, tag + "mask", [P, NL * P], I32)
        A = c.sb(ctx, tag + "A", [P, 2, T])
        E = c.sb(ctx, tag + "E", [P, 2, T])
        M = c.sb(ctx, tag + "M", [P, 2, T])
        kend = c.sb(ctx, tag + "kend", [P, T])
        kendT = c.sb(ctx, tag + "kendT", [P, T])
        Ed = c.sb(ctx, tag + "Ed", [P, T])
        dec = c.sb(ctx, tag + "dec", [P, NCH])
        S = c.sb(ctx, tag + "S", [P, 3, W])
        load(c, [(mask[:], c.dram["level_masks"])])
        with nc.Block() as block:
            @block.scalar
            def _(act):
                ch = Chain(c.act_chain, act)
                for n, (h, l) in enumerate(items):
                    act.wait_ge(c.a_ready.sem, c.a_ready.at(n + 1))
                    ch.link(act.activation(E[:, n % 2, :], E[:, n % 2, :], ACT.Abs))
                    act.activation(E[:, n % 2, :], E[:, n % 2, :], ACT.Exp, scale=-1.0).then_inc(c.b_ready.sem, 1)
                    if l == NL - 1:
                        if h >= 1:
                            act.wait_ge(c.f_ready.sem, c.f_ready.at(3 * h - 2 + 1))
                        act.activation(Ed[:], B(h), ACT.Exp).then_inc(c.e_ready.sem, 1)
                        act.activation(dec[:], B(h)[:, P - 1:T:P], ACT.Exp).then_inc(c.e_ready.sem, 1)
                        act.wait_ge(c.f_ready.sem, c.f_ready.at(3 * h + 1))
                        act.activation(kend[:], kend[:], ACT.Exp).then_inc(c.e_ready.sem, 1)
                ch.close()

            @block.vector
            def _(dve):
                ch = Chain(c.dve_chain, dve)

                def sub(n):
                    h, l = items[n]
                    w = lv[l]
                    if n >= 2:
                        dve.wait_ge(c.c_ready.sem, c.c_ready.at(n - 1))
                        dve.wait_ge(c.d_ready.sem, c.d_ready.at(n - 1))
                    b = B(h).rearrange("p (n w) -> p n w", w=2 * w)
                    dve.tensor_tensor(E[:, n % 2, :].rearrange("p (n w) -> p n w", w=2 * w), b,
                                      b[:, :, w - 1:w].broadcast_to([P, T // (2 * w), 2 * w]),
                                      ALU.subtract).then_inc(c.a_ready.sem, 1)
                sub(0)
                for n, (h, l) in enumerate(items):
                    w = lv[l]
                    if n + 1 < len(items):
                        sub(n + 1)
                    if l == 0:
                        dve.wait_ge(c.h_ready.sem, c.h_ready.at(h + 1))
                        if h >= 2:
                            dve.wait_ge(c.g_ready.sem, c.g_ready.at(h - 1))
                        ch.link(dve.tensor_tensor(A[:, h % 2, :].rearrange("p (n t) -> p n t", t=P),
                                                  c.ps[:, 2, :].rearrange("p (n t) -> p n t", t=P),
                                                  c.ident.unsqueeze(1).broadcast_to([P, NCH, P]), ALU.mult))
                    dve.wait_ge(c.b_ready.sem, c.b_ready.at(n + 1))
                    if n >= 2:
                        dve.wait_ge(c.mm_done.sem, c.mm_done.at(n - 1))
                    vw = lambda t: t.rearrange("p (n w) -> p n w", w=2 * w)[:, :, w:2 * w]
                    dve.tensor_tensor(vw(M[:, n % 2, :]), vw(q(h)), vw(E[:, n % 2, :]), ALU.mult
                                      ).then_inc(c.c_ready.sem, 1)
                    dve.wait_ge(c.mm_done.sem, c.mm_done.at(n + 1))
                    ch.link(dve.copy_predicated(A[:, h % 2, :].rearrange("p (n t) -> p n t", t=P),
                                                mask[:, l * P:(l + 1) * P].unsqueeze(1).broadcast_to([P, NCH, P]),
                                                c.ps[:, n % 2, :].rearrange("p (n t) -> p n t", t=P)))
                    dve.sem_inc(c.dve_done.sem, 1)
                    if l < NL - 1:
                        continue
                    if h >= 1:
                        dve.wait_ge(c.summed.sem, c.summed.at(h))
                    b4 = B(h).rearrange("p (n w) -> p n w", w=P)
                    dve.tensor_tensor(kend[:].rearrange("p (n w) -> p n w", w=P),
                                      b4[:, :, P - 1:P].broadcast_to([P, NCH, P]), b4, ALU.subtract
                                      ).then_inc(c.f_ready.sem, 1)
                    dve.wait_ge(c.e_ready.sem, c.e_ready.at(3 * h + 2))
                    dve.tensor_tensor(q(h), q(h), Ed[:], ALU.mult).then_inc(c.f_ready.sem, 1)
                    dve.wait_ge(c.e_ready.sem, c.e_ready.at(3 * h + 3))
                    dve.tensor_tensor(kend[:], kend[:], k(h), ALU.mult).then_inc(c.f_ready.sem, 1)
                    dve.wait_ge(c.summed.sem, c.summed.at(h + 1))
                    if h >= 1:
                        dve.wait_ge(c.g_ready.sem, c.g_ready.at(h))
                    dve.tensor_copy(kendT[:], c.ps[:, 3, :]).then_inc(c.log_done.sem, 1)
                    for j in range(3):
                        dve.wait_ge(c.rstd_done.sem, c.rstd_done.at(3 * h + j + 1))
                        if j == 0:
                            ch.link(dve.tensor_copy(S[:, 0, :], c.ps[:, 4, 0:W]))
                        else:
                            ch.link(dve.scalar_tensor_tensor(S[:, j, :], S[:, j - 1, :], dec[:, j:j + 1],
                                                             c.ps[:, 4, 0:W], ALU.mult, ALU.add))
                        dve.sem_inc(c.squared.sem, 1)
                    dve.wait_ge(c.g_ready.sem, c.g_ready.at(h + 1))
                    for x in range(vt):
                        dve.tensor_copy(out(h * vt + x), c.ps[:, 5 + x, :]).then_inc(c.bank_free.sem, 1)
                dve.wait_ge(c.bank_free.sem, c.bank_free.at(heads * vt))
                ch.close()

            @block.gpsimd
            def _(pool):
                for n, (h, l) in enumerate(items):
                    w = lv[l]
                    pool.wait_ge(c.b_ready.sem, c.b_ready.at(n + 1))
                    if n >= 2:
                        pool.wait_ge(c.mm_done.sem, c.mm_done.at(n - 1))
                    vw = lambda t: t.rearrange("p (n w) -> p n w", w=2 * w)[:, :, 0:w]
                    pool.tensor_tensor(vw(M[:, n % 2, :]), vw(k(h)), vw(E[:, n % 2, :]), ALU.mult
                                       ).then_inc(c.d_ready.sem, 1)

            @block.tensor
            def _(pe):
                def cut(x, j):
                    return x[:, j * P:(j + 1) * P]
                for n, (h, l) in enumerate(items):
                    if l == 0:
                        if h >= 1:
                            pe.wait_ge(c.dve_done.sem, c.dve_done.at(n))
                        for j in range(NCH):
                            mm = pe.matmul(cut(c.ps[:, 2, :], j), cut(k(h), j), cut(q(h), j), start=True, stop=True)
                        mm.then_inc(c.h_ready.sem, 1)
                    if n >= 2:
                        pe.wait_ge(c.dve_done.sem, c.dve_done.at(n - 1))
                    pe.wait_ge(c.c_ready.sem, c.c_ready.at(n + 1))
                    pe.wait_ge(c.d_ready.sem, c.d_ready.at(n + 1))
                    for j in range(NCH):
                        mm = pe.matmul(cut(c.ps[:, n % 2, :], j), cut(M[:, n % 2, :], j), cut(M[:, n % 2, :], j),
                                       start=True, stop=True)
                    mm.then_inc(c.mm_done.sem, 1)
                    if l < NL - 1:
                        continue
                    pe.wait_ge(c.f_ready.sem, c.f_ready.at(3 * h + 3))
                    for j in range(NCH):
                        mm = pe.transpose(cut(c.ps[:, 3, :], j), cut(kend, j), c.ident)
                    mm.then_inc(c.summed.sem, 1)
                    pe.wait_ge(c.log_done.sem, c.log_done.at(h + 1))
                    for j in range(3):
                        if j:
                            pe.wait_ge(c.squared.sem, c.squared.at(3 * h + j))
                        pe.matmul(c.ps[:, 4, 0:W], cut(kendT, j), v(j)[:, h * W:(h + 1) * W],
                                  start=True, stop=True).then_inc(c.rstd_done.sem, 1)
                    pe.wait_ge(c.dve_done.sem, c.dve_done.at(n + 1))
                    pe.wait_ge(c.squared.sem, c.squared.at(3 * h + 3))
                    if h >= 1:
                        pe.wait_ge(c.bank_free.sem, c.bank_free.at(h * vt))
                    for x in range(vt):
                        for j in range(NCH):
                            o = cut(c.ps[:, 5 + x, :], j)
                            mm = pe.matmul(o, v(j)[:, h * W + x * P:h * W + (x + 1) * P], cut(A[:, h % 2, :], j),
                                           start=True, stop=j == 0)
                            if j:
                                mm = pe.matmul(o, S[:, j - 1, x * P:(x + 1) * P], cut(q(h), j),
                                               start=False, stop=True)
                    mm.then_inc(c.g_ready.sem, 1)
    ni = len(items)
    for t, n in ((c.a_ready, ni), (c.b_ready, ni), (c.c_ready, ni), (c.d_ready, ni), (c.mm_done, ni),
                 (c.dve_done, ni), (c.h_ready, heads), (c.g_ready, heads), (c.f_ready, 3 * heads),
                 (c.e_ready, 3 * heads), (c.summed, heads), (c.log_done, heads), (c.rstd_done, 3 * heads),
                 (c.squared, 3 * heads), (c.bank_free, heads * vt)):
        t.close(n)


def gla_gates(c, small, w2, B):
    with ExitStack() as ctx:
        keep = c.sb(ctx, "keep", [P, T])
        curve = c.sb(ctx, "curve", [P, 4, T])
        nb = c.sb(ctx, "gk_sum", [P, 4, T])
        w2s = c.sb(ctx, "w2s", [48, T])
        load(c, [(keep[:], c.const("keep")), (w2s[32:48, :], w2)])
        with c.nc.Block() as block:
            @block.tensor
            def _(pe):
                for m in range(4):
                    pe.matmul(c.ps[:, m, :], w2s[32:48, m * P:(m + 1) * P], small[32:48, :],
                              start=True, stop=True).then_inc(c.mm_done.sem, 1)

            @block.scalar
            def _(act):
                ch = Chain(c.act_chain, act)
                for m in range(4):
                    act.wait_ge(c.mm_done.sem, c.mm_done.at(m + 1))
                    act.activation(curve[:, m, :], c.ps[:, m, :], ACT.Abs, bias=c.col("gla_gk_b", m)
                                   ).then_inc(c.a_ready.sem, 1)
                act.wait_ge(c.a_ready.sem, c.a_ready.at(4))
                for m in range(4):
                    ch.link(act.activation(curve[:, m, :], curve[:, m, :], ACT.Exp, scale=-1.0))
                for m in range(4):
                    act.activation(curve[:, m, :], curve[:, m, :], ACT.Ln, bias=1.0).then_inc(c.act_done.sem, 1)
                ch.close()

            @block.vector
            def _(dve):
                ch = Chain(c.dve_chain, dve)
                for m in range(4):
                    dve.wait_ge(c.a_ready.sem, c.a_ready.at(m + 1))
                    ch.link(dve.tensor_scalar(nb[:, m, :], c.ps[:, m, :], c.col("gla_gk_b", m), 0.0,
                                              ALU.add, ALU.min))
                    dve.wait_ge(c.act_done.sem, c.act_done.at(m + 1))
                    ch.link(dve.tensor_tensor(nb[:, m, :], nb[:, m, :], curve[:, m, :], ALU.subtract))
                    ch.link(dve.tensor_scalar(nb[:, m, :], nb[:, m, :], 1.0 / 16.0, None, ALU.mult))
                    ch.link(dve.tensor_tensor_scan(B[:, m, :], keep[:], nb[:, m, :], 0.0, ALU.mult, ALU.add))
                ch.close()
    c.mm_done.close(4)
    c.a_ready.close(4)
    c.act_done.close(4)


def scale_tiles(c, x, n, factor):
    with c.nc.Block() as block:
        @block.vector
        def _(dve):
            dve.tensor_scalar(x[:, 0:n, :], x[:, 0:n, :], factor, None, ALU.mult).then_inc(c.dve_done.sem, 1)
            dve.wait_ge(c.dve_done.sem, c.dve_done.at(1))
    c.dve_done.close(1)


def even_layer(c):
    d = c.dram
    x, h = (lambda k: c.xT[:, k, :]), (lambda k: c.hT[:, k, :])
    norm(c, 1, DT, x, h, D, weight=lambda k: c.col("mix_norm_even", k))
    with ExitStack() as ctx:
        proj = c.sb(ctx, "proj", [P, 37, T])
        linear(c, d["w_even"], DT, 37, h, proj)
        z, xbc, small = proj[:, 0:8, :], proj[:, 8:20, :], proj[:, 36, :]
        q, k, g = proj[:, 20:24, :], proj[:, 24:28, :], proj[:, 28:36, :]
        conv_silu(c, xbc)
        y_ssd, y_gla = xbc[:, 0:8, :], z
        ssd(c, z, xbc, small, y_ssd)
        norm(c, 2, 4, lambda t: y_ssd[:, t, :], lambda t: y_ssd[:, t, :], 512,
             weight=lambda t: c.col("ssd_norm", t))
        B = xbc[:, 8:12, :]
        v = c.sb(ctx, "v", [P, NCH, D])
        linear_tokens(c, d["w_v_even"], DT, 2, h, v)
        scale_tiles(c, q, 4, 128.0 ** -0.5)
        gla_gates(c, small, d["gla_gk_w2"], B)
        silu_tiles(c, g, 8)
        gated_linear(c, "gla_", 4, 2, lambda i: q[:, i, :], lambda i: k[:, i, :], lambda i: B[:, i, :],
                     lambda j: v[:, j, :], lambda i: y_gla[:, i, :])
        norm(c, 4, 2, lambda t: y_gla[:, t, :], lambda t: y_gla[:, t, :], 256,
             weight=lambda t: c.col("gla_norm", t % 2), gate=lambda t: g[:, t, :])
        linear(c, d["w_out_even"], 16, DT, lambda t: y_ssd[:, t, :] if t < 8 else y_gla[:, t - 8, :], c.xT, add=True)


def swiglu(c, layer):
    d = c.dram
    x, h = (lambda k: c.xT[:, k, :]), (lambda k: c.hT[:, k, :])
    norm(c, 1, DT, x, h, D, weight=lambda k: c.col(f"ffn_norm{layer}", k))
    wgu = d["w_gate_up"]
    with ExitStack() as ctx:
        hid = c.sb(ctx, f"hid{layer}", [P, HT, T])
        gate = c.sb(ctx, f"gate{layer}", [P, 2, T])
        loaded = (c.slot0_loaded, c.slot1_loaded)
        with c.nc.Block() as block:
            @block.sync
            def _(sp):
                with sp.Fori(0, HT // 2) as p:
                    for r in range(2):
                        sp.wait_ge(c.bank_free.sem, c.bank_free.at(1) + p * 2 + r)
                        sp.dma_start(c.ring[:, r, 0:2 * D], wgu[layer, bass.ds(p * 2 + r, 1), :, :]
                                     .rearrange("a p n -> p (a n)")).then_inc(loaded[r].sem, 16)

            @block.tensor
            def _(pe):
                with pe.Fori(0, HT // 2) as p:
                    for r in range(2):
                        pe.wait_ge(loaded[r].sem, loaded[r].at(16) + p * 16)
                        pe.wait_ge(c.bank_free.sem, c.bank_free.at(1) + p * 2 + r)
                        for u in range(2):
                            for k in range(DT):
                                mm = pe.matmul(c.ps[:, 2 * r + u, :], c.ring[:, r, u * D + k * P:u * D + (k + 1) * P],
                                               h(k), start=k == 0, stop=k == DT - 1)
                            mm.then_inc(c.mm_done.sem, 1)

            @block.scalar
            def _(act):
                with act.Fori(0, HT // 2) as p:
                    for r in range(2):
                        act.wait_ge(c.mm_done.sem, c.mm_done.at(1) + (p * 2 + r) * 2)
                        act.wait_ge(c.bank_free.sem, c.bank_free.at(1) + p * 2 + r)
                        act.activation(gate[:, r, :], c.ps[:, 2 * r, :], ACT.Silu).then_inc(c.act_done.sem, 1)

            @block.vector
            def _(dve):
                dve.sem_inc(c.bank_free.sem, 2)
                with dve.Fori(0, HT // 2) as p:
                    for r in range(2):
                        dve.wait_ge(c.act_done.sem, c.act_done.at(1) + p * 2 + r)
                        dve.wait_ge(c.mm_done.sem, c.mm_done.at(2) + (p * 2 + r) * 2)
                        dve.tensor_tensor(hid[:, bass.ds(p * 2 + r, 1), :].rearrange("p a t -> p (a t)"), gate[:, r, :],
                                          c.ps[:, 2 * r + 1, :], ALU.mult).then_inc(c.bank_free.sem, 1)
                dve.wait_ge(c.bank_free.sem, c.bank_free.at(HT + 2))
        c.slot0_loaded.close(8 * HT)
        c.slot1_loaded.close(8 * HT)
        c.mm_done.close(2 * HT)
        c.act_done.close(HT)
        c.bank_free.close(HT + 2)
        linear(c, d[f"w_down{layer}"], HT, DT, lambda k: hid[:, k, :], c.xT, add=True)


def rope(c, x, tiles):
    with ExitStack() as ctx:
        swap = c.sb(ctx, "swap", [P, P])
        cs = c.sb(ctx, "cos", [P, T])
        sn = c.sb(ctx, "sin", [P, T])
        load(c, [(swap[:], c.const("swap")), (cs[:], c.const("mla_cos")), (sn[:], c.const("mla_sin"))])
        rot = c.sb(ctx, "rot", [P, 2, T])
        with c.nc.Block() as block:
            @block.tensor
            def _(pe):
                for n, k in enumerate(tiles):
                    if n >= 2:
                        pe.wait_ge(c.a_ready.sem, c.a_ready.at(n - 1))
                    pe.matmul(c.ps[:, n % 2, :], swap[:], x(k), start=True, stop=True).then_inc(c.mm_done.sem, 1)

            @block.vector
            def _(dve):
                ch = Chain(c.dve_chain, dve)
                for n, k in enumerate(tiles):
                    dve.wait_ge(c.mm_done.sem, c.mm_done.at(n + 1))
                    dve.tensor_tensor(rot[:, n % 2, :], c.ps[:, n % 2, :], sn[:], ALU.mult).then_inc(c.a_ready.sem, 1)
                    ch.link(dve.tensor_tensor(x(k), x(k), cs[:], ALU.mult))
                    dve.wait_ge(c.a_ready.sem, c.a_ready.at(n + 1))
                    ch.link(dve.tensor_tensor(x(k), x(k), rot[:, n % 2, :], ALU.add))
                ch.close()
    c.mm_done.close(len(tiles))
    c.a_ready.close(len(tiles))


def attention(c, qn, qr, kn, kr, v, out):
    scale = 96.0 ** -0.5
    items = [(h, i) for h in range(16) for i in range(NCH)]
    ni = len(items)
    with ExitStack() as ctx:
        future = c.sb(ctx, "future", [P, P])
        pr = c.sb(ctx, "probs", [P, 2, T])
        pT = c.sb(ctx, "probsT", [P, 2, T])
        mx = c.sb(ctx, "row_max", [P, 2])
        nm = c.sb(ctx, "neg_max", [P, 2])
        sm = c.sb(ctx, "row_sum", [P, 2])
        load(c, [(future[:], c.const("future"))])
        with c.nc.Block() as block:
            @block.tensor
            def _(pe):
                def scores(n):
                    h, i = items[n]
                    w = P * (i + 1)
                    a, b = 64 * (h % 2), 32 * (h % 4)
                    if n >= 2:
                        pe.wait_ge(c.act_done.sem, c.act_done.at(n - 1))
                    pe.matmul(c.ps[:, n % 2, 0:w], qn(h // 2)[a:a + 64, i * P:(i + 1) * P], kn(h // 2)[a:a + 64, 0:w],
                              start=True, stop=False)
                    pe.matmul(c.ps[:, n % 2, 0:w], qr(h // 4)[b:b + 32, i * P:(i + 1) * P], kr[b:b + 32, 0:w],
                              start=False, stop=True).then_inc(c.mm_done.sem, 1)

                def weigh(n):
                    h, i = items[n]
                    if h % 2 == 0 and i == 0 and h >= 4:
                        pe.wait_ge(c.e_ready.sem, c.e_ready.at(h // 2 - 1))
                    pe.wait_ge(c.d_ready.sem, c.d_ready.at(n + 1))
                    a = 64 * (h % 2)
                    for j in range(i + 1):
                        mm = pe.matmul(c.ps[a:a + 64, 4 + (h // 2) % 2, i * P:(i + 1) * P], v(j)[:, 64 * h:64 * h + 64],
                                       pT[:, n % 2, j * P:(j + 1) * P], start=j == 0, stop=j == i)
                    mm.then_inc(c.f_ready.sem, 1)
                scores(0)
                for n, (h, i) in enumerate(items):
                    if n + 1 < ni:
                        scores(n + 1)
                    pe.wait_ge(c.b_ready.sem, c.b_ready.at(n + 1))
                    if n >= 2:
                        pe.wait_ge(c.d_ready.sem, c.d_ready.at(n - 1))
                    for j in range(i + 1):
                        mm = pe.transpose(c.ps[:, 2 + n % 2, j * P:(j + 1) * P], pr[:, n % 2, j * P:(j + 1) * P], c.ident)
                    mm.then_inc(c.c_ready.sem, 1)
                    if n:
                        weigh(n - 1)
                weigh(ni - 1)

            @block.vector
            def _(dve):
                ch = Chain(c.dve_chain, dve)

                def top(n):
                    h, i = items[n]
                    dve.wait_ge(c.mm_done.sem, c.mm_done.at(n + 1))
                    d = c.ps[:, n % 2, i * P:(i + 1) * P]
                    ch.link(dve.tensor_tensor(d, d, future[:], ALU.add))
                    ch.link(dve.reduce_max(mx[:, n % 2:n % 2 + 1], c.ps[:, n % 2, 0:(i + 1) * P], AX.X))
                    dve.tensor_scalar(nm[:, n % 2:n % 2 + 1], mx[:, n % 2:n % 2 + 1], -scale, None, ALU.mult
                                      ).then_inc(c.a_ready.sem, 1)
                def keep(k):
                    dve.wait_ge(c.f_ready.sem, c.f_ready.at(8 * (k + 1)))
                    dve.tensor_copy(out(k), c.ps[:, 4 + k % 2, :]).then_inc(c.e_ready.sem, 1)
                top(0)
                for n, (h, i) in enumerate(items):
                    s = sm[:, n % 2:n % 2 + 1]
                    if n + 1 < ni:
                        top(n + 1)
                    dve.wait_ge(c.act_done.sem, c.act_done.at(n + 1))
                    ch.link(dve.reciprocal(s, s))
                    dve.tensor_scalar(pr[:, n % 2, 0:(i + 1) * P], pr[:, n % 2, 0:(i + 1) * P], s, None, ALU.mult
                                      ).then_inc(c.b_ready.sem, 1)
                    if n and items[n - 1][0] % 2 == 1 and items[n - 1][1] == 3:
                        keep(items[n - 1][0] // 2)
                    if n == ni - 1:
                        keep(7)
                dve.wait_ge(c.e_ready.sem, c.e_ready.at(8))
                ch.close()

            @block.scalar
            def _(act):
                def turn(n):
                    h, i = items[n]
                    act.wait_ge(c.c_ready.sem, c.c_ready.at(n + 1))
                    if n >= 2:
                        act.wait_ge(c.f_ready.sem, c.f_ready.at(n - 1))
                    act.copy(pT[:, n % 2, 0:(i + 1) * P], c.ps[:, 2 + n % 2, 0:(i + 1) * P]).then_inc(c.d_ready.sem, 1)
                for n, (h, i) in enumerate(items):
                    act.wait_ge(c.a_ready.sem, c.a_ready.at(n + 1))
                    if n >= 2:
                        act.wait_ge(c.c_ready.sem, c.c_ready.at(n - 1))
                    act.activation(pr[:, n % 2, 0:(i + 1) * P], c.ps[:, n % 2, 0:(i + 1) * P], ACT.Exp,
                                   bias=nm[:, n % 2:n % 2 + 1], scale=scale,
                                   accum_out=sm[:, n % 2:n % 2 + 1]).then_inc(c.act_done.sem, 1)
                    if n:
                        turn(n - 1)
                turn(ni - 1)
    for t, n in ((c.mm_done, ni), (c.a_ready, ni), (c.b_ready, ni), (c.c_ready, ni), (c.d_ready, ni),
                 (c.e_ready, 8), (c.f_ready, ni), (c.act_done, ni)):
        t.close(n)


def mla(c):
    d = c.dram
    x, h = (lambda k: c.xT[:, k, :]), (lambda k: c.hT[:, k, :])
    norm(c, 1, DT, x, h, D, weight=lambda k: c.col("mix_norm_odd", k))
    with ExitStack() as ctx:
        ones64 = c.sb(ctx, "ones64", [P, P])
        ones32 = c.sb(ctx, "ones32", [P, P])
        load(c, [(ones64[:], c.const("ones64")), (ones32[:], c.const("ones32"))])
        lat = c.sb(ctx, "latent", [P, 6, T])
        q = c.sb(ctx, "q", [P, 12, T])
        kn = c.sb(ctx, "k_nope", [P, 8, T])
        v = c.sb(ctx, "v", [P, NCH, D])
        L, Q, K = (lambda k: lat[:, k, :]), (lambda k: q[:, k, :]), (lambda k: kn[:, k, :])
        linear(c, d["w_dqkv"], DT, 6, h, lat)
        norm(c, 1, 3, L, L, 384, weight=lambda k: c.col("q_lora_norm", k))
        norm(c, 1, 2, lambda k: L(3 + k), lambda k: L(3 + k), 256, weight=lambda k: c.col("kv_lora_norm", k))
        norm(c, 1, 1, lambda k: L(5), lambda k: L(5), 32, weight=lambda k: c.col("k_rope_norm"), ones=ones32)
        linear(c, d["w_uq"], 3, 12, L, q)
        linear(c, d["w_uk"], 2, 8, lambda k: L(3 + k), kn)
        linear_tokens(c, d["w_uv"], 2, 2, lambda k: L(3 + k), v)
        norm(c, 8, 1, Q, Q, 64, weight=lambda k: c.col("q_nope_norm"), ones=ones64)
        norm(c, 4, 1, lambda k: Q(8 + k), lambda k: Q(8 + k), 32, weight=lambda k: c.col("q_rope_norm"), ones=ones32)
        norm(c, 8, 1, K, K, 64, weight=lambda k: c.col("k_nope_norm"), ones=ones64)
        rope(c, lambda k: Q(8 + k) if k < 4 else L(5), range(5))
        attention(c, Q, lambda k: Q(8 + k), K, L(5), lambda j: v[:, j, :], h)
        linear(c, d["w_o"], DT, DT, h, c.xT, add=True)


def hgrn_gates(c, f, B, lower):
    with ExitStack() as ctx:
        keep = c.sb(ctx, "keep", [P, T])
        lg = c.sb(ctx, "log_forget", [P, 2, T])
        load(c, [(keep[:], c.const("keep"))])
        with c.nc.Block() as block:
            @block.scalar
            def _(act):
                act.wait_ge(c.a_ready.sem, c.a_ready.at(2))
                act.activation(lower[:, 0:16], lower[:, 0:16], ACT.Exp).then_inc(c.b_ready.sem, 1)
                for k in range(8):
                    act.activation(f[:, k, :], f[:, k, :], ACT.Sigmoid).then_inc(c.act_done.sem, 1)
                for k in range(8):
                    act.wait_ge(c.dve_done.sem, c.dve_done.at(k + 1))
                    if k >= 2:
                        act.wait_ge(c.d_ready.sem, c.d_ready.at(k - 1))
                    act.activation(lg[:, k % 2, :], f[:, k, :], ACT.Ln).then_inc(c.c_ready.sem, 1)

            @block.vector
            def _(dve):
                ch = Chain(c.dve_chain, dve)
                a0, a1 = COL_AT["lb0"][0], COL_AT["lb1"][0]
                lb0, lb1 = c.cols[:, a0:a0 + 8], c.cols[:, a1:a1 + 8]
                ch.link(dve.tensor_tensor(lower[:, 16:24], lb0, lb1, ALU.max))
                dve.tensor_tensor(lower[:, 0:8], lb0, lower[:, 16:24], ALU.subtract).then_inc(c.a_ready.sem, 1)
                dve.tensor_tensor(lower[:, 8:16], lb1, lower[:, 16:24], ALU.subtract).then_inc(c.a_ready.sem, 1)
                dve.wait_ge(c.b_ready.sem, c.b_ready.at(1))
                ch.link(dve.tensor_tensor(lower[:, 8:16], lower[:, 0:8], lower[:, 8:16], ALU.add))
                ch.link(dve.reciprocal(lower[:, 8:16], lower[:, 8:16]))
                ch.link(dve.tensor_tensor(lower[:, 0:8], lower[:, 0:8], lower[:, 8:16], ALU.mult))
                ch.link(dve.tensor_scalar(lower[:, 8:16], lower[:, 0:8], -1.0, 1.0, ALU.mult, ALU.add))
                for k in range(8):
                    dve.wait_ge(c.act_done.sem, c.act_done.at(k + 1))
                    dve.tensor_scalar(f[:, k, :], f[:, k, :], lower[:, 8 + k:9 + k], lower[:, k:k + 1],
                                      ALU.mult, ALU.add).then_inc(c.dve_done.sem, 1)
                for k in range(8):
                    dve.wait_ge(c.c_ready.sem, c.c_ready.at(k + 1))
                    dve.tensor_tensor_scan(B[:, k, :], keep[:], lg[:, k % 2, :], 0.0, ALU.mult, ALU.add
                                           ).then_inc(c.d_ready.sem, 1)
                    ch.link(dve.tensor_scalar(f[:, k, :], f[:, k, :], -1.0, 1.0, ALU.mult, ALU.add))
                dve.wait_ge(c.d_ready.sem, c.d_ready.at(8))
                ch.close()
    for t, n in ((c.a_ready, 2), (c.b_ready, 1), (c.act_done, 8), (c.dve_done, 8), (c.c_ready, 8), (c.d_ready, 8)):
        t.close(n)


def retention(c, qk, v, out):
    with ExitStack() as ctx:
        cs = c.sb(ctx, "cos", [P, T])
        sn = c.sb(ctx, "sin", [P, T])
        dec = c.sb(ctx, "gammas", [P, 4, T])
        tmp = c.sb(ctx, "rotary", [P, 4, T])
        A = c.sb(ctx, "scores", [P, 2, WID])
        load(c, [(cs[:], c.const("ret_cos")), (sn[:], c.const("ret_sin"))] +
             [(dec[:, h, :], c.const(f"ret_decay{h}")) for h in range(4)])
        with c.nc.Block() as block:
            @block.vector
            def _(dve):
                ch = Chain(c.dve_chain, dve)

                def rotate(h):
                    for s in range(2):
                        x1, x2 = qk(4 * h + 2 * s), qk(4 * h + 2 * s + 1)
                        dve.tensor_tensor(tmp[:, 0, :], x1, sn[:], ALU.mult).then_inc(c.a_ready.sem, 1)
                        dve.tensor_tensor(tmp[:, 1, :], x2, sn[:], ALU.mult).then_inc(c.a_ready.sem, 1)
                        dve.wait_ge(c.a_ready.sem, c.a_ready.at(4 * h + 2 * s + 2))
                        ch.link(dve.tensor_tensor(x1, x1, cs[:], ALU.mult))
                        ch.link(dve.tensor_tensor(x2, x2, cs[:], ALU.mult))
                        ch.link(dve.tensor_tensor(x1, x1, tmp[:, 1, :], ALU.subtract))
                        ch.link(dve.tensor_tensor(x2, x2, tmp[:, 0, :], ALU.add))
                    dve.sem_inc(c.b_ready.sem, 1)
                rotate(0)
                for h in range(4):
                    if h < 3:
                        rotate(h + 1)
                    for j in range(NCH):
                        n = NCH * h + j
                        dve.wait_ge(c.mm_done.sem, c.mm_done.at(n + 1))
                        dve.tensor_tensor(A[:, h % 2, OFF[j]:OFF[j] + T - j * P], c.ps[:, n % 2, 0:T - j * P],
                                          dec[:, h, 0:T - j * P], ALU.mult).then_inc(c.c_ready.sem, 1)
                    for x in range(4):
                        dve.wait_ge(c.d_ready.sem, c.d_ready.at(4 * h + x + 1))
                        dve.tensor_copy(out(4 * h + x), c.ps[:, 2 + x, :]).then_inc(c.e_ready.sem, 1)
                dve.wait_ge(c.e_ready.sem, c.e_ready.at(16))
                ch.close()

            @block.tensor
            def _(pe):
                for h in range(4):
                    pe.wait_ge(c.b_ready.sem, c.b_ready.at(h + 1))
                    for j in range(NCH):
                        n = NCH * h + j
                        if n >= 2:
                            pe.wait_ge(c.c_ready.sem, c.c_ready.at(n - 1))
                        for y in range(2):
                            mm = pe.matmul(c.ps[:, n % 2, 0:T - j * P], qk(4 * h + 2 + y)[:, j * P:(j + 1) * P],
                                           qk(4 * h + y)[:, j * P:T], start=y == 0, stop=y == 1)
                        mm.then_inc(c.mm_done.sem, 1)
                    pe.wait_ge(c.c_ready.sem, c.c_ready.at(4 * h + 4))
                    for x in range(4):
                        if h:
                            pe.wait_ge(c.e_ready.sem, c.e_ready.at(4 * (h - 1) + x + 1))
                        for j in range(NCH):
                            mm = pe.matmul(c.ps[:, 2 + x, j * P:T], v(j)[:, h * T + x * P:h * T + (x + 1) * P],
                                           A[:, h % 2, OFF[j]:OFF[j] + T - j * P], start=j == 0, stop=j == NCH - 1)
                        mm.then_inc(c.d_ready.sem, 1)
    for t, n in ((c.a_ready, 16), (c.b_ready, 4), (c.c_ready, 16), (c.mm_done, 16), (c.d_ready, 16), (c.e_ready, 16)):
        t.close(n)


def merge(c, a, b, ga, gb):
    with c.nc.Block() as block:
        @block.scalar
        def _(act):
            for k in range(DT):
                act.activation(ga(k), ga(k), ACT.Sigmoid).then_inc(c.act_done.sem, 1)
                act.activation(gb(k), gb(k), ACT.Sigmoid).then_inc(c.act_done.sem, 1)

        @block.vector
        def _(dve):
            ch = Chain(c.dve_chain, dve)
            for k in range(DT):
                dve.wait_ge(c.act_done.sem, c.act_done.at(2 * k + 2))
                dve.tensor_tensor(a(k), a(k), ga(k), ALU.mult).then_inc(c.dve_done.sem, 1)
                ch.link(dve.tensor_tensor(b(k), b(k), gb(k), ALU.mult))
                dve.wait_ge(c.dve_done.sem, c.dve_done.at(k + 1))
                ch.link(dve.tensor_tensor(a(k), a(k), b(k), ALU.add))
            ch.close()
    c.act_done.close(2 * DT)
    c.dve_done.close(DT)


def mix2(c):
    d = c.dram
    x, h = (lambda k: c.xT[:, k, :]), (lambda k: c.hT[:, k, :])
    norm(c, 1, DT, x, h, D, weight=lambda k: c.col("norm_mix_w_2", k))
    with ExitStack() as outer:
        y_hg = c.sb(outer, "y_hg", [P, DT, T])
        with ExitStack() as ctx:
            proj = c.sb(ctx, "proj_hg", [P, 24, T])
            v = c.sb(ctx, "v_hg", [P, NCH, D])
            B = c.sb(ctx, "B_hg", [P, 8, T])
            lower = c.sb(ctx, "lower", [P, 24])
            q, f, g = proj[:, 0:8, :], proj[:, 8:16, :], proj[:, 16:24, :]
            linear(c, d["w_hg"], DT, 24, h, proj)
            linear_tokens(c, d["w_hg_v"], DT, 2, h, v)
            scale_tiles(c, q, 8, 128.0 ** -0.5)
            hgrn_gates(c, f, B, lower)
            silu_tiles(c, g, 8)
            gated_linear(c, "hg_", 8, 1, lambda i: q[:, i, :], lambda i: f[:, i, :], lambda i: B[:, i, :],
                         lambda j: v[:, j, :], lambda i: q[:, i, :])
            with ExitStack() as _:
                norm(c, 8, 1, lambda t: q[:, t, :], lambda t: q[:, t, :], 128,
                     weight=lambda t: c.col("hg_norm_w_2", t), gate=lambda t: g[:, t, :])
            linear(c, d["w_branch_hg"], DT, DT, lambda k: q[:, k, :], y_hg)
        with ExitStack() as ctx:
            qk = c.sb(ctx, "qk_ret", [P, 16, T])
            with ExitStack() as inner:
                v = c.sb(inner, "v_ret", [P, NCH, 2 * D])
                linear(c, d["w_ret"], DT, 16, h, qk)
                linear_tokens(c, d["w_ret_v"], DT, 4, h, v)
                retention(c, lambda k: qk[:, k, :], lambda j: v[:, j, :], lambda k: qk[:, k, :])
            g = c.sb(ctx, "g_ret", [P, 16, T])
            linear(c, d["w_ret_g"], DT, 16, h, g)
            silu_tiles(c, g, 16)
            norm(c, 4, 4, lambda t: qk[:, t, :], lambda t: qk[:, t, :], 512, gate=lambda t: g[:, t, :])
            y_ret = g[:, 0:8, :]
            linear(c, d["w_branch_ret"], 16, DT, lambda k: qk[:, k, :], y_ret)
            linear(c, d["w_gates"], DT, 16, h, qk)
            merge(c, lambda k: y_hg[:, k, :], lambda k: y_ret[:, k, :], lambda k: qk[:, k, :], lambda k: qk[:, 8 + k, :])
        linear(c, d["w_out_2"], DT, DT, lambda k: y_hg[:, k, :], c.xT, add=True)


K16 = 16
LOW = -3e38
GI = 8


def peer_choose(c, pq, IT, JT, GT):
    nc = c.nc
    with ExitStack() as ctx:
        keys = c.sb(ctx, "keys", [P, 16 * P])
        iota = c.sb(ctx, "iota", [P, P])
        sc = c.sb(ctx, "sub_scores", [P, 2, 16, P])
        alt = c.sb(ctx, "less_top8", [P, 2 * P])
        tv = c.sb(ctx, "top_values", [P, 16, K16])
        ti = c.sb(ctx, "top_index", [P, 16, K16], U32)
        tf = c.sb(ctx, "top_index_f", [P, 16, K16])
        cand = c.sb(ctx, "candidates", [P, 8, 2 * P])
        bv = c.sb(ctx, "best_values", [P, 8, K16])
        bc = c.sb(ctx, "best_place", [P, 8, K16], U32)
        half = c.sb(ctx, "place_half", [P, P], U32)
        hf = c.sb(ctx, "place_half_f", [P, P])
        hot = c.sb(ctx, "hot", [P, P, K16])
        rs = c.sb(ctx, "gate_sum", [P, 8])
        IJG = c.sb(ctx, "chosen", [P, 3, P])
        load(c, [(keys[:], c.dram["peer_keys"]), (iota[:], c.const("iota"))])
        with nc.Block() as block:
            @block.tensor
            def _(pe):
                def turn(t):
                    pe.wait_ge(c.d_ready.sem, c.d_ready.at(t + 1))
                    if t:
                        pe.wait_ge(c.f_ready.sem, c.f_ready.at(t))
                    for x in range(3):
                        mm = pe.transpose(c.ps[:, 7, x * P:(x + 1) * P], IJG[:, x, :], c.ident)
                    mm.then_inc(c.e_ready.sem, 1)
                for t in range(NCH):
                    for b in range(4):
                        if t:
                            pe.wait_ge(c.b_ready.sem, c.b_ready.at(4 * (t - 1) + b + 1))
                        for y in range(4):
                            m = 4 * b + y
                            mm = pe.matmul(c.ps[:, b, y * P:(y + 1) * P], pq[:, m, t * P:(t + 1) * P],
                                           keys[:, m * P:(m + 1) * P], start=True, stop=True)
                        mm.then_inc(c.a_ready.sem, 1)
                    if t:
                        turn(t - 1)
                turn(NCH - 1)

            @block.scalar
            def _(act):
                for t in range(NCH):
                    for b in range(4):
                        act.wait_ge(c.a_ready.sem, c.a_ready.at(4 * t + b + 1))
                        if t >= 2:
                            act.wait_ge(c.c_ready.sem, c.c_ready.at(t - 1))
                        act.copy(sc[:, t % 2, 4 * b:4 * b + 4, :].rearrange("p a n -> p (a n)"), c.ps[:, b, :]
                                 ).then_inc(c.b_ready.sem, 1)
                    act.wait_ge(c.g_ready.sem, c.g_ready.at(t + 1))
                    act.activation(bv[:], bv[:], ACT.Exp).then_inc(c.h_ready.sem, 1)

            @block.vector
            def _(dve):
                ch = Chain(c.dve_chain, dve)

                def top16(values, width, out_v, out_i):
                    ch.link(dve.max(out_v[:, 0:8], values))
                    ch.link(dve.max_index(out_i[:, 0:8], out_v[:, 0:8], values))
                    ch.link(dve.match_replace(alt[:, 0:width], out_v[:, 0:8], values, LOW))
                    ch.link(dve.max(out_v[:, 8:16], alt[:, 0:width]))
                    ch.link(dve.max_index(out_i[:, 8:16], out_v[:, 8:16], alt[:, 0:width]))

                def looked_up(side, op, number, out):
                    ch.link(dve.tensor_scalar(half[:], bc[:].rearrange("p h k -> p (h k)"), number, None, op))
                    ch.link(dve.tensor_copy(hf[:], half[:]))
                    ch.link(dve.tensor_tensor(hot[:], iota[:, 0:K16].unsqueeze(1).broadcast_to([P, P, K16]),
                                              hf[:].unsqueeze(2).broadcast_to([P, P, K16]), ALU.is_equal))
                    idx = tf[:].rearrange("p (h s) m -> p h s m", s=2)[:, :, side, :]
                    view = hot[:].rearrange("p (h k) m -> p h k m", k=K16)
                    ch.link(dve.tensor_tensor(view, view, idx.unsqueeze(2).broadcast_to([P, 8, K16, K16]), ALU.mult))
                    ch.link(dve.tensor_reduce(out, hot[:], AX.X, ALU.add))
                for t in range(NCH):
                    dve.wait_ge(c.b_ready.sem, c.b_ready.at(4 * t + 4))
                    for m in range(16):
                        top16(sc[:, t % 2, m, :], P, tv[:, m, :], ti[:, m, :])
                    dve.sem_inc(c.c_ready.sem, 1)
                    ch.link(dve.tensor_copy(tf[:], ti[:]))
                    pair = tv[:].rearrange("p (h s) m -> p h s m", s=2)
                    ch.link(dve.tensor_tensor(cand[:].rearrange("p h (i j) -> p h i j", j=K16),
                                              pair[:, :, 0, :].unsqueeze(3).broadcast_to([P, 8, K16, K16]),
                                              pair[:, :, 1, :].unsqueeze(2).broadcast_to([P, 8, K16, K16]), ALU.add))
                    for h in range(8):
                        top16(cand[:, h, :], 2 * P, bv[:, h, :], bc[:, h, :])
                    if t:
                        dve.wait_ge(c.e_ready.sem, c.e_ready.at(t))
                    ch.link(dve.tensor_copy(rs[:], bv[:, :, 0]))
                    dve.tensor_tensor(bv[:], bv[:], rs[:].unsqueeze(2).broadcast_to([P, 8, K16]), ALU.subtract
                                      ).then_inc(c.g_ready.sem, 1)
                    looked_up(0, ALU.logical_shift_right, 4, IJG[:, 0, :])
                    looked_up(1, ALU.bitwise_and, 15, IJG[:, 1, :])
                    dve.wait_ge(c.h_ready.sem, c.h_ready.at(t + 1))
                    ch.link(dve.tensor_reduce(rs[:], bv[:], AX.X, ALU.add))
                    ch.link(dve.reciprocal(rs[:], rs[:]))
                    dve.tensor_tensor(IJG[:, 2, :].rearrange("p (h k) -> p h k", k=K16), bv[:],
                                      rs[:].unsqueeze(2).broadcast_to([P, 8, K16]), ALU.mult).then_inc(c.d_ready.sem, 1)
                    dve.wait_ge(c.e_ready.sem, c.e_ready.at(t + 1))
                    for x, to in enumerate((IT, JT, GT)):
                        ch.link(dve.tensor_copy(to[:, t * P:(t + 1) * P], c.ps[:, 7, x * P:(x + 1) * P]))
                    dve.sem_inc(c.f_ready.sem, 1)
                ch.close()
    for t, n in ((c.a_ready, 16), (c.b_ready, 16), (c.c_ready, 4), (c.d_ready, 4), (c.e_ready, 4), (c.f_ready, 4),
                 (c.g_ready, 4), (c.h_ready, 4)):
        t.close(n)


def peer_gates(c, IT, JT, GT):
    nc = c.nc
    SUB = 4
    groups = P // SUB
    with ExitStack() as ctx:
        iota = c.sb(ctx, "iota", [P, P])
        hot_i = c.sb(ctx, "hot_i", [P, 2, SUB, P])
        hot_j = c.sb(ctx, "gate_j", [P, 2, SUB, P])
        stage = c.sb(ctx, "gate_stage", [P, P, P])
        load(c, [(iota[:], c.const("iota"))])
        total = NCH * groups
        with nc.Block() as block:
            @block.vector
            def _(dve):
                with dve.Fori(0, total // 2) as p:
                    for r in range(2):
                        g = p * 2 + r
                        dve.wait_ge(c.b_ready.sem, c.b_ready.at(1) + g)
                        for hot, index, made in ((hot_j, JT, c.a_ready), (hot_i, IT, c.dve_done)):
                            dve.tensor_tensor(hot[:, r, :, :], iota[:].unsqueeze(1).broadcast_to([P, SUB, P]),
                                              index[:, bass.ds(g * SUB, SUB)].unsqueeze(2).broadcast_to([P, SUB, P]),
                                              ALU.is_equal).then_inc(made.sem, 1)

            @block.gpsimd
            def _(pool):
                with pool.Fori(0, total // 2) as p:
                    for r in range(2):
                        g = p * 2 + r
                        pool.wait_ge(c.a_ready.sem, c.a_ready.at(1) + g)
                        pool.tensor_tensor(hot_j[:, r, :, :], hot_j[:, r, :, :],
                                           GT[:, bass.ds(g * SUB, SUB)].unsqueeze(2).broadcast_to([P, SUB, P]),
                                           ALU.mult).then_inc(c.pool_done.sem, 1)

            @block.tensor
            def _(pe):
                pe.sem_inc(c.b_ready.sem, 2)
                with pe.Fori(0, total // 2) as p:
                    for r in range(2):
                        pe.wait_ge(c.dve_done.sem, c.dve_done.at(1) + p * 2 + r)
                        pe.wait_ge(c.pool_done.sem, c.pool_done.at(1) + p * 2 + r)
                        pe.wait_ge(c.bank_free.sem, c.bank_free.at(1) + p * 2 + r)
                        for s in range(SUB):
                            mm = pe.matmul(c.ps[:, r, s * P:(s + 1) * P], hot_j[:, r, s, :], hot_i[:, r, s, :],
                                           start=True, stop=True)
                        mm.then_inc(c.b_ready.sem, 1)

            @block.scalar
            def _(act):
                act.sem_inc(c.bank_free.sem, 2)
                act.sem_inc(c.stored.sem, 16)
                with act.Fori(0, NCH) as t:
                    act.wait_ge(c.stored.sem, c.stored.at(16) + t * 16)
                    with act.Fori(0, groups // 2) as p:
                        for r in range(2):
                            act.wait_ge(c.b_ready.sem, c.b_ready.at(3) + t * groups + p * 2 + r)
                            act.copy(stage[:, :, bass.ds((p * 2 + r) * SUB, SUB)].rearrange("p i t -> p t i"),
                                     c.ps[:, r, :].rearrange("p (t i) -> p t i", i=P)).then_inc(c.bank_free.sem, 1)

            @block.sync
            def _(sp):
                with sp.Fori(0, NCH) as t:
                    sp.wait_ge(c.bank_free.sem, c.bank_free.at(2 + groups) + t * groups)
                    sp.dma_start(c.dram["gates"][:, bass.ds(t, 1), :, :].rearrange("p a i t -> p (a i t)"),
                                 stage[:].rearrange("p i t -> p (i t)")).then_inc(c.stored.sem, 16)
                sp.wait_ge(c.stored.sem, c.stored.at(16 * (NCH + 1)))
    for t, n in ((c.pool_done, total), (c.a_ready, total), (c.dve_done, total), (c.b_ready, total + 2),
                 (c.bank_free, total + 2), (c.stored, 16 * (NCH + 1))):
        t.close(n)


def peer_experts(c):
    nc, d = c.nc, c.dram
    with ExitStack() as ctx:
        vs = c.sb(ctx, "v_slots", [P, GI, D])
        gs = c.sb(ctx, "gate_slots", [P, 2, T])
        w = c.sb(ctx, "weighted", [P, GI, T])
        act_s = c.sb(ctx, "gelu", [P, 2, T])
        groups = P // GI
        u_loaded = (c.slot0_loaded, c.slot1_loaded)
        g_loaded = (c.loaded, c.pool_chain)
        v_loaded = (c.a_ready, c.b_ready)
        with nc.Block() as block:
            @block.sync
            def _(sp):
                with sp.Fori(0, groups) as g:
                    for i in range(GI):
                        r = i % 2
                        sp.wait_ge(c.dve_done.sem, c.dve_done.at(1 + i) + g * GI)
                        sp.dma_start(c.ring[:, r, 0:D], d["expert_u"][bass.ds(g * GI + i, 1), :, :]
                                     .rearrange("a p n -> p (a n)")).then_inc(u_loaded[r].sem, 16)
                        sp.dma_start(gs[:, r, :].rearrange("p (n t) -> p n t", t=P),
                                     d["gates"][:, :, bass.ds(g * GI + i, 1), :].rearrange("p n a t -> p n (a t)")
                                     ).then_inc(g_loaded[r].sem, 16)
                        if i != 1:
                            continue
                        sp.wait_ge(c.c_ready.sem, c.c_ready.at(1) + g)
                        for q in range(2):
                            sp.dma_start(vs[:, 4 * q:4 * q + 4, :],
                                         d["expert_v"][bass.ds(g * GI + 4 * q, 4), :, :].rearrange("a p n -> p a n")
                                         ).then_inc(v_loaded[q].sem, 16)

            @block.tensor
            def _(pe):
                pe.sem_inc(c.c_ready.sem, 1)
                with pe.Fori(0, groups) as g:
                    for i in range(GI):
                        r = i % 2
                        pe.wait_ge(u_loaded[r].sem, u_loaded[r].at(16 * (i // 2 + 1)) + g * (8 * GI))
                        pe.wait_ge(c.act_done.sem, c.act_done.at(1 + i) + g * GI)
                        for k in range(DT):
                            mm = pe.matmul(c.ps[:, r, :], c.ring[:, r, k * P:(k + 1) * P], c.hT[:, k, :],
                                           start=k == 0, stop=k == DT - 1)
                        mm.then_inc(c.mm_done.sem, 1)
                    for q in range(2):
                        pe.wait_ge(v_loaded[q].sem, v_loaded[q].at(16) + g * 16)
                    for k in range(DT):
                        pe.wait_ge(c.e_ready.sem, c.e_ready.at(1 + k) + g * DT)
                        for i in range(GI):
                            if k == 0:
                                pe.wait_ge(c.dve_done.sem, c.dve_done.at(3 + i) + g * GI)
                            mm = pe.matmul(c.ps[:, 2 + k % 4, :], vs[:, i, k * P:(k + 1) * P], w[:, i, :],
                                           start=i == 0, stop=i == GI - 1)
                        mm.then_inc(c.d_ready.sem, 1)
                    pe.wait_ge(c.d_ready.sem, c.d_ready.at(DT) + g * DT)
                    pe.sem_inc(c.c_ready.sem, 1)

            @block.scalar
            def _(act):
                act.sem_inc(c.act_done.sem, 2)
                with act.Fori(0, groups) as g:
                    for i in range(GI):
                        act.wait_ge(c.mm_done.sem, c.mm_done.at(1 + i) + g * GI)
                        act.wait_ge(c.dve_done.sem, c.dve_done.at(1 + i) + g * GI)
                        act.activation(act_s[:, i % 2, :], c.ps[:, i % 2, :], ACT.Gelu_apprx_tanh
                                       ).then_inc(c.act_done.sem, 1)

            @block.vector
            def _(dve):
                dve.sem_inc(c.dve_done.sem, 2)
                dve.sem_inc(c.e_ready.sem, 4)
                with dve.Fori(0, groups) as g:
                    for i in range(GI):
                        r = i % 2
                        dve.wait_ge(c.act_done.sem, c.act_done.at(3 + i) + g * GI)
                        dve.wait_ge(g_loaded[r].sem, g_loaded[r].at(16 * (i // 2 + 1)) + g * (8 * GI))
                        dve.wait_ge(c.c_ready.sem, c.c_ready.at(1) + g)
                        dve.tensor_tensor(w[:, i, :], act_s[:, r, :], gs[:, r, :], ALU.mult
                                          ).then_inc(c.dve_done.sem, 1)
                    for k in range(DT):
                        dve.wait_ge(c.d_ready.sem, c.d_ready.at(1 + k) + g * DT)
                        dve.tensor_tensor(c.xT[:, k, :], c.xT[:, k, :], c.ps[:, 2 + k % 4, :], ALU.add
                                          ).then_inc(c.e_ready.sem, 1)
                dve.wait_ge(c.e_ready.sem, c.e_ready.at(4 + groups * DT))
    for t, n in ((u_loaded[0], 8 * P), (u_loaded[1], 8 * P), (g_loaded[0], 8 * P), (g_loaded[1], 8 * P),
                 (v_loaded[0], 16 * groups), (v_loaded[1], 16 * groups), (c.dve_done, P + 2), (c.act_done, P + 2),
                 (c.mm_done, P), (c.c_ready, groups + 1), (c.d_ready, groups * DT), (c.e_ready, groups * DT + 4)):
        t.close(n)


def peer(c):
    x, h = (lambda k: c.xT[:, k, :]), (lambda k: c.hT[:, k, :])
    norm(c, 1, DT, x, h, D, weight=lambda k: c.col("norm_ffn_w_2", k))
    with ExitStack() as ctx:
        IT = c.sb(ctx, "index_i", [P, T])
        JT = c.sb(ctx, "index_j", [P, T])
        GT = c.sb(ctx, "gate", [P, T])
        with ExitStack() as inner:
            pq = c.sb(inner, "peer_q", [P, 16, T])
            linear(c, c.dram["w_peer_q"], DT, 16, h, pq)
            peer_choose(c, pq, IT, JT, GT)
        peer_gates(c, IT, JT, GT)
    peer_experts(c)


def build(nc, dram, out):
    with ExitStack() as ctx:
        c = Core(nc, ctx, dram)
        start(c, dram["x"])
        even_layer(c)
        swiglu(c, 0)
        mla(c)
        swiglu(c, 1)
        mix2(c)
        peer(c)
        x = lambda k: c.xT[:, k, :]
        norm(c, 1, DT, x, x, D, weight=lambda k: c.col("final_norm_w_2", k))
        with nc.Block() as block:
            @block.sync
            def _(sp):
                sp.dma_start(out, c.xT[:]).then_inc(c.stored.sem, 16)
                sp.wait_ge(c.stored.sem, c.stored.at(16))


def tiles_of(w):
    k, n = w.shape
    return np.ascontiguousarray(w.reshape(k // P, P, n // P, P).transpose(2, 1, 0, 3)).reshape(n // P, P, k)


def wide_tiles_of(w):
    k, n = w.shape
    return np.ascontiguousarray(w.reshape(k // P, P, n // T, T).transpose(2, 1, 0, 3)).reshape(n // T, P, k * 4)


def column(v):
    return v.reshape(-1, P).T


def layout(i):
    out = {}
    out["x"] = i["x"][0].T.reshape(DT, P, T).transpose(1, 0, 2)
    w = i["w_in_even"][0]
    dt_w, gk_w = w[:, 2560:2576], w[:, 5648:5664]
    even = [w[:, 0:2560], w[:, 2576:3600], w[:, 4624:5648], dt_w, dt_w, gk_w, gk_w, dt_w, dt_w, gk_w, gk_w]
    out["w_even"] = tiles_of(np.concatenate(even, axis=1))
    out["w_v_even"] = wide_tiles_of(w[:, 3600:4624])
    out["gla_gk_w2"] = i["gla_gk_w2"][0]
    out["w_out_even"] = tiles_of(i["w_out_even"][0])
    gu = [[tiles_of(i[n][l]) for n in ("w_gate", "w_up")] for l in range(2)]
    out["w_gate_up"] = np.stack([np.concatenate(p, axis=2) for p in gu])
    for l in range(2):
        out[f"w_down{l}"] = tiles_of(i["w_down"][l])
    dq = i["w_dqkv"][0]
    out["w_dqkv"] = tiles_of(np.concatenate([dq[:, 0:640]] + 4 * [dq[:, 640:672]], axis=1))
    uq = i["w_uq"][0].reshape(384, 16, 96)
    out["w_uq"] = tiles_of(np.concatenate([uq[:, :, 0:64].reshape(384, 1024), uq[:, :, 64:96].reshape(384, 512)], axis=1))
    ukv = i["w_ukv"][0].reshape(256, 16, 128)
    out["w_uk"] = tiles_of(ukv[:, :, 0:64].reshape(256, 1024))
    out["w_uv"] = wide_tiles_of(ukv[:, :, 64:128].reshape(256, 1024))
    out["w_o"] = tiles_of(i["w_o_mla"][0])
    w = i["w_in_2"][0]
    out["w_hg"] = tiles_of(np.concatenate([w[:, 0:2048], w[:, 3072:4096]], axis=1))
    out["w_hg_v"] = wide_tiles_of(w[:, 2048:3072])
    rq, rk = (w[:, a:a + 1024].reshape(D, 4, 256) for a in (4096, 5120))
    out["w_ret"] = tiles_of(np.stack([rq, rk], axis=2).reshape(D, 2048))
    out["w_ret_g"] = tiles_of(w[:, 8192:10240])
    out["w_ret_v"] = wide_tiles_of(w[:, 6144:8192])
    out["w_gates"] = tiles_of(w[:, 10240:12288])
    out["w_branch_hg"] = tiles_of(i["w_branch_hg_2"][0])
    out["w_branch_ret"] = tiles_of(i["w_branch_ret_2"][0])
    out["w_out_2"] = tiles_of(i["w_out_2"][0])
    out["w_peer_q"] = tiles_of(i["peer_w_q_2"][0])
    out["peer_keys"] = i["peer_sub_keys_2"][0].transpose(3, 0, 1, 2).reshape(P, 2048)
    out["expert_u"] = tiles_of(i["expert_u_2"][0].T)
    out["expert_v"] = i["expert_v_2"][0].reshape(P, P, D)
    cols = {
        "mix_norm_even": column(i["mix_norm_even"][0]),
        "conv_w": i["conv_w"][0].reshape(4, CONVT, P).transpose(2, 1, 0).reshape(P, 48),
        "conv_b": column(i["conv_b"][0]),
        "dt_bias": np.tile(i["dt_bias"][0], 8)[:, None], "a_log": np.tile(i["a_log"][0], 8)[:, None],
        "d_skip": column(np.repeat(i["d_skip"][0], 64)),
        "ssd_norm": column(i["ssd_norm"][0]), "gla_gk_b": column(i["gla_gk_b"][0]),
        "gla_norm": column(i["gla_norm"][0]), "mix_norm_odd": column(i["mix_norm_odd"][0]),
        "q_lora_norm": column(i["q_lora_norm"][0]), "kv_lora_norm": column(i["kv_lora_norm"][0]),
        "q_nope_norm": np.tile(i["q_nope_norm"][0], 2)[:, None],
        "q_rope_norm": np.tile(i["q_rope_norm"][0], 4)[:, None],
        "k_nope_norm": np.tile(i["k_nope_norm"][0], 2)[:, None],
        "k_rope_norm": np.tile(i["k_rope_norm"][0], 4)[:, None],
        "ffn_norm0": column(i["ffn_norm"][0]), "ffn_norm1": column(i["ffn_norm"][1]),
        "norm_mix_w_2": column(i["norm_mix_w_2"][0]),
        "lb0": column(i["hg_lower_bounds_2"][0]), "lb1": column(i["hg_lower_bounds_2"][1]),
        "hg_norm_w_2": column(i["hg_norm_w_2"][0]), "norm_ffn_w_2": column(i["norm_ffn_w_2"][0]),
        "final_norm_w_2": column(i["final_norm_w_2"]),
    }
    out["cols"] = np.concatenate([cols[k] for k in COL_AT], axis=1)
    out["consts"] = np.concatenate(list(const_table().values()), axis=1)
    out["level_masks"] = level_masks()
    return {k: np.ascontiguousarray(v) for k, v in out.items()}


def kernel(**inputs):
    import concourse.bacc as bacc
    from concourse.bass_utils import run_bass_kernel_spmd

    nc = bacc.Bacc("TRN2", target_bir_lowering=False, num_devices=1)
    arrays = {f"in_{k}": v for k, v in layout({k: np.asarray(v) for k, v in inputs.items()}).items()}
    dram = {k[3:]: nc.dram_tensor(k, v.shape, mybir.dt.from_np(v.dtype), kind="ExternalInput").ap()
            for k, v in arrays.items()}
    dram["gates"] = nc.dram_tensor("gates", [P, NCH, P, P], F32, kind="Internal").ap()
    out = nc.dram_tensor("out", [P, DT, T], F32, kind="ExternalOutput").ap()
    build(nc, dram, out)
    r = run_bass_kernel_spmd(nc, [arrays], core_ids=[0])
    got = r.results[0]["out"]
    return np.ascontiguousarray(got.transpose(1, 0, 2).reshape(D, T).T)[None]
```

```python
from contextlib import ExitStack

import numpy as np
import concourse.bass as bass
from concourse import mybir

F32 = mybir.dt.float32
F32R = mybir.dt.float32r
I32 = mybir.dt.int32
U32 = mybir.dt.uint32
ALU = mybir.AluOpType
ACT = mybir.ActivationFunctionType
AX = mybir.AxisListType

P = 128
T = 512
D = 1024
DT = D // P
NCH = T // P
EPS = 1e-6
HID = 2816
HT = HID // P
CONVT = 12
PARTS = 4096
SLOT = PARTS // 2


class Tally:

    def __init__(self, nc, ctx, name):
        self.sem = ctx.enter_context(nc.semaphore(name))
        self.base = 0

    def at(self, n):
        return self.base + n

    def close(self, n):
        self.base += n


class Chain:

    def __init__(self, tally, engine):
        self.tally, self.engine, self.n = tally, engine, 0

    def link(self, ins):
        self.n += 1
        ins.then_inc(self.tally.sem, 1)
        self.engine.wait_ge(self.tally.sem, self.tally.at(self.n))

    def close(self):
        self.tally.close(self.n)


def levels():
    return [64, 32, 16, 8, 4, 2, 1]


def const_table():
    f = np.float32
    eye = np.eye(P, dtype=f)
    s = np.arange(P)
    out = {"ident": eye, "ones": np.ones((P, P), f), "tri": (s[:, None] <= s[None, :]).astype(f)}
    out["ones64"] = (s[:, None] // 64 == s[None, :] // 64).astype(f)
    out["ones32"] = (s[:, None] // 32 == s[None, :] // 32).astype(f)
    swap = np.zeros((P, P), f)
    for o in range(P):
        r = o % 32
        swap[o + 16 if r < 16 else o - 16, o] = -1.0 if r < 16 else 1.0
    out["swap"] = swap
    out["future"] = np.where(s[None, :] <= s[:, None], 0.0, -3e38).astype(f)
    keep = np.ones((P, T), f)
    keep[:, ::P] = 0.0
    out["keep"] = keep
    out["iota"] = np.broadcast_to(s.astype(f), (P, P)).copy()
    pos = np.arange(T, dtype=f)
    inv = (f(1.0) / np.power(f(10000.0), np.arange(0, 32, 2, dtype=f) / f(32))).astype(f)
    ang = pos[None, :] * inv[:, None]
    out["mla_cos"] = np.tile(np.cos(ang), (8, 1)).astype(f)
    out["mla_sin"] = np.tile(np.sin(ang), (8, 1)).astype(f)
    inv = np.power(f(10000.0), -np.arange(128, dtype=f) / f(128)).astype(f)
    ang = pos[None, :] * inv[:, None]
    out["ret_cos"] = np.cos(ang).astype(f)
    out["ret_sin"] = np.sin(ang).astype(f)
    for h in range(4):
        log_g = np.log(1.0 - np.exp2(-5.0 - h))
        rel = np.arange(T)[None, :] - s[:, None]
        out[f"ret_decay{h}"] = np.where(rel >= 0, np.exp(log_g * np.maximum(rel, 0)) / 16.0, 0.0).astype(f)
    sel = np.zeros((P, 16 * P), f)
    for h in range(16):
        sel[h, h * P:(h + 1) * P] = 1.0
    out["sel"] = sel
    return out


def level_masks():
    s, t = np.arange(P)[:, None], np.arange(P)[None, :]
    m = [((s // (2 * w) == t // (2 * w)) & (s % (2 * w) < w) & (t % (2 * w) >= w)) for w in levels()]
    return np.concatenate(m, axis=1).astype(np.int32)


CONST_AT, _at = {}, 0
for _k, _v in const_table().items():
    CONST_AT[_k] = (_at, _v.shape[1])
    _at += _v.shape[1]
CONST_W = _at

COL_AT, COL_W = {}, 0
for _k, _n in (("mix_norm_even", 8), ("conv_w", 48), ("conv_b", 12), ("dt_bias", 1), ("a_log", 1), ("d_skip", 8),
               ("ssd_norm", 8), ("gla_gk_b", 4), ("gla_norm", 2), ("mix_norm_odd", 8), ("q_lora_norm", 3),
               ("kv_lora_norm", 2), ("q_nope_norm", 1), ("q_rope_norm", 1), ("k_nope_norm", 1),
               ("k_rope_norm", 1), ("ffn_norm0", 8), ("ffn_norm1", 8), ("norm_mix_w_2", 8), ("lb0", 8),
               ("lb1", 8), ("hg_norm_w_2", 8), ("norm_ffn_w_2", 8), ("final_norm_w_2", 8)):
    COL_AT[_k] = (COL_W, _n)
    COL_W += _n


class Core:

    def __init__(self, nc, ctx, dram):
        self.nc, self.ctx, self.dram, self.n_tensors = nc, ctx, dram, 0
        self.xT = self.sb(ctx, "xT", [P, DT, T])
        self.h_hi = self.sb(ctx, "h_hi", [P, DT, T], F32R)
        self.h_lo = self.sb(ctx, "h_lo", [P, DT, T], F32R)
        self.ring = self.sb(ctx, "ring", [P, PARTS])
        self.w_hi = self.sb(ctx, "w_hi", [P, PARTS], F32R)
        self.w_lo = self.sb(ctx, "w_lo", [P, PARTS], F32R)
        self.cols = self.sb(ctx, "cols_sb", [P, COL_W])
        self.basic = self.sb(ctx, "basic", [P, 3 * P])
        self.eps = self.sb(ctx, "eps", [P, 1])
        self.ident = self.basic[:, 0:P]
        self.ones = self.basic[:, P:2 * P]
        self.tri = self.basic[:, 2 * P:3 * P]
        self.ps = ctx.enter_context(nc.psum_tensor("ps", [P, 8, T], F32))
        def tally(name):
            return Tally(nc, ctx, name)

        self.loaded = tally("loaded")
        self.slot0_loaded = tally("slot0_loaded")
        self.slot1_loaded = tally("slot1_loaded")
        self.mm_done = tally("mm_done")
        self.bank_free = tally("bank_free")
        self.act_done = tally("act_done")
        self.dve_done = tally("dve_done")
        self.pool_done = tally("pool_done")
        self.piece_free = tally("piece_free")
        self.hi_done = tally("hi_done")
        self.lo_done = tally("lo_done")
        self.high_done = tally("high_done")
        self.stored = tally("stored")
        self.squared = tally("squared")
        self.summed = tally("summed")
        self.log_done = tally("log_done")
        self.rstd_done = tally("rstd_done")
        self.dve_chain = tally("dve_chain")
        self.act_chain = tally("act_chain")
        self.pool_chain = tally("pool_chain")
        self.a_ready = tally("a_ready")
        self.b_ready = tally("b_ready")
        self.c_ready = tally("c_ready")
        self.d_ready = tally("d_ready")
        self.e_ready = tally("e_ready")
        self.f_ready = tally("f_ready")
        self.g_ready = tally("g_ready")
        self.h_ready = tally("h_ready")
        self.i_ready = tally("i_ready")

        self.started = (0, 0)

    def sb(self, ctx, name, shape, dt=F32):
        self.n_tensors += 1
        return ctx.enter_context(self.nc.sbuf_tensor(f"{name}_{self.n_tensors}", shape, dt))

    def col(self, name, k=0, parts=P):
        return self.cols[0:parts, COL_AT[name][0] + k:COL_AT[name][0] + k + 1]

    def const(self, name):
        at, n = CONST_AT[name]
        return self.dram["consts"][:, at:at + n]


def load(c, pairs):
    with c.nc.Block() as block:
        @block.sync
        def _(sp):
            for dst, src in pairs:
                sp.dma_start(dst, src).then_inc(c.loaded.sem, 16)
            sp.wait_ge(c.loaded.sem, c.loaded.at(16 * len(pairs)))
    c.loaded.close(16 * len(pairs))


def start(c, x_dram):
    at = CONST_AT["ident"][0]
    load(c, [(c.xT[:], x_dram), (c.cols[:], c.dram["cols"]), (c.basic[:], c.dram["consts"][:, at:at + 3 * P])])
    with c.nc.Block() as block:
        @block.vector
        def _(dve):
            dve.memset(c.eps[:], EPS).then_inc(c.dve_done.sem, 1)
            dve.wait_ge(c.dve_done.sem, c.dve_done.at(1))
    c.dve_done.close(1)


def first_pieces(w):
    return [w[m, :, :] for m in range(min(2, w.shape[0]))]


def first_pieces_tokens(w):
    return [w[0, :, 0:2 * T], w[0, :, 2 * T:4 * T] if w.shape[2] > 2 * T else w[1, :, 0:2 * T]]


def start_pieces(c, block, then, more=None):
    then = then or []
    if then:
        c.started = (len(then), len(then))

    @block.sync
    def _(sp):
        for s, piece in enumerate(then):
            sp.dma_start(c.ring[:, s * SLOT:s * SLOT + piece.shape[1]], piece
                         ).then_inc((c.slot0_loaded, c.slot1_loaded)[s].sem, 16)

    @block.gpsimd
    def _(pool):
        if then:
            pool.sem_inc(c.lo_done.sem, 2)
        for s, piece in enumerate(then):
            at = slice(s * SLOT, s * SLOT + piece.shape[1])
            pool.wait_ge(c.hi_done.sem, c.hi_done.at(s + 1))
            pool.tensor_tensor(c.w_lo[:, at], c.ring[:, at], c.w_hi[:, at].bitcast(F32), ALU.subtract
                               ).then_inc(c.lo_done.sem, 1)
        if more:
            more(pool)


def high_pieces(c, act, then):
    for s, piece in enumerate(then or []):
        at = slice(s * SLOT, s * SLOT + piece.shape[1])
        arrived(act, (c.slot0_loaded, c.slot1_loaded), s, s)
        act.copy(c.w_hi[:, at], c.ring[:, at]).then_inc(c.hi_done.sem, 1)


def norm(c, groups, tiles, src, dst, width, weight=None, gate=None, ones=None, halves=None, few=False, then=None):
    n = groups * tiles
    parts = P
    slots = min(n, 4 if few else 8)
    both = 2 if tiles % 2 == 0 else 1
    sums = n // both
    with ExitStack() as ctx:
        sq = c.sb(ctx, "sq", [parts, slots, T])
        rs = c.sb(ctx, "rs", [parts, groups, T])
        if halves:
            whole = c.sb(ctx, "whole", [P, 4, T])
            dst = lambda k: whole[:, k % 4, :]

        def odd_lows(pool):
            for k in range(1, n, 2):
                pool.wait_ge(c.high_done.sem, c.high_done.at(k + 1))
                pool.tensor_tensor(halves[1](k), dst(k), halves[0](k).bitcast(F32), ALU.subtract
                                   ).then_inc(c.pool_done.sem, 1)

        with c.nc.Block() as block:
            start_pieces(c, block, then, odd_lows if halves else None)

            @block.scalar
            def _(act):
                for k in range(n):
                    if k >= slots:
                        act.wait_ge(c.summed.sem, c.summed.at((k - slots) // both + 1))
                    act.activation(sq[:, k % slots, :], src(k), ACT.Square).then_inc(c.squared.sem, 1)
                high_pieces(c, act, then)
                for g in range(groups):
                    act.wait_ge(c.summed.sem, c.summed.at((g + 1) * tiles // both))
                    act.activation(rs[:, g, :], c.ps[0:parts, g % 8, :], ACT.Ln, bias=c.eps[0:parts, :],
                                   scale=1.0 / width).then_inc(c.log_done.sem, 1)
                for g in range(groups):
                    act.wait_ge(c.log_done.sem, c.log_done.at(g + 1))
                    act.activation(rs[:, g, :], rs[:, g, :], ACT.Exp, scale=-0.5).then_inc(c.rstd_done.sem, 1)
                for k in range(n if halves else 0):
                    act.wait_ge(c.dve_done.sem, c.dve_done.at(k + 1))
                    act.copy(halves[0](k), dst(k)).then_inc(c.high_done.sem, 1)

            @block.tensor
            def _(pe):
                for k in range(0, n, both):
                    g = k // tiles
                    if g >= 8 and k % tiles == 0:
                        pe.wait_ge(c.log_done.sem, c.log_done.at(g - 7))
                    if both == 2:
                        pe.wait_ge(c.c_ready.sem, c.c_ready.at(k // 2 + 1))
                    else:
                        pe.wait_ge(c.squared.sem, c.squared.at(k + 1))
                    pe.matmul(c.ps[0:parts, g % 8, :], (ones if ones is not None else c.ones)[0:parts, 0:parts],
                              sq[:, k % slots, :], start=k % tiles == 0,
                              stop=k % tiles == tiles - both).then_inc(c.summed.sem, 1)

            @block.vector
            def _(dve):
                ch = Chain(c.dve_chain, dve)
                for k in range(0, n if both == 2 else 0, 2):
                    dve.wait_ge(c.squared.sem, c.squared.at(k + 2))
                    dve.tensor_tensor(sq[:, k % slots, :], sq[:, k % slots, :], sq[:, (k + 1) % slots, :], ALU.add
                                      ).then_inc(c.c_ready.sem, 1)

                def low(k):
                    dve.wait_ge(c.high_done.sem, c.high_done.at(k + 1))
                    ch.link(dve.tensor_tensor(halves[1](k), dst(k), halves[0](k).bitcast(F32), ALU.subtract))
                for k in range(n):
                    g = k // tiles
                    if k % tiles == 0:
                        dve.wait_ge(c.rstd_done.sem, c.rstd_done.at(g + 1))
                    w = weight(k) if weight else 1.0
                    if halves:
                        if k >= 4 and k % 2:
                            dve.wait_ge(c.pool_done.sem, c.pool_done.at((k - 4) // 2 + 1))
                        dve.scalar_tensor_tensor(dst(k), src(k), w, rs[:, g, :], ALU.mult, ALU.mult
                                                 ).then_inc(c.dve_done.sem, 1)
                        if k % 2:
                            low(k - 1)
                        elif k == n - 1:
                            low(k)
                        continue
                    ch.link(dve.scalar_tensor_tensor(dst(k), src(k), w, rs[:, g, :], ALU.mult, ALU.mult))
                    if gate:
                        ch.link(dve.tensor_tensor(dst(k), dst(k), gate(k), ALU.mult))
                ch.close()
    c.squared.close(n)
    c.summed.close(sums)
    if both == 2:
        c.c_ready.close(sums)
    c.log_done.close(groups)
    c.rstd_done.close(groups)
    if halves:
        c.dve_done.close(n)
        c.high_done.close(n)
        c.pool_done.close(n // 2)


def passes(pe, out, w_hi, w_lo, x_hi, x_lo, start, stop):
    pe.matmul(out, w_hi, x_hi, start=start, stop=False)
    pe.matmul(out, w_hi, x_lo, start=False, stop=False)
    return pe.matmul(out, w_lo, x_hi, start=False, stop=stop)


def linear(c, w, kt, nb, hi, lo, dst, add=False, src=None, then=None, beside=None):
    np_ = 1 if kt <= DT else 2
    pt = kt // np_
    wd = pt * P
    loaded = (c.slot0_loaded, c.slot1_loaded)
    pairs, odd = nb // 2, nb % 2
    total = nb * np_
    (loads, halved), c.started = c.started, (len(then), 1) if then else (0, 0)

    def pieces(one, fori, done=0):
        if done or fori is None:
            for m in range(done, total if fori is None else min(2 * np_, total)):
                one(m // np_, m // np_ % 2, m % np_, m, m % 2)
        if fori is None:
            return
        p0 = 1 if done else 0
        if pairs > p0:
            with fori(p0, pairs) as p:
                for r in range(2):
                    for q in range(np_):
                        m = r * np_ + q
                        one(p * 2 + r, r, q, p * (2 * np_) + m, m % 2)
        if odd and (pairs or not done):
            for q in range(np_):
                one(2 * pairs, 0, q, 2 * pairs * np_ + q, q % 2)

    def raw(s, width=wd):
        return c.ring[:, s * SLOT:s * SLOT + width]

    def half(t, s, width=wd):
        return t[:, s * SLOT:s * SLOT + width]

    last = [total - 1 - (total - 1 - s) % 2 for s in range(2)]
    with c.nc.Block() as block:
        @block.sync
        def _(sp):
            def one(i, r, q, m, s):
                sp.wait_ge(c.lo_done.sem, c.lo_done.at(1) + m)
                sp.dma_start(raw(s), w[bass.ds(i, 1), :, q * wd:(q + 1) * wd].rearrange("a p n -> p (a n)")
                             ).then_inc(loaded[s].sem, 16)
            pieces(one, sp.Fori, loads)
            for s, piece in enumerate(then or []):
                if last[s] >= 0:
                    sp.wait_ge(c.lo_done.sem, c.lo_done.at(3 + last[s]))
                sp.dma_start(raw(s, piece.shape[1]), piece).then_inc(loaded[s].sem, 16)

        @block.scalar
        def _(act):
            for k in range(kt if src else 0):
                act.copy(hi(k), src(k)).then_inc(c.high_done.sem, 1)

            def one(i, r, q, m, s):
                arrived(act, loaded, m, s)
                act.wait_ge(c.piece_free.sem, c.piece_free.at(1) + m)
                act.copy(half(c.w_hi, s), raw(s)).then_inc(c.hi_done.sem, 1)
                if beside:
                    beside[1](act, m)
            if beside:
                for m in range(halved):
                    beside[1](act, m)
            pieces(one, None if beside else act.Fori, halved)
            for m in range(nb, nb + 3 if beside else nb):
                beside[1](act, m)
            if then:
                nw = then[0].shape[1]
                act.wait_ge(loaded[0].sem, loaded[0].at(16 * ((total + 1) // 2) + 16))
                act.wait_ge(c.piece_free.sem, c.piece_free.at(3 + last[0]))
                act.copy(half(c.w_hi, 0, nw), raw(0, nw)).then_inc(c.hi_done.sem, 1)

        @block.gpsimd
        def _(pool):
            if not loads:
                pool.sem_inc(c.lo_done.sem, 2)

            def one(i, r, q, m, s):
                pool.wait_ge(c.hi_done.sem, c.hi_done.at(1) + m)
                pool.tensor_tensor(half(c.w_lo, s), raw(s), half(c.w_hi, s).bitcast(F32), ALU.subtract
                                   ).then_inc(c.lo_done.sem, 1)
            pieces(one, pool.Fori, halved)
            if then:
                nw = then[0].shape[1]
                pool.wait_ge(c.lo_done.sem, c.lo_done.at(2 + total))
                pool.sem_inc(c.lo_done.sem, 2)
                pool.wait_ge(c.hi_done.sem, c.hi_done.at(1 + total))
                pool.tensor_tensor(half(c.w_lo, 0, nw), raw(0, nw), half(c.w_hi, 0, nw).bitcast(F32), ALU.subtract
                                   ).then_inc(c.lo_done.sem, 1)

        @block.tensor
        def _(pe):
            pe.sem_inc(c.piece_free.sem, 2)

            def one(i, r, q, m, s, first=False):
                pe.wait_ge(c.lo_done.sem, c.lo_done.at(3) + m)
                if q == 0:
                    pe.wait_ge(c.bank_free.sem, c.bank_free.at(1) + i)
                for k in range(pt):
                    at = slice(k * P, (k + 1) * P)
                    if first:
                        pe.wait_ge(c.dve_done.sem, c.dve_done.at(k + 1))
                    mm = passes(pe, c.ps[:, r, :], half(c.w_hi, s)[:, at], half(c.w_lo, s)[:, at],
                                hi(q * pt + k), lo(q * pt + k), q == 0 and k == 0, q == np_ - 1 and k == pt - 1)
                mm.then_inc(c.piece_free.sem, 1)
            if src:
                one(0, 0, 0, 0, 0, first=True)
            pieces(one, pe.Fori, 1 if src else 0)

        @block.vector
        def _(dve):
            dve.sem_inc(c.bank_free.sem, 2)
            for k in range(kt if src else 0):
                dve.wait_ge(c.high_done.sem, c.high_done.at(k + 1))
                dve.tensor_tensor(lo(k), src(k), hi(k).bitcast(F32), ALU.subtract).then_inc(c.dve_done.sem, 1)

            def one(i, r, q, m, s):
                if q < np_ - 1:
                    return
                dve.wait_ge(c.piece_free.sem, c.piece_free.at(3) + m)
                out = dst[:, bass.ds(i, 1), :].rearrange("p a t -> p (a t)")
                if add:
                    ins = dve.tensor_tensor(out, out, c.ps[:, r, :], ALU.add)
                else:
                    ins = dve.tensor_copy(out, c.ps[:, r, :])
                ins.then_inc(c.bank_free.sem, 1)
                if beside:
                    beside[0](dve, i)
            pieces(one, None if beside else dve.Fori)
            dve.wait_ge(c.bank_free.sem, c.bank_free.at(nb + 2))
    if src:
        c.high_done.close(kt)
        c.dve_done.close(kt)
    close_pieces(c, total)
    c.bank_free.close(nb + 2)


def arrived(engine, loaded, m, s):
    engine.wait_ge(loaded[s].sem, loaded[s].at(16 - 8 * s) + m * 8)


def close_pieces(c, total):
    c.slot0_loaded.close(16 * ((total + 1) // 2))
    c.slot1_loaded.close(16 * (total // 2))
    c.hi_done.close(total)
    c.lo_done.close(total + 2)
    c.piece_free.close(total + 2)


def linear_tokens(c, w, kt, nb, hi, lo, dst, beside=None):
    np_ = kt // 2
    wd = 2 * T
    loaded = (c.slot0_loaded, c.slot1_loaded)
    total = nb * np_
    (loads, halved), c.started = c.started, (0, 0)

    steps = beside[1] if beside else []
    each = -(-len(steps) // total)
    assert not steps or nb == 2

    def pieces(one, fori, done=0):
        if done or steps:
            for m in range(done, 2 * np_):
                one(m // np_, m // np_, m % np_, m, m % 2)
        if nb // 2 > (1 if done or steps else 0):
            with fori(1 if done else 0, nb // 2) as p:
                for r in range(2):
                    for q in range(np_):
                        m = r * np_ + q
                        one(p * 2 + r, r, q, p * (2 * np_) + m, m % 2)

    with c.nc.Block() as block:
        @block.sync
        def _(sp):
            def one(i, r, q, m, s):
                sp.wait_ge(c.lo_done.sem, c.lo_done.at(1) + m)
                sp.dma_start(c.ring[:, s * SLOT:s * SLOT + wd], w[bass.ds(i, 1), :, q * wd:(q + 1) * wd]
                             .rearrange("a p n -> p (a n)")).then_inc(loaded[s].sem, 16)
            pieces(one, sp.Fori, loads)

        @block.scalar
        def _(act):
            def one(i, r, q, m, s):
                arrived(act, loaded, m, s)
                act.wait_ge(c.piece_free.sem, c.piece_free.at(1) + m)
                act.copy(c.w_hi[:, s * SLOT:s * SLOT + wd], c.ring[:, s * SLOT:s * SLOT + wd]).then_inc(c.hi_done.sem, 1)
                for step in steps[m * each:(m + 1) * each]:
                    step(act)
            for step in steps[:halved * each]:
                step(act)
            pieces(one, act.Fori, halved)
            for step in steps[total * each:]:
                step(act)

        @block.gpsimd
        def _(pool):
            if not loads:
                pool.sem_inc(c.lo_done.sem, 2)

            def one(i, r, q, m, s):
                at = slice(s * SLOT, s * SLOT + wd)
                pool.wait_ge(c.hi_done.sem, c.hi_done.at(1) + m)
                pool.tensor_tensor(c.w_lo[:, at], c.ring[:, s * SLOT:s * SLOT + wd], c.w_hi[:, at].bitcast(F32), ALU.subtract
                                   ).then_inc(c.lo_done.sem, 1)
            pieces(one, pool.Fori, halved)

        @block.tensor
        def _(pe):
            pe.sem_inc(c.piece_free.sem, 2)

            def one(i, r, q, m, s):
                pe.wait_ge(c.lo_done.sem, c.lo_done.at(3) + m)
                for t in range(NCH):
                    if q == 0:
                        pe.wait_ge(c.bank_free.sem, c.bank_free.at(1 + t) + i * NCH)
                    tt = slice(t * P, (t + 1) * P)
                    for k in range(2):
                        at = slice(s * SLOT + k * T, s * SLOT + (k + 1) * T)
                        mm = passes(pe, c.ps[:, 4 * r + t, :], hi(2 * q + k)[:, tt], lo(2 * q + k)[:, tt],
                                    c.w_hi[:, at], c.w_lo[:, at], q == 0 and k == 0, q == np_ - 1 and k == 1)
                mm.then_inc(c.piece_free.sem, 1)
            pieces(one, pe.Fori)

        @block.vector
        def _(dve):
            dve.sem_inc(c.bank_free.sem, 2 * NCH)
            if beside:
                beside[0](dve)

            def one(i, r, q, m, s):
                if q < np_ - 1:
                    return
                dve.wait_ge(c.piece_free.sem, c.piece_free.at(3) + m)
                for t in range(NCH):
                    dve.tensor_copy(dst[:, t, bass.ds(i * T, T)], c.ps[:, 4 * r + t, :]).then_inc(c.bank_free.sem, 1)
            pieces(one, dve.Fori)
            dve.wait_ge(c.bank_free.sem, c.bank_free.at((nb + 2) * NCH))
    close_pieces(c, total)
    c.bank_free.close((nb + 2) * NCH)


def conv_silu(c, ctx, x):
    SLOTS = 6
    y = c.sb(ctx, "conv_y", [P, SLOTS, T])
    tiles = lambda i: range(3 * i // 2, 3 * (i + 1) // 2)

    def convolve(dve, i):
        ch = Chain(c.dve_chain, dve)
        for n in tiles(i):
            if n >= SLOTS:
                dve.wait_ge(c.act_done.sem, c.act_done.at(n - SLOTS + 1))
            ch.link(dve.tensor_scalar(y[:, n % SLOTS, :], x[:, n, :], c.col("conv_w", 4 * n + 3), None, ALU.mult))
            for back in range(1, 4):
                part = y[:, n % SLOTS, back:T]
                ch.link(dve.scalar_tensor_tensor(part, x[:, n, 0:T - back], c.col("conv_w", 4 * n + 3 - back),
                                                 part, ALU.mult, ALU.add))
            dve.sem_inc(c.dve_done.sem, 1)
        ch.close()

    def silu(act, m):
        if m < 3:
            return
        for n in tiles(m - 3):
            act.wait_ge(c.dve_done.sem, c.dve_done.at(n + 1))
            act.activation(x[:, n, :], y[:, n % SLOTS, :], ACT.Silu, bias=c.col("conv_b", n)
                           ).then_inc(c.act_done.sem, 1)

    return convolve, silu


NH, NG = 16, 2
OFF = [0, 512, 896, 1152]
WID = 1280


def ssd(c, z, xbc, small, out):
    nc = c.nc
    xs = lambda k: xbc[:, k, :]
    Bf = lambda g: xbc[:, 8 + g, :]
    Cf = lambda g: xbc[:, 10 + g, :]
    with ExitStack() as ctx:
        sel = c.ring[0:NH, 0:NH * P]
        sel_hi = c.w_hi[0:NH, 0:NH * P]
        lin = c.ring[0:NH, NH * P:NH * P + T]
        acum_hi = c.w_hi[0:NH, NH * P:NH * P + OFF[3]]
        acum_lo = c.w_lo[0:NH, NH * P:NH * P + OFF[3]]
        dt = c.sb(ctx, "dt", [NH, T])
        a = c.sb(ctx, "a", [NH, T])
        one = c.sb(ctx, "one_row", [NH, T])
        ea = c.sb(ctx, "exp_a_log", [NH, 1])
        acum = c.sb(ctx, "acum", [NH, WID])
        dtT = c.sb(ctx, "dtT", [P, NCH, NH])
        negT = c.sb(ctx, "neg_acumT", [P, NCH, NH])
        xdt = c.sb(ctx, "xdt", [P, NCH, D])
        cbm = c.sb(ctx, "cbm", [P, NG, WID])
        diag = c.sb(ctx, "seg_diag", [P, 3, P])
        E = c.sb(ctx, "decay", [P, 3, T])
        M = c.sb(ctx, "weights_st", [P, 2, T])
        load(c, [(sel, c.const("sel")[0:NH, :])])
        with nc.Block() as block:
            @block.scalar
            def _(act):
                ch = Chain(c.act_chain, act)
                ch.link(act.activation(dt[:], small[0:NH, :], ACT.Abs, bias=c.col("dt_bias", 0, NH)))
                ch.link(act.activation(dt[:], dt[:], ACT.Exp, scale=-1.0))
                act.activation(ea[:], c.col("a_log", 0, NH), ACT.Exp).then_inc(c.act_done.sem, 1)
                act.activation(dt[:], dt[:], ACT.Ln, bias=1.0).then_inc(c.act_done.sem, 1)
                for j in range(3):
                    act.wait_ge(c.dve_done.sem, c.dve_done.at(j + 1))
                    at = slice(OFF[j], OFF[j] + T - j * P)
                    act.copy(acum_hi[:, at], acum[:, at]).then_inc(c.high_done.sem, 1)
                act.copy(sel_hi, sel).then_inc(c.high_done.sem, 1)
                for k in range(DT):
                    act.activation(z[:, k, :], z[:, k, :], ACT.Silu).then_inc(c.act_done.sem, 1)
                ch.close()

            @block.gpsimd
            def _(pool):
                pool.memset(one[:], 1.0).then_inc(c.pool_done.sem, 1)

            @block.vector
            def _(dve):
                ch = Chain(c.dve_chain, dve)
                ch.link(dve.tensor_scalar(lin, small[0:NH, :], c.col("dt_bias", 0, NH), 0.0, ALU.add, ALU.max))
                dve.wait_ge(c.act_done.sem, c.act_done.at(2))
                ch.link(dve.tensor_tensor(dt[:], dt[:], lin, ALU.add))
                ch.link(dve.tensor_scalar(a[:], dt[:], ea[:], -1.0, ALU.mult, ALU.mult))
                dve.wait_ge(c.pool_done.sem, c.pool_done.at(1))
                for j in range(NCH):
                    dve.tensor_tensor_scan(acum[:, OFF[j]:OFF[j] + T - j * P], one[:, j * P:T], a[:, j * P:T], 0.0,
                                           ALU.mult, ALU.add).then_inc(c.dve_done.sem, 1)
                for j in range(3):
                    dve.wait_ge(c.high_done.sem, c.high_done.at(j + 1))
                    ch.link(dve.tensor_tensor(acum_lo[:, OFF[j]:OFF[j] + T - j * P], acum[:, OFF[j]:OFF[j] + T - j * P],
                                              acum_hi[:, OFF[j]:OFF[j] + T - j * P].bitcast(F32), ALU.subtract))
                dve.wait_ge(c.mm_done.sem, c.mm_done.at(2 * NCH))
                for j in range(NCH):
                    ch.link(dve.tensor_copy(dtT[:, j, :], c.ps[:, 0, 32 * j:32 * j + NH]))
                    ch.link(dve.tensor_scalar(negT[:, j, :], c.ps[:, 1, 32 * j:32 * j + NH], -1.0, None, ALU.mult))
                for j in range(NCH):
                    for f in range(2):
                        n = 2 * j + f
                        dve.wait_ge(c.a_ready.sem, c.a_ready.at(n + 1))
                        dve.tensor_tensor(xdt[:, j, f * T:(f + 1) * T].rearrange("p (h d) -> p h d", d=64),
                                          c.ps[:, 2 + n % 2, :].rearrange("p (h d) -> p h d", d=64),
                                          dtT[:, j, 8 * f:8 * f + 8].unsqueeze(2).broadcast_to([P, 8, 64]),
                                          ALU.mult).then_inc(c.b_ready.sem, 1)
                for g in range(NG):
                    for j in range(NCH):
                        n = NCH * g + j
                        dve.wait_ge(c.c_ready.sem, c.c_ready.at(n + 1))
                        dve.tensor_tensor(cbm[:, g, OFF[j]:OFF[j] + P], c.ps[:, 4 + n % 2, 0:P], c.tri, ALU.mult
                                          ).then_inc(c.d_ready.sem, 1)
                        if j < 3:
                            ch.link(dve.tensor_copy(cbm[:, g, OFF[j] + P:OFF[j] + T - j * P],
                                                    c.ps[:, 4 + n % 2, P:T - j * P]))
                        dve.sem_inc(c.d_ready.sem, 1)
                dve.wait_ge(c.b_ready.sem, c.b_ready.at(8))
                dve.wait_ge(c.d_ready.sem, c.d_ready.at(16))
                ch.close()

            @block.tensor
            def _(pe):
                pe.wait_ge(c.dve_done.sem, c.dve_done.at(NCH))
                for j in range(NCH):
                    pe.transpose(c.ps[:, 0, 32 * j:32 * j + NH], dt[:, j * P:(j + 1) * P],
                                 c.ident[0:NH, 0:NH]).then_inc(c.mm_done.sem, 1)
                    pe.transpose(c.ps[:, 1, 32 * j:32 * j + NH], acum[:, OFF[j]:OFF[j] + P],
                                 c.ident[0:NH, 0:NH]).then_inc(c.mm_done.sem, 1)
                for j in range(NCH):
                    for f in range(2):
                        n = 2 * j + f
                        if n >= 2:
                            pe.wait_ge(c.b_ready.sem, c.b_ready.at(n - 1))
                        for q in range(4):
                            mm = pe.transpose(c.ps[:, 2 + n % 2, q * P:(q + 1) * P],
                                              xs(4 * f + q)[:, j * P:(j + 1) * P], c.ident)
                        mm.then_inc(c.a_ready.sem, 1)
                for g in range(NG):
                    for j in range(NCH):
                        n = NCH * g + j
                        if n >= 2:
                            pe.wait_ge(c.d_ready.sem, c.d_ready.at(2 * (n - 1)))
                        pe.matmul(c.ps[:, 4 + n % 2, 0:T - j * P], Bf(g)[:, j * P:(j + 1) * P], Cf(g)[:, j * P:T],
                                  start=True, stop=True).then_inc(c.c_ready.sem, 1)
        c.act_done.close(2 + DT)
        c.high_done.close(4)
        c.pool_done.close(1)
        c.dve_done.close(NCH)
        c.mm_done.close(8)
        c.a_ready.close(8)
        c.b_ready.close(8)
        c.c_ready.close(8)
        c.d_ready.close(16)
        steps = [(h, j) for h in range(NH) for j in range(NCH)]
        banks = (0, 1, 4)
        with nc.Block() as block:
            @block.tensor
            def _(pe):
                def spread(n):
                    h, j = steps[n]
                    if n >= 3:
                        pe.wait_ge(c.a_ready.sem, c.a_ready.at(n - 2))
                        pe.wait_ge(c.act_done.sem, c.act_done.at(n - 2))
                    to = c.ps[:, banks[n % 3], 0:T - j * P]
                    if j < 3:
                        at = slice(OFF[j], OFF[j] + T - j * P)
                        pe.matmul(to, sel_hi[:, h * P:(h + 1) * P], acum_hi[:, at], start=True, stop=False)
                        mm = pe.matmul(to, sel_hi[:, h * P:(h + 1) * P], acum_lo[:, at], start=False, stop=True)
                    else:
                        mm = pe.matmul(to, sel[:, h * P:(h + 1) * P], acum[:, OFF[j]:OFF[j] + T - j * P], start=True, stop=True)
                    mm.then_inc(c.mm_done.sem, 1)
                spread(0)
                spread(1)
                for n, (h, j) in enumerate(steps):
                    if n + 2 < len(steps):
                        spread(n + 2)
                    if j == 0 and h % 2 == 0 and h >= 4:
                        pe.wait_ge(c.c_ready.sem, c.c_ready.at(h // 2 - 1))
                    pe.wait_ge(c.b_ready.sem, c.b_ready.at(n + 1))
                    p0 = 64 * (h % 2)
                    mm = pe.matmul(c.ps[p0:p0 + 64, 2 + (h // 2) % 2, j * P:T], xdt[:, j, 64 * h:64 * h + 64],
                                   M[:, n % 2, 0:T - j * P], start=j == 0, stop=j == NCH - 1)
                    mm.then_inc(c.d_ready.sem, 1)

            @block.scalar
            def _(act):
                for n, (h, j) in enumerate(steps):
                    if n >= 3:
                        act.wait_ge(c.b_ready.sem, c.b_ready.at(n - 2))
                    act.wait_ge(c.mm_done.sem, c.mm_done.at(n + 1))
                    act.wait_ge(c.a_ready.sem, c.a_ready.at(n + 1))
                    if j < 3:
                        act.activation(E[:, n % 3, P:T - j * P], c.ps[:, banks[n % 3], P:T - j * P], ACT.Exp,
                                       bias=negT[:, j, h:h + 1]).then_inc(c.e_ready.sem, 1)
                    act.activation(E[:, n % 3, 0:P], diag[:, n % 3, :], ACT.Exp).then_inc(c.act_done.sem, 1)

            @block.vector
            def _(dve):
                def seg(n):
                    h, j = steps[n]
                    dve.wait_ge(c.mm_done.sem, c.mm_done.at(n + 1))
                    if n >= 3:
                        dve.wait_ge(c.act_done.sem, c.act_done.at(n - 2))
                    dve.tensor_scalar(diag[:, n % 3, :], c.ps[:, banks[n % 3], 0:P], negT[:, j, h:h + 1], 0.0,
                                      ALU.add, ALU.min).then_inc(c.a_ready.sem, 1)

                def pair(k):
                    dve.wait_ge(c.d_ready.sem, c.d_ready.at(2 * NCH * (k + 1)))
                    dve.scalar_tensor_tensor(out[:, k, :], xs(k), c.col("d_skip", k),
                                             c.ps[:, 2 + k % 2, :], ALU.mult, ALU.add).then_inc(c.c_ready.sem, 1)
                    dve.wait_ge(c.c_ready.sem, c.c_ready.at(k + 1))
                    dve.tensor_tensor(out[:, k, :], out[:, k, :], z[:, k, :], ALU.mult).then_inc(c.dve_done.sem, 1)
                seg(0)
                seg(1)
                for n, (h, j) in enumerate(steps):
                    dve.wait_ge(c.act_done.sem, c.act_done.at(n + 1))
                    if j < 3:
                        dve.wait_ge(c.e_ready.sem, c.e_ready.at(3 * h + j + 1))
                    if n >= 2:
                        dve.wait_ge(c.d_ready.sem, c.d_ready.at(n - 1))
                    dve.tensor_tensor(M[:, n % 2, 0:T - j * P], E[:, n % 3, 0:T - j * P],
                                      cbm[:, h // 8, OFF[j]:OFF[j] + T - j * P], ALU.mult).then_inc(c.b_ready.sem, 1)
                    if n + 2 < len(steps):
                        seg(n + 2)
                    if j == 0 and h >= 2 and h % 2 == 0:
                        pair(h // 2 - 1)
                pair(NH // 2 - 1)
                dve.wait_ge(c.dve_done.sem, c.dve_done.at(DT))
        ns = len(steps)
        c.mm_done.close(ns)
        c.a_ready.close(ns)
        c.b_ready.close(ns)
        c.act_done.close(ns)
        c.e_ready.close(3 * NH)
        c.d_ready.close(ns)
        c.c_ready.close(NH // 2)
        c.dve_done.close(DT)


def curved(c, x, func):
    def step(act, m):
        if m < 3:
            return
        act.wait_ge(c.bank_free.sem, c.bank_free.at(m))
        act.activation(x[:, m - 3, :], x[:, m - 3, :], func).then_inc(c.act_done.sem, 1)

    return (lambda dve, i: None), step


def silu_steps(c, x, n):
    return [lambda act, k=k: act.activation(x[:, k, :], x[:, k, :], ACT.Silu).then_inc(c.g_ready.sem, 1)
            for k in range(n)] + [lambda act: act.wait_ge(c.g_ready.sem, c.g_ready.at(n))]


def scaled(c, x, n, factor):
    def program(dve):
        dve.tensor_scalar(x[:, 0:n, :], x[:, 0:n, :], factor, None, ALU.mult).then_inc(c.h_ready.sem, 1)
        dve.wait_ge(c.h_ready.sem, c.h_ready.at(1))
    return program


def gated_linear(c, tag, heads, vt, q, k, B, v, out):
    nc = c.nc
    lv = levels()
    NL = len(lv)
    W = vt * P
    items = [(h, l) for h in range(heads) for l in range(NL)]
    with ExitStack() as ctx:
        mask = c.sb(ctx, tag + "mask", [P, NL * P], I32)
        A = c.sb(ctx, tag + "A", [P, 2, T])
        E = c.sb(ctx, tag + "E", [P, 3, T])
        M = c.sb(ctx, tag + "M", [P, 2, T])
        kend = c.sb(ctx, tag + "kend", [P, T])
        kendT = c.sb(ctx, tag + "kendT", [P, T])
        Ed = c.sb(ctx, tag + "Ed", [P, T])
        dec = c.sb(ctx, tag + "dec", [P, NCH])
        S = c.sb(ctx, tag + "S", [P, 3, W])
        load(c, [(mask[:], c.dram["level_masks"])])
        with nc.Block() as block:
            @block.scalar
            def _(act):
                ch = Chain(c.act_chain, act)

                def outputs(h):
                    act.wait_ge(c.g_ready.sem, c.g_ready.at(h + 1))
                    for x in range(vt):
                        act.copy(out(h * vt + x), c.ps[:, 5 + x, :]).then_inc(c.bank_free.sem, 1)
                for n, (h, l) in enumerate(items):
                    act.wait_ge(c.a_ready.sem, c.a_ready.at(n + 1))
                    ch.link(act.activation(E[:, n % 3, :], E[:, n % 3, :], ACT.Abs))
                    act.activation(E[:, n % 3, :], E[:, n % 3, :], ACT.Exp, scale=-1.0).then_inc(c.b_ready.sem, 1)
                    if l == 2:
                        act.wait_ge(c.f_ready.sem, c.f_ready.at(3 * h + 1))
                        act.activation(kend[:], kend[:], ACT.Exp).then_inc(c.e_ready.sem, 1)
                    if l == 4:
                        if h >= 1:
                            act.wait_ge(c.g_ready.sem, c.g_ready.at(h))
                            act.wait_ge(c.squared.sem, c.squared.at(3 * h))
                        act.activation(Ed[:], B(h), ACT.Exp).then_inc(c.e_ready.sem, 1)
                        act.activation(dec[:], B(h)[:, P - 1:T:P], ACT.Exp).then_inc(c.e_ready.sem, 1)
                        if h >= 1:
                            outputs(h - 1)
                    if l == 5:
                        act.wait_ge(c.summed.sem, c.summed.at(h + 1))
                        if h >= 1:
                            act.wait_ge(c.rstd_done.sem, c.rstd_done.at(3 * h))
                        act.copy(kendT[:], c.ps[:, 3, :]).then_inc(c.log_done.sem, 1)
                outputs(heads - 1)
                act.wait_ge(c.bank_free.sem, c.bank_free.at(heads * vt))
                ch.close()

            @block.vector
            def _(dve):
                ch = Chain(c.dve_chain, dve)

                def sub(n):
                    h, l = items[n]
                    w = lv[l]
                    if n >= 3:
                        dve.wait_ge(c.c_ready.sem, c.c_ready.at(n - 2))
                        dve.wait_ge(c.d_ready.sem, c.d_ready.at(n - 2))
                    b = B(h).rearrange("p (n w) -> p n w", w=2 * w)
                    dve.tensor_tensor(E[:, n % 3, :].rearrange("p (n w) -> p n w", w=2 * w), b,
                                      b[:, :, w - 1:w].broadcast_to([P, T // (2 * w), 2 * w]),
                                      ALU.subtract).then_inc(c.a_ready.sem, 1)

                def mul(n):
                    h, l = items[n]
                    w = lv[l]
                    dve.wait_ge(c.b_ready.sem, c.b_ready.at(n + 1))
                    if n >= 2:
                        dve.wait_ge(c.mm_done.sem, c.mm_done.at(n - 1))
                    vw = lambda t: t.rearrange("p (n w) -> p n w", w=2 * w)[:, :, w:2 * w]
                    dve.tensor_tensor(vw(M[:, n % 2, :]), vw(q(h)), vw(E[:, n % 3, :]), ALU.mult
                                      ).then_inc(c.c_ready.sem, 1)

                sub(0)
                sub(1)
                mul(0)
                for n, (h, l) in enumerate(items):
                    if n + 2 < len(items):
                        sub(n + 2)
                    if n + 1 < len(items):
                        mul(n + 1)
                    if l == 0:
                        dve.wait_ge(c.h_ready.sem, c.h_ready.at(h + 1))
                        if h >= 2:
                            dve.wait_ge(c.g_ready.sem, c.g_ready.at(h - 1))
                        ch.link(dve.tensor_tensor(A[:, h % 2, :].rearrange("p (n t) -> p n t", t=P),
                                                  c.ps[:, 2, :].rearrange("p (n t) -> p n t", t=P),
                                                  c.ident.unsqueeze(1).broadcast_to([P, NCH, P]), ALU.mult))
                    dve.wait_ge(c.mm_done.sem, c.mm_done.at(n + 1))
                    ch.link(dve.copy_predicated(A[:, h % 2, :].rearrange("p (n t) -> p n t", t=P),
                                                mask[:, l * P:(l + 1) * P].unsqueeze(1).broadcast_to([P, NCH, P]),
                                                c.ps[:, n % 2, :].rearrange("p (n t) -> p n t", t=P)))
                    dve.sem_inc(c.dve_done.sem, 1)
                    if l >= 4:
                        j = l - 4
                        dve.wait_ge(c.rstd_done.sem, c.rstd_done.at(3 * h + j + 1))
                        if j == 0:
                            ch.link(dve.tensor_copy(S[:, 0, :], c.ps[:, 4, 0:W]))
                        else:
                            ch.link(dve.scalar_tensor_tensor(S[:, j, :], S[:, j - 1, :], dec[:, j:j + 1],
                                                             c.ps[:, 4, 0:W], ALU.mult, ALU.add))
                        dve.sem_inc(c.squared.sem, 1)
                ch.close()

            @block.gpsimd
            def _(pool):
                for n, (h, l) in enumerate(items):
                    w = lv[l]
                    pool.wait_ge(c.b_ready.sem, c.b_ready.at(n + 1))
                    if n >= 2:
                        pool.wait_ge(c.mm_done.sem, c.mm_done.at(n - 1))
                    vw = lambda t: t.rearrange("p (n w) -> p n w", w=2 * w)[:, :, 0:w]
                    pool.tensor_tensor(vw(M[:, n % 2, :]), vw(k(h)), vw(E[:, n % 3, :]), ALU.mult
                                       ).then_inc(c.d_ready.sem, 1)
                    if l == 0:
                        if h >= 1:
                            pool.wait_ge(c.summed.sem, c.summed.at(h))
                        b4 = B(h).rearrange("p (n w) -> p n w", w=P)
                        pool.tensor_tensor(kend[:].rearrange("p (n w) -> p n w", w=P),
                                           b4[:, :, P - 1:P].broadcast_to([P, NCH, P]), b4, ALU.subtract
                                           ).then_inc(c.f_ready.sem, 1)
                    if l == 2:
                        pool.wait_ge(c.e_ready.sem, c.e_ready.at(3 * h + 1))
                        pool.tensor_tensor(kend[:], kend[:], k(h), ALU.mult).then_inc(c.f_ready.sem, 1)
                    if l == 5:
                        pool.wait_ge(c.e_ready.sem, c.e_ready.at(3 * h + 3))
                        pool.tensor_tensor(Ed[:], q(h), Ed[:], ALU.mult).then_inc(c.f_ready.sem, 1)

            @block.tensor
            def _(pe):
                def cut(x, j):
                    return x[:, j * P:(j + 1) * P]

                def outputs(h):
                    pe.wait_ge(c.dve_done.sem, c.dve_done.at((h + 1) * NL))
                    pe.wait_ge(c.f_ready.sem, c.f_ready.at(3 * h + 3))
                    pe.wait_ge(c.squared.sem, c.squared.at(3 * h + 3))
                    if h >= 1:
                        pe.wait_ge(c.bank_free.sem, c.bank_free.at(h * vt))
                    for x in range(vt):
                        for j in range(NCH):
                            o = cut(c.ps[:, 5 + x, :], j)
                            mm = pe.matmul(o, v(j)[:, h * W + x * P:h * W + (x + 1) * P], cut(A[:, h % 2, :], j),
                                           start=True, stop=j == 0)
                            if j:
                                mm = pe.matmul(o, S[:, j - 1, x * P:(x + 1) * P], cut(Ed[:], j),
                                               start=False, stop=True)
                    mm.then_inc(c.g_ready.sem, 1)
                for n, (h, l) in enumerate(items):
                    if l == 0:
                        if h >= 1:
                            pe.wait_ge(c.dve_done.sem, c.dve_done.at(n - NL + 1))
                        for j in range(NCH):
                            mm = pe.matmul(cut(c.ps[:, 2, :], j), cut(k(h), j), cut(q(h), j), start=True, stop=True)
                        mm.then_inc(c.h_ready.sem, 1)
                    if n >= 2:
                        pe.wait_ge(c.dve_done.sem, c.dve_done.at(n - 1))
                    pe.wait_ge(c.c_ready.sem, c.c_ready.at(n + 1))
                    pe.wait_ge(c.d_ready.sem, c.d_ready.at(n + 1))
                    for j in range(NCH):
                        mm = pe.matmul(cut(c.ps[:, n % 2, :], j), cut(M[:, n % 2, :], j), cut(M[:, n % 2, :], j),
                                       start=True, stop=True)
                    mm.then_inc(c.mm_done.sem, 1)
                    if l == 1 and h >= 1:
                        outputs(h - 1)
                    if l == 3:
                        pe.wait_ge(c.f_ready.sem, c.f_ready.at(3 * h + 2))
                        if h >= 1:
                            pe.wait_ge(c.log_done.sem, c.log_done.at(h))
                        for j in range(NCH):
                            mm = pe.transpose(cut(c.ps[:, 3, :], j), cut(kend, j), c.ident)
                        mm.then_inc(c.summed.sem, 1)
                    if l >= 4:
                        j = l - 4
                        pe.wait_ge(c.log_done.sem, c.log_done.at(h + 1))
                        if 3 * h + j:
                            pe.wait_ge(c.squared.sem, c.squared.at(3 * h + j))
                        pe.matmul(c.ps[:, 4, 0:W], cut(kendT, j), v(j)[:, h * W:(h + 1) * W],
                                  start=True, stop=True).then_inc(c.rstd_done.sem, 1)
                outputs(heads - 1)
    ni = len(items)
    for t, n in ((c.a_ready, ni), (c.b_ready, ni), (c.c_ready, ni), (c.d_ready, ni), (c.mm_done, ni),
                 (c.dve_done, ni), (c.h_ready, heads), (c.g_ready, heads), (c.f_ready, 3 * heads),
                 (c.e_ready, 3 * heads), (c.summed, heads), (c.log_done, heads), (c.rstd_done, 3 * heads),
                 (c.squared, 3 * heads), (c.bank_free, heads * vt)):
        t.close(n)


def gla_gates(c, small, w2, B):
    with ExitStack() as ctx:
        keep = c.sb(ctx, "keep", [P, T])
        curve = c.sb(ctx, "curve", [P, 4, T])
        nb = c.sb(ctx, "gk_sum", [P, 4, T])
        w2s = c.sb(ctx, "w2s", [48, T])
        load(c, [(keep[:], c.const("keep")), (w2s[32:48, :], w2)])
        with c.nc.Block() as block:
            @block.tensor
            def _(pe):
                for m in range(4):
                    pe.matmul(c.ps[:, m, :], w2s[32:48, m * P:(m + 1) * P], small[32:48, :],
                              start=True, stop=True).then_inc(c.mm_done.sem, 1)

            @block.scalar
            def _(act):
                ch = Chain(c.act_chain, act)
                for m in range(4):
                    act.wait_ge(c.mm_done.sem, c.mm_done.at(m + 1))
                    act.activation(curve[:, m, :], c.ps[:, m, :], ACT.Abs, bias=c.col("gla_gk_b", m)
                                   ).then_inc(c.a_ready.sem, 1)
                act.wait_ge(c.a_ready.sem, c.a_ready.at(4))
                for m in range(4):
                    ch.link(act.activation(curve[:, m, :], curve[:, m, :], ACT.Exp, scale=-1.0))
                for m in range(4):
                    act.activation(curve[:, m, :], curve[:, m, :], ACT.Ln, bias=1.0).then_inc(c.act_done.sem, 1)
                ch.close()

            @block.vector
            def _(dve):
                ch = Chain(c.dve_chain, dve)
                for m in range(4):
                    dve.wait_ge(c.a_ready.sem, c.a_ready.at(m + 1))
                    ch.link(dve.tensor_scalar(nb[:, m, :], c.ps[:, m, :], c.col("gla_gk_b", m), 0.0,
                                              ALU.add, ALU.min))
                    dve.wait_ge(c.act_done.sem, c.act_done.at(m + 1))
                    ch.link(dve.tensor_tensor(nb[:, m, :], nb[:, m, :], curve[:, m, :], ALU.subtract))
                    ch.link(dve.tensor_scalar(nb[:, m, :], nb[:, m, :], 1.0 / 16.0, None, ALU.mult))
                    ch.link(dve.tensor_tensor_scan(B[:, m, :], keep[:], nb[:, m, :], 0.0, ALU.mult, ALU.add))
                ch.close()
    c.mm_done.close(4)
    c.a_ready.close(4)
    c.act_done.close(4)


def even_layer(c):
    d = c.dram
    x, hh, hl = (lambda k: c.xT[:, k, :]), (lambda k: c.h_hi[:, k, :]), (lambda k: c.h_lo[:, k, :])
    norm(c, 1, DT, x, None, D, weight=lambda k: c.col("mix_norm_even", k), halves=(hh, hl),
         then=first_pieces(d["w_small"]))
    with ExitStack() as outer:
        low_rank = c.sb(outer, "low_rank", [P, 1, T])
        linear(c, d["w_small"], DT, 1, hh, hl, low_rank, then=first_pieces(d["w_ssd"][8:20]))
        small = low_rank[:, 0, :]
        with ExitStack() as ctx:
            proj = c.sb(ctx, "proj_ssd", [P, 20, T])
            z, xbc = proj[:, 0:8, :], proj[:, 8:20, :]
            linear(c, d["w_ssd"][8:20], DT, CONVT, hh, hl, xbc, then=first_pieces(d["w_ssd"][0:8]))
            with ExitStack() as inner:
                linear(c, d["w_ssd"][0:8], DT, DT, hh, hl, z, beside=conv_silu(c, inner, xbc))
            c.dve_done.close(CONVT)
            c.act_done.close(CONVT)
            y = xbc[:, 0:8, :]
            ssd(c, z, xbc, small, y)
            norm(c, 2, 4, lambda t: y[:, t, :], lambda t: y[:, t, :], 512, weight=lambda t: c.col("ssd_norm", t),
                 then=first_pieces(d["w_out_even"]))
            branch_out(c, d["w_out_even"], y, first_pieces(d["w_gla"]))
        with ExitStack() as ctx:
            proj = c.sb(ctx, "proj_gla", [P, 16, T])
            v = c.sb(ctx, "v", [P, NCH, D])
            B = c.sb(ctx, "B_gla", [P, 4, T])
            y = c.sb(ctx, "y_gla", [P, 8, T])
            linear(c, d["w_gla"], DT, 16, hh, hl, proj, then=first_pieces_tokens(d["w_v_even"]))
            q, k, g = proj[:, 0:4, :], proj[:, 4:8, :], proj[:, 8:16, :]
            linear_tokens(c, d["w_v_even"], DT, 2, hh, hl, v,
                          beside=(scaled(c, q, 4, 128.0 ** -0.5), silu_steps(c, g, 8)))
            c.g_ready.close(8)
            c.h_ready.close(1)
            gla_gates(c, small, d["gla_gk_w2"], B)
            gated_linear(c, "gla_", 4, 2, lambda i: q[:, i, :], lambda i: k[:, i, :], lambda i: B[:, i, :],
                         lambda j: v[:, j, :], lambda i: y[:, i, :])
            norm(c, 4, 2, lambda t: y[:, t, :], lambda t: y[:, t, :], 256,
                 weight=lambda t: c.col("gla_norm", t % 2), gate=lambda t: g[:, t, :],
                 then=first_pieces(d["w_out_even2"]))
            linear(c, d["w_out_even2"], DT, DT, hh, hl, c.xT, add=True, src=lambda t: y[:, t, :])


def branch_out(c, w, part, then):
    with ExitStack() as ctx:
        hi = c.sb(ctx, "part_hi", [P, DT, T], F32R)
        lo = c.sb(ctx, "part_lo", [P, DT, T], F32R)
        linear(c, w, DT, DT, lambda t: hi[:, t, :], lambda t: lo[:, t, :], c.xT, add=True,
               src=lambda t: part[:, t, :], then=then)


def swiglu(c, layer):
    d = c.dram
    x, hh, hl = (lambda k: c.xT[:, k, :]), (lambda k: c.h_hi[:, k, :]), (lambda k: c.h_lo[:, k, :])
    norm(c, 1, DT, x, None, D, weight=lambda k: c.col(f"ffn_norm{layer}", k), halves=(hh, hl),
         then=[d["w_gate_up"][layer, 0, :, 0:D], d["w_gate_up"][layer, 0, :, D:2 * D]])
    wgu = d["w_gate_up"]
    c.started = (0, 0)
    pairs = HT // 2
    wd, DW = d[f"w_down{layer}"], HT // 2 * P
    with ExitStack() as ctx:
        hid_hi = c.sb(ctx, f"hid_hi{layer}", [P, HT, T], F32R)
        hid_lo = c.sb(ctx, f"hid_lo{layer}", [P, HT, T], F32R)
        gate = c.sb(ctx, f"gate{layer}", [P, 2, T])
        loaded = (c.slot0_loaded, c.slot1_loaded)
        with c.nc.Block() as block:
            @block.sync
            def _(sp):
                with sp.Fori(1, HT) as i:
                    for u in range(2):
                        sp.wait_ge(c.lo_done.sem, c.lo_done.at(1 + u) + i * 2)
                        sp.dma_start(c.ring[:, u * SLOT:u * SLOT + D], wgu[layer, bass.ds(i, 1), :, u * D:(u + 1) * D]
                                     .rearrange("a p n -> p (a n)")).then_inc(loaded[u].sem, 16)
                sp.wait_ge(c.lo_done.sem, c.lo_done.at(2 + 2 * HT))
                for u in range(2):
                    sp.dma_start(c.ring[:, u * SLOT:u * SLOT + DW], wd[0, :, u * DW:(u + 1) * DW]
                                 ).then_inc(loaded[u].sem, 16)

            @block.scalar
            def _(act):
                def high(i, r):
                    for u in range(2):
                        at = slice((2 * u + r) * D, (2 * u + r + 1) * D)
                        act.wait_ge(loaded[u].sem, loaded[u].at(16) + i * 16)
                        act.wait_ge(c.piece_free.sem, c.piece_free.at(1 + u) + i * 2)
                        act.copy(c.w_hi[:, at], c.ring[:, u * SLOT:u * SLOT + D]).then_inc(c.hi_done.sem, 1)

                def silu(i, r):
                    act.wait_ge(c.piece_free.sem, c.piece_free.at(5) + i * 2)
                    act.wait_ge(c.bank_free.sem, c.bank_free.at(1) + i)
                    act.activation(gate[:, r, :], c.ps[:, 2 * r, :], ACT.Silu).then_inc(c.act_done.sem, 1)
                with act.Fori(0, pairs - 1) as p:
                    for r in range(2):
                        high(p * 2 + r + 1, (r + 1) % 2)
                        silu(p * 2 + r, r)
                high(HT - 1, 1)
                silu(HT - 2, 0)
                silu(HT - 1, 1)
                act.wait_ge(loaded[0].sem, loaded[0].at(16 * HT + 16))
                act.wait_ge(c.piece_free.sem, c.piece_free.at(3 + 2 * HT))
                act.copy(c.w_hi[:, 0:DW], c.ring[:, 0:DW]).then_inc(c.hi_done.sem, 1)

            @block.gpsimd
            def _(pool):
                def low(p, m):
                        u, at = m % 2, slice((2 * (m % 2) + m // 2) * D, (2 * (m % 2) + m // 2 + 1) * D)
                        pool.wait_ge(c.hi_done.sem, c.hi_done.at(1 + m) + p * 4)
                        pool.tensor_tensor(c.w_lo[:, at], c.ring[:, u * SLOT:u * SLOT + D], c.w_hi[:, at].bitcast(F32),
                                           ALU.subtract).then_inc(c.lo_done.sem, 1)
                low(0, 2)
                low(0, 3)
                with pool.Fori(1, pairs) as p:
                    for m in range(4):
                        low(p, m)
                pool.wait_ge(c.lo_done.sem, c.lo_done.at(2 + 2 * HT))
                pool.sem_inc(c.lo_done.sem, 2)
                pool.wait_ge(c.hi_done.sem, c.hi_done.at(2 * HT + 1))
                pool.tensor_tensor(c.w_lo[:, 0:DW], c.ring[:, 0:DW], c.w_hi[:, 0:DW].bitcast(F32), ALU.subtract
                                   ).then_inc(c.lo_done.sem, 1)

            @block.tensor
            def _(pe):
                pe.sem_inc(c.piece_free.sem, 4)
                with pe.Fori(0, pairs) as p:
                    for m in range(4):
                        pe.wait_ge(c.lo_done.sem, c.lo_done.at(3 + m) + p * 4)
                        pe.wait_ge(c.bank_free.sem, c.bank_free.at(1 + m // 2) + p * 2)
                        for k in range(DT):
                            w0 = (2 * (m % 2) + m // 2) * D
                            at = slice(w0 + k * P, w0 + (k + 1) * P)
                            mm = passes(pe, c.ps[:, m, :], c.w_hi[:, at], c.w_lo[:, at], hh(k), hl(k),
                                        k == 0, k == DT - 1)
                        mm.then_inc(c.piece_free.sem, 1)

            @block.vector
            def _(dve):
                dve.sem_inc(c.bank_free.sem, 2)
                with dve.Fori(0, pairs) as p:
                    for r in range(2):
                        i = p * 2 + r
                        tile = lambda t: t[:, bass.ds(i, 1), :].rearrange("p a t -> p (a t)")
                        dve.wait_ge(c.act_done.sem, c.act_done.at(1) + i)
                        dve.wait_ge(c.piece_free.sem, c.piece_free.at(6) + i * 2)
                        dve.tensor_tensor(gate[:, r, :], gate[:, r, :], c.ps[:, 2 * r + 1, :], ALU.mult
                                          ).then_inc(c.a_ready.sem, 1)
                        dve.wait_ge(c.a_ready.sem, c.a_ready.at(1) + i)
                        dve.tensor_copy(tile(hid_hi), gate[:, r, :]).then_inc(c.b_ready.sem, 1)
                        dve.wait_ge(c.b_ready.sem, c.b_ready.at(1) + i)
                        dve.tensor_tensor(tile(hid_lo), gate[:, r, :], tile(hid_hi).bitcast(F32), ALU.subtract
                                          ).then_inc(c.bank_free.sem, 1)
                dve.wait_ge(c.bank_free.sem, c.bank_free.at(HT + 2))
        c.slot0_loaded.close(16 * HT)
        c.slot1_loaded.close(16 * HT)
        c.hi_done.close(2 * HT)
        c.lo_done.close(2 * HT + 2)
        c.piece_free.close(2 * HT + 4)
        c.act_done.close(HT)
        c.a_ready.close(HT)
        c.b_ready.close(HT)
        c.bank_free.close(HT + 2)
        c.started = (2, 1)
        linear(c, d[f"w_down{layer}"], HT, DT, lambda k: hid_hi[:, k, :], lambda k: hid_lo[:, k, :], c.xT, add=True)


def rope(c, x, tiles):
    with ExitStack() as ctx:
        swap = c.sb(ctx, "swap", [P, P])
        cs = c.sb(ctx, "cos", [P, T])
        sn = c.sb(ctx, "sin", [P, T])
        load(c, [(swap[:], c.const("swap")), (cs[:], c.const("mla_cos")), (sn[:], c.const("mla_sin"))])
        rot = c.sb(ctx, "rot", [P, 2, T])
        with c.nc.Block() as block:
            @block.tensor
            def _(pe):
                for n, k in enumerate(tiles):
                    if n >= 2:
                        pe.wait_ge(c.a_ready.sem, c.a_ready.at(n - 1))
                    pe.matmul(c.ps[:, n % 2, :], swap[:], x(k), start=True, stop=True).then_inc(c.mm_done.sem, 1)

            @block.vector
            def _(dve):
                ch = Chain(c.dve_chain, dve)
                for n, k in enumerate(tiles):
                    dve.wait_ge(c.mm_done.sem, c.mm_done.at(n + 1))
                    dve.tensor_tensor(rot[:, n % 2, :], c.ps[:, n % 2, :], sn[:], ALU.mult).then_inc(c.a_ready.sem, 1)
                    ch.link(dve.tensor_tensor(x(k), x(k), cs[:], ALU.mult))
                    dve.wait_ge(c.a_ready.sem, c.a_ready.at(n + 1))
                    ch.link(dve.tensor_tensor(x(k), x(k), rot[:, n % 2, :], ALU.add))
                ch.close()
    c.mm_done.close(len(tiles))
    c.a_ready.close(len(tiles))


def attention(c, qn, qr, kn, kr, v, out, then):
    scale = 96.0 ** -0.5
    items = [(h, i) for h in range(16) for i in range(NCH)]
    ni = len(items)
    banks = (0, 1, 6)
    with ExitStack() as ctx:
        future = c.sb(ctx, "future", [P, P])
        pr = c.sb(ctx, "probs", [P, 3, T])
        pT = c.sb(ctx, "probsT", [P, 2, T])
        mx = c.sb(ctx, "row_max", [P, 3])
        nm = c.sb(ctx, "neg_max", [P, 3])
        sm = c.sb(ctx, "row_sum", [P, 3])
        load(c, [(future[:], c.const("future"))])
        with c.nc.Block() as block:
            start_pieces(c, block, then)

            @block.tensor
            def _(pe):
                def scores(n):
                    h, i = items[n]
                    w = P * (i + 1)
                    a, b = 64 * (h % 2), 32 * (h % 4)
                    if n >= 3:
                        pe.wait_ge(c.act_done.sem, c.act_done.at(n - 2))
                    pe.matmul(c.ps[:, banks[n % 3], 0:w], qn(h // 2)[a:a + 64, i * P:(i + 1) * P], kn(h // 2)[a:a + 64, 0:w],
                              start=True, stop=False)
                    pe.matmul(c.ps[:, banks[n % 3], 0:w], qr(h // 4)[b:b + 32, i * P:(i + 1) * P], kr[b:b + 32, 0:w],
                              start=False, stop=True).then_inc(c.mm_done.sem, 1)

                def weigh(n):
                    h, i = items[n]
                    if h % 2 == 0 and i == 0 and h >= 4:
                        pe.wait_ge(c.e_ready.sem, c.e_ready.at(h // 2 - 1))
                    pe.wait_ge(c.d_ready.sem, c.d_ready.at(n + 1))
                    a = 64 * (h % 2)
                    for j in range(i + 1):
                        mm = pe.matmul(c.ps[a:a + 64, 4 + (h // 2) % 2, i * P:(i + 1) * P], v(j)[:, 64 * h:64 * h + 64],
                                       pT[:, n % 2, j * P:(j + 1) * P], start=j == 0, stop=j == i)
                    mm.then_inc(c.f_ready.sem, 1)
                scores(0)
                scores(1)
                for n, (h, i) in enumerate(items):
                    if n + 2 < ni:
                        scores(n + 2)
                    pe.wait_ge(c.b_ready.sem, c.b_ready.at(n + 1))
                    if n >= 2:
                        pe.wait_ge(c.d_ready.sem, c.d_ready.at(n - 1))
                    for j in range(i + 1):
                        mm = pe.transpose(c.ps[:, 2 + n % 2, j * P:(j + 1) * P], pr[:, n % 3, j * P:(j + 1) * P], c.ident)
                    mm.then_inc(c.c_ready.sem, 1)
                    if n:
                        weigh(n - 1)
                weigh(ni - 1)

            @block.vector
            def _(dve):
                ch = Chain(c.dve_chain, dve)

                def top(n):
                    h, i = items[n]
                    dve.wait_ge(c.mm_done.sem, c.mm_done.at(n + 1))
                    d = c.ps[:, banks[n % 3], i * P:(i + 1) * P]
                    ch.link(dve.tensor_tensor(d, d, future[:], ALU.add))
                    ch.link(dve.reduce_max(mx[:, n % 3:n % 3 + 1], c.ps[:, banks[n % 3], 0:(i + 1) * P], AX.X))
                    dve.tensor_scalar(nm[:, n % 3:n % 3 + 1], mx[:, n % 3:n % 3 + 1], -scale, None, ALU.mult
                                      ).then_inc(c.a_ready.sem, 1)
                def keep(k):
                    dve.wait_ge(c.f_ready.sem, c.f_ready.at(8 * (k + 1)))
                    dve.tensor_copy(out(k), c.ps[:, 4 + k % 2, :]).then_inc(c.e_ready.sem, 1)
                top(0)
                top(1)
                for n, (h, i) in enumerate(items):
                    s = sm[:, n % 3:n % 3 + 1]
                    dve.wait_ge(c.act_done.sem, c.act_done.at(n + 1))
                    ch.link(dve.reciprocal(s, s))
                    dve.tensor_scalar(pr[:, n % 3, 0:(i + 1) * P], pr[:, n % 3, 0:(i + 1) * P], s, None, ALU.mult
                                      ).then_inc(c.b_ready.sem, 1)
                    if n + 2 < ni:
                        top(n + 2)
                    if n and items[n - 1][0] % 2 == 1 and items[n - 1][1] == 3:
                        keep(items[n - 1][0] // 2)
                    if n == ni - 1:
                        keep(7)
                dve.wait_ge(c.e_ready.sem, c.e_ready.at(8))
                ch.close()

            @block.scalar
            def _(act):
                def turn(n):
                    h, i = items[n]
                    act.wait_ge(c.c_ready.sem, c.c_ready.at(n + 1))
                    if n >= 2:
                        act.wait_ge(c.f_ready.sem, c.f_ready.at(n - 1))
                    act.copy(pT[:, n % 2, 0:(i + 1) * P], c.ps[:, 2 + n % 2, 0:(i + 1) * P]).then_inc(c.d_ready.sem, 1)
                high_pieces(c, act, then)
                for n, (h, i) in enumerate(items):
                    act.wait_ge(c.a_ready.sem, c.a_ready.at(n + 1))
                    if n >= 3:
                        act.wait_ge(c.c_ready.sem, c.c_ready.at(n - 2))
                    act.activation(pr[:, n % 3, 0:(i + 1) * P], c.ps[:, banks[n % 3], 0:(i + 1) * P], ACT.Exp,
                                   bias=nm[:, n % 3:n % 3 + 1], scale=scale,
                                   accum_out=sm[:, n % 3:n % 3 + 1]).then_inc(c.act_done.sem, 1)
                    if n >= 2:
                        turn(n - 2)
                turn(ni - 2)
                turn(ni - 1)
    for t, n in ((c.mm_done, ni), (c.a_ready, ni), (c.b_ready, ni), (c.c_ready, ni), (c.d_ready, ni),
                 (c.e_ready, 8), (c.f_ready, ni), (c.act_done, ni)):
        t.close(n)


def mla(c):
    d = c.dram
    x, hh, hl = (lambda k: c.xT[:, k, :]), (lambda k: c.h_hi[:, k, :]), (lambda k: c.h_lo[:, k, :])
    norm(c, 1, DT, x, None, D, weight=lambda k: c.col("mix_norm_odd", k), halves=(hh, hl),
         then=first_pieces(d["w_dqkv"]))
    with ExitStack() as ctx:
        ones64 = c.sb(ctx, "ones64", [P, P])
        ones32 = c.sb(ctx, "ones32", [P, P])
        load(c, [(ones64[:], c.const("ones64")), (ones32[:], c.const("ones32"))])
        lat = c.sb(ctx, "latent", [P, 6, T])
        q = c.sb(ctx, "q", [P, 12, T])
        kn = c.sb(ctx, "k_nope", [P, 8, T])
        v = c.sb(ctx, "v", [P, NCH, D])
        L, Q, K = (lambda k: lat[:, k, :]), (lambda k: q[:, k, :]), (lambda k: kn[:, k, :])
        linear(c, d["w_dqkv"], DT, 6, hh, hl, lat)
        norm(c, 1, 3, L, None, 384, weight=lambda k: c.col("q_lora_norm", k), halves=(hh, hl))
        kv = (lambda k: hh(3 + k)), (lambda k: hl(3 + k))
        norm(c, 1, 2, lambda k: L(3 + k), None, 256, weight=lambda k: c.col("kv_lora_norm", k), halves=kv)
        norm(c, 1, 1, lambda k: L(5), lambda k: L(5), 32, weight=lambda k: c.col("k_rope_norm"), ones=ones32,
             then=first_pieces(d["w_uq"]))
        linear(c, d["w_uq"], 3, 12, hh, hl, q, then=first_pieces(d["w_uk"]))
        linear(c, d["w_uk"], 2, 8, kv[0], kv[1], kn, then=first_pieces_tokens(d["w_uv"]))
        linear_tokens(c, d["w_uv"], 2, 2, kv[0], kv[1], v)
        norm(c, 8, 1, Q, Q, 64, weight=lambda k: c.col("q_nope_norm"), ones=ones64)
        norm(c, 4, 1, lambda k: Q(8 + k), lambda k: Q(8 + k), 32, weight=lambda k: c.col("q_rope_norm"), ones=ones32)
        norm(c, 8, 1, K, K, 64, weight=lambda k: c.col("k_nope_norm"), ones=ones64)
        rope(c, lambda k: Q(8 + k) if k < 4 else L(5), range(5))
        o = c.sb(ctx, "o", [P, DT, T])
        attention(c, Q, lambda k: Q(8 + k), K, L(5), lambda j: v[:, j, :], lambda k: o[:, k, :],
                  first_pieces(d["w_o"]))
        linear(c, d["w_o"], DT, DT, hh, hl, c.xT, add=True, src=lambda k: o[:, k, :])


def hgrn_gates(c, ctx, f, B, lower):
    keep = c.sb(ctx, "keep", [P, T])
    lg = c.sb(ctx, "log_forget", [P, 2, T])
    load(c, [(keep[:], c.const("keep"))])

    def bounds(act):
        act.wait_ge(c.a_ready.sem, c.a_ready.at(2))
        act.activation(lower[:, 0:16], lower[:, 0:16], ACT.Exp).then_inc(c.b_ready.sem, 1)

    def sigmoid(k):
        return lambda act: act.activation(f[:, k, :], f[:, k, :], ACT.Sigmoid).then_inc(c.act_done.sem, 1)

    def log(k):
        def step(act):
            act.wait_ge(c.dve_done.sem, c.dve_done.at(k + 1))
            if k >= 2:
                act.wait_ge(c.d_ready.sem, c.d_ready.at(k - 1))
            act.activation(lg[:, k % 2, :], f[:, k, :], ACT.Ln).then_inc(c.c_ready.sem, 1)
        return step

    def vector(dve):
        ch = Chain(c.dve_chain, dve)
        a0, a1 = COL_AT["lb0"][0], COL_AT["lb1"][0]
        lb0, lb1 = c.cols[:, a0:a0 + 8], c.cols[:, a1:a1 + 8]
        ch.link(dve.tensor_tensor(lower[:, 16:24], lb0, lb1, ALU.max))
        dve.tensor_tensor(lower[:, 0:8], lb0, lower[:, 16:24], ALU.subtract).then_inc(c.a_ready.sem, 1)
        dve.tensor_tensor(lower[:, 8:16], lb1, lower[:, 16:24], ALU.subtract).then_inc(c.a_ready.sem, 1)
        dve.wait_ge(c.b_ready.sem, c.b_ready.at(1))
        ch.link(dve.tensor_tensor(lower[:, 8:16], lower[:, 0:8], lower[:, 8:16], ALU.add))
        ch.link(dve.reciprocal(lower[:, 8:16], lower[:, 8:16]))
        ch.link(dve.tensor_tensor(lower[:, 0:8], lower[:, 0:8], lower[:, 8:16], ALU.mult))
        ch.link(dve.tensor_scalar(lower[:, 8:16], lower[:, 0:8], -1.0, 1.0, ALU.mult, ALU.add))
        for k in range(8):
            dve.wait_ge(c.act_done.sem, c.act_done.at(k + 1))
            dve.tensor_scalar(f[:, k, :], f[:, k, :], lower[:, 8 + k:9 + k], lower[:, k:k + 1],
                              ALU.mult, ALU.add).then_inc(c.dve_done.sem, 1)
        for k in range(8):
            dve.wait_ge(c.c_ready.sem, c.c_ready.at(k + 1))
            dve.tensor_tensor_scan(B[:, k, :], keep[:], lg[:, k % 2, :], 0.0, ALU.mult, ALU.add
                                   ).then_inc(c.d_ready.sem, 1)
            ch.link(dve.tensor_scalar(f[:, k, :], f[:, k, :], -1.0, 1.0, ALU.mult, ALU.add))
        dve.wait_ge(c.d_ready.sem, c.d_ready.at(8))
        ch.close()

    return vector, [bounds] + [sigmoid(k) for k in range(8)] + [log(k) for k in range(8)]


def retention(c, qk, v, out, then):
    with ExitStack() as ctx:
        cs = c.sb(ctx, "cos", [P, T])
        sn = c.sb(ctx, "sin", [P, T])
        dec = c.sb(ctx, "gammas", [P, 4, T])
        tmp = c.sb(ctx, "rotary", [P, 2, T])
        A = c.sb(ctx, "scores", [P, 2, WID])
        load(c, [(cs[:], c.const("ret_cos")), (sn[:], c.const("ret_sin"))] +
             [(dec[:, h, :], c.const(f"ret_decay{h}")) for h in range(4)])
        with c.nc.Block() as block:
            start_pieces(c, block, then)

            @block.scalar
            def _(act):
                high_pieces(c, act, then)
                for n in range(16):
                    act.wait_ge(c.d_ready.sem, c.d_ready.at(n + 1))
                    act.copy(out(n), c.ps[:, 2 + n % 4, :]).then_inc(c.e_ready.sem, 1)

            @block.vector
            def _(dve):
                ch = Chain(c.dve_chain, dve)

                def rotate(h):
                    for s in range(2):
                        x1, x2 = qk(4 * h + 2 * s), qk(4 * h + 2 * s + 1)
                        dve.tensor_tensor(tmp[:, 0, :], x1, sn[:], ALU.mult).then_inc(c.a_ready.sem, 1)
                        dve.tensor_tensor(tmp[:, 1, :], x2, sn[:], ALU.mult).then_inc(c.a_ready.sem, 1)
                        dve.wait_ge(c.a_ready.sem, c.a_ready.at(4 * h + 2 * s + 2))
                        ch.link(dve.tensor_tensor(x1, x1, cs[:], ALU.mult))
                        ch.link(dve.tensor_tensor(x2, x2, cs[:], ALU.mult))
                        ch.link(dve.tensor_tensor(x1, x1, tmp[:, 1, :], ALU.subtract))
                        ch.link(dve.tensor_tensor(x2, x2, tmp[:, 0, :], ALU.add))
                    dve.sem_inc(c.b_ready.sem, 1)
                rotate(0)
                for h in range(4):
                    if h < 3:
                        rotate(h + 1)
                    if h >= 2:
                        dve.wait_ge(c.d_ready.sem, c.d_ready.at(4 * (h - 1)))
                    for j in range(NCH):
                        n = NCH * h + j
                        dve.wait_ge(c.mm_done.sem, c.mm_done.at(n + 1))
                        dve.tensor_tensor(A[:, h % 2, OFF[j]:OFF[j] + T - j * P], c.ps[:, n % 2, 0:T - j * P],
                                          dec[:, h, 0:T - j * P], ALU.mult).then_inc(c.c_ready.sem, 1)
                dve.wait_ge(c.c_ready.sem, c.c_ready.at(16))
                ch.close()

            @block.tensor
            def _(pe):
                def scores(h):
                    pe.wait_ge(c.b_ready.sem, c.b_ready.at(h + 1))
                    for j in range(NCH):
                        n = NCH * h + j
                        if n >= 2:
                            pe.wait_ge(c.c_ready.sem, c.c_ready.at(n - 1))
                        for y in range(2):
                            mm = pe.matmul(c.ps[:, n % 2, 0:T - j * P], qk(4 * h + 2 + y)[:, j * P:(j + 1) * P],
                                           qk(4 * h + y)[:, j * P:T], start=y == 0, stop=y == 1)
                        mm.then_inc(c.mm_done.sem, 1)
                scores(0)
                for h in range(4):
                    if h < 3:
                        scores(h + 1)
                    pe.wait_ge(c.c_ready.sem, c.c_ready.at(4 * h + 4))
                    for x in range(4):
                        if h:
                            pe.wait_ge(c.e_ready.sem, c.e_ready.at(4 * (h - 1) + x + 1))
                        for j in range(NCH):
                            mm = pe.matmul(c.ps[:, 2 + x, j * P:T], v(j)[:, h * T + x * P:h * T + (x + 1) * P],
                                           A[:, h % 2, OFF[j]:OFF[j] + T - j * P], start=j == 0, stop=j == NCH - 1)
                        mm.then_inc(c.d_ready.sem, 1)
    for t, n in ((c.a_ready, 16), (c.b_ready, 4), (c.c_ready, 16), (c.mm_done, 16), (c.d_ready, 16), (c.e_ready, 16)):
        t.close(n)


def merge(c, a, b, ga, gb, then):
    with c.nc.Block() as block:
        start_pieces(c, block, then)

        @block.scalar
        def _(act):
            high_pieces(c, act, then)

        @block.vector
        def _(dve):
            ch = Chain(c.dve_chain, dve)
            for k in range(DT):
                dve.tensor_tensor(a(k), a(k), ga(k), ALU.mult).then_inc(c.dve_done.sem, 1)
                ch.link(dve.tensor_tensor(b(k), b(k), gb(k), ALU.mult))
                dve.wait_ge(c.dve_done.sem, c.dve_done.at(k + 1))
                ch.link(dve.tensor_tensor(a(k), a(k), b(k), ALU.add))
            ch.close()
    c.dve_done.close(DT)


def mix2(c):
    d = c.dram
    x, hh, hl = (lambda k: c.xT[:, k, :]), (lambda k: c.h_hi[:, k, :]), (lambda k: c.h_lo[:, k, :])
    norm(c, 1, DT, x, None, D, weight=lambda k: c.col("norm_mix_w_2", k), halves=(hh, hl),
         then=first_pieces(d["w_hg"]))
    with ExitStack() as outer:
        y_hg = c.sb(outer, "y_hg", [P, DT, T])
        v = y_hg[:].rearrange("p (j a) t -> p j (a t)", j=NCH)
        with ExitStack() as ctx:
            proj = c.sb(ctx, "proj_hg", [P, 24, T])
            q, f, g = proj[:, 0:8, :], proj[:, 8:16, :], proj[:, 16:24, :]
            linear(c, d["w_hg"], DT, 24, hh, hl, proj, then=first_pieces_tokens(d["w_hg_v"]))
            with ExitStack() as inner:
                B = c.sb(inner, "B_hg", [P, 8, T])
                with ExitStack() as gates:
                    lower = c.sb(gates, "lower", [P, 24])
                    vector, steps = hgrn_gates(c, gates, f, B, lower)
                    scale = scaled(c, q, 8, 128.0 ** -0.5)
                    linear_tokens(c, d["w_hg_v"], DT, 2, hh, hl, v,
                                  beside=(lambda dve: (vector(dve), scale(dve)), steps + silu_steps(c, g, 8)))
                for t, n in ((c.a_ready, 2), (c.b_ready, 1), (c.act_done, 8), (c.dve_done, 8), (c.c_ready, 8),
                             (c.d_ready, 8), (c.g_ready, 8), (c.h_ready, 1)):
                    t.close(n)
                gated_linear(c, "hg_", 8, 1, lambda i: q[:, i, :], lambda i: f[:, i, :], lambda i: B[:, i, :],
                             lambda j: v[:, j, :], lambda i: q[:, i, :])
            norm(c, 8, 1, lambda t: q[:, t, :], lambda t: q[:, t, :], 128,
                 weight=lambda t: c.col("hg_norm_w_2", t), gate=lambda t: g[:, t, :], few=True,
                 then=first_pieces(d["w_branch_hg"]))
            with ExitStack() as inner:
                hi = c.sb(inner, "o_hi", [P, DT, T], F32R)
                lo = c.sb(inner, "o_lo", [P, DT, T], F32R)
                o = (lambda t: hi[:, t, :]), (lambda t: lo[:, t, :])
                linear(c, d["w_branch_hg"], DT, DT, *o, y_hg, src=lambda t: q[:, t, :], then=first_pieces(d["w_ret"]))
        with ExitStack() as ctx:
            qk = c.sb(ctx, "qk_ret", [P, 16, T])
            with ExitStack() as inner:
                v = c.sb(inner, "v_ret", [P, NCH, 2 * D])
                linear(c, d["w_ret"], DT, 16, hh, hl, qk, then=first_pieces_tokens(d["w_ret_v"]))
                linear_tokens(c, d["w_ret_v"], DT, 4, hh, hl, v)
                retention(c, lambda k: qk[:, k, :], lambda j: v[:, j, :], lambda k: qk[:, k, :],
                          first_pieces(d["w_ret_g"]))
            with ExitStack() as inner:
                g = c.sb(inner, "g_ret", [P, 16, T])
                linear(c, d["w_ret_g"], DT, 16, hh, hl, g, beside=curved(c, g, ACT.Silu))
                c.act_done.close(16)
                norm(c, 4, 4, lambda t: qk[:, t, :], lambda t: qk[:, t, :], 512, gate=lambda t: g[:, t, :], few=True,
                     then=first_pieces(d["w_branch_ret0"]))
            y_ret = c.sb(ctx, "y_ret", [P, DT, T])
            with ExitStack() as inner:
                hi = c.sb(inner, "o_hi", [P, DT, T], F32R)
                lo = c.sb(inner, "o_lo", [P, DT, T], F32R)
                o = (lambda t: hi[:, t, :]), (lambda t: lo[:, t, :])
                for s in range(2):
                    linear(c, d[f"w_branch_ret{s}"], DT, DT, *o, y_ret, add=s == 1, src=lambda t: qk[:, 8 * s + t, :],
                           then=first_pieces(d[("w_branch_ret1", "w_gates")[s]]))
            linear(c, d["w_gates"], DT, 16, hh, hl, qk, beside=curved(c, qk, ACT.Sigmoid))
            c.act_done.close(16)
            merge(c, lambda k: y_hg[:, k, :], lambda k: y_ret[:, k, :], lambda k: qk[:, k, :], lambda k: qk[:, 8 + k, :],
                  first_pieces(d["w_out_2"]))
        linear(c, d["w_out_2"], DT, DT, hh, hl, c.xT, add=True, src=lambda k: y_hg[:, k, :])


K16 = 16
LOW = -3e38
GI = 4


class Lanes:

    def __init__(self, ch, lanes):
        self.ch, self.lanes = ch, lanes

    def run(self, steps):
        ch, tally = self.ch, self.ch.tally
        start = ch.n
        for s, step in enumerate(steps):
            for lane in range(self.lanes):
                if s:
                    ch.engine.wait_ge(tally.sem, tally.at(start + (s - 1) * self.lanes + lane + 1))
                step(lane).then_inc(tally.sem, 1)
        ch.n += len(steps) * self.lanes
        ch.engine.wait_ge(tally.sem, tally.at(ch.n))


def top16(dve, values, alt, out_v, out_i):
    return [lambda n: dve.max(out_v(n)[:, 0:8], values(n)),
            lambda n: dve.max_index(out_i(n)[:, 0:8], out_v(n)[:, 0:8], values(n)),
            lambda n: dve.match_replace(alt(n), out_v(n)[:, 0:8], values(n), LOW),
            lambda n: dve.max(out_v(n)[:, 8:16], alt(n)),
            lambda n: dve.max_index(out_i(n)[:, 8:16], out_v(n)[:, 8:16], alt(n))]


def peer_choose(c, hh, hl, IT, JT, GT):
    nc = c.nc
    w = c.dram["w_peer_q"]
    NM = 16
    with ExitStack() as ctx:
        keys = c.sb(ctx, "keys", [P, NM * P])
        iota = c.sb(ctx, "iota", [P, P])
        query = c.sb(ctx, "query", [P, 2, T])
        sc = c.sb(ctx, "sub_scores", [P, 2, NCH, P])
        alt = c.sb(ctx, "less_top8", [P, 4, 2 * P])
        tv = c.sb(ctx, "top_values", [P, NCH, NM, K16])
        ti = c.sb(ctx, "top_index", [P, NCH, NM, K16], U32)
        cand = c.sb(ctx, "candidates", [P, NCH, 2 * P])
        bv = c.sb(ctx, "best_values", [P, NCH, 8, K16])
        bc = c.sb(ctx, "best_place", [P, NCH, 8, K16], U32)
        loaded = (c.slot0_loaded, c.slot1_loaded)
        load(c, [(keys[:], c.dram["peer_keys"]), (iota[:], c.const("iota"))])
        with nc.Block() as block:
            @block.sync
            def _(sp):
                for m in range(2, NM):
                    s = m % 2
                    sp.wait_ge(c.lo_done.sem, c.lo_done.at(m + 1))
                    sp.dma_start(c.ring[:, s * SLOT:s * SLOT + D], w[m, :, :]).then_inc(loaded[s].sem, 16)

            @block.gpsimd
            def _(pool):
                for m in range(2, NM):
                    at = slice(m % 2 * SLOT, m % 2 * SLOT + D)
                    pool.wait_ge(c.hi_done.sem, c.hi_done.at(m + 1))
                    pool.tensor_tensor(c.w_lo[:, at], c.ring[:, at], c.w_hi[:, at].bitcast(F32), ALU.subtract
                                       ).then_inc(c.lo_done.sem, 1)

            @block.scalar
            def _(act):
                def high(m):
                    at = slice(m % 2 * SLOT, m % 2 * SLOT + D)
                    act.wait_ge(loaded[m % 2].sem, loaded[m % 2].at(16 * (m // 2 + 1)))
                    act.wait_ge(c.mm_done.sem, c.mm_done.at(m - 1))
                    act.copy(c.w_hi[:, at], c.ring[:, at]).then_inc(c.hi_done.sem, 1)

                def keep_scores(m):
                    act.wait_ge(c.b_ready.sem, c.b_ready.at(m + 1))
                    if m >= 2:
                        act.wait_ge(c.d_ready.sem, c.d_ready.at(m - 1))
                    act.copy(sc[:, m % 2, :, :].rearrange("p t n -> p (t n)"), c.ps[:, 2 + m % 2, :]
                             ).then_inc(c.c_ready.sem, 1)
                for m in range(NM):
                    if 2 <= m + 1 < NM:
                        high(m + 1)
                    act.wait_ge(c.mm_done.sem, c.mm_done.at(m + 1))
                    if m >= 2:
                        act.wait_ge(c.b_ready.sem, c.b_ready.at(m - 1))
                    act.copy(query[:, m % 2, :], c.ps[:, m % 2, :]).then_inc(c.a_ready.sem, 1)
                    if m:
                        keep_scores(m - 1)
                keep_scores(NM - 1)

            @block.tensor
            def _(pe):
                def scores(m):
                    pe.wait_ge(c.a_ready.sem, c.a_ready.at(m + 1))
                    if m >= 2:
                        pe.wait_ge(c.c_ready.sem, c.c_ready.at(m - 1))
                    for t in range(NCH):
                        mm = pe.matmul(c.ps[:, 2 + m % 2, t * P:(t + 1) * P], query[:, m % 2, t * P:(t + 1) * P],
                                       keys[:, m * P:(m + 1) * P], start=True, stop=True)
                    mm.then_inc(c.b_ready.sem, 1)
                for m in range(NM):
                    pe.wait_ge(c.lo_done.sem, c.lo_done.at(m + 3))
                    if m >= 2:
                        pe.wait_ge(c.a_ready.sem, c.a_ready.at(m - 1))
                    for k in range(DT):
                        at = slice(m % 2 * SLOT + k * P, m % 2 * SLOT + (k + 1) * P)
                        mm = passes(pe, c.ps[:, m % 2, :], c.w_hi[:, at], c.w_lo[:, at], hh(k), hl(k),
                                    k == 0, k == DT - 1)
                    mm.then_inc(c.mm_done.sem, 1)
                    if m:
                        scores(m - 1)
                scores(NM - 1)

            @block.vector
            def _(dve):
                ch = Chain(c.dve_chain, dve)
                for m in range(NM):
                    dve.wait_ge(c.c_ready.sem, c.c_ready.at(m + 1))
                    Lanes(ch, NCH).run(top16(dve, lambda t: sc[:, m % 2, t, :], lambda t: alt[:, t, 0:P],
                                             lambda t: tv[:, t, m, :], lambda t: ti[:, t, m, :]))
                    dve.sem_inc(c.d_ready.sem, 1)
                    if m % 2 == 0:
                        continue
                    h = m // 2
                    ch.link(dve.tensor_tensor(cand[:].rearrange("p t (i j) -> p t i j", j=K16),
                                              tv[:, :, m - 1, :].unsqueeze(3).broadcast_to([P, NCH, K16, K16]),
                                              tv[:, :, m, :].unsqueeze(2).broadcast_to([P, NCH, K16, K16]), ALU.add))
                    Lanes(ch, NCH).run(top16(dve, lambda t: cand[:, t, :], lambda t: alt[:, t, :],
                                             lambda t: bv[:, t, h, :], lambda t: bc[:, t, h, :]))
                ch.close()
        for t in (c.hi_done, c.lo_done, c.mm_done, c.a_ready, c.b_ready, c.c_ready, c.d_ready):
            t.close(NM)
        c.lo_done.close(2)
        c.started = (0, 0)
        c.slot0_loaded.close(8 * NM)
        c.slot1_loaded.close(8 * NM)
        tf = c.sb(ctx, "top_index_f", [P, 2, NM, K16])
        top = c.sb(ctx, "largest", [P, 8])
        half = c.sb(ctx, "place_half", [P, 2, P], U32)
        hf = c.sb(ctx, "place_half_f", [P, 2, P])
        hot = c.sb(ctx, "hot", [P, 4, P, K16])
        rs = c.sb(ctx, "gate_sum", [P, 8])
        IJG = c.sb(ctx, "chosen", [P, 3, P])
        with nc.Block() as block:
            @block.tensor
            def _(pe):
                for t in range(NCH):
                    pe.wait_ge(c.d_ready.sem, c.d_ready.at(t + 1))
                    for x in range(3):
                        mm = pe.transpose(c.ps[:, t % 2, x * P:(x + 1) * P], IJG[:, x, :], c.ident)
                    mm.then_inc(c.e_ready.sem, 1)

            @block.scalar
            def _(act):
                for t in range(NCH):
                    act.wait_ge(c.g_ready.sem, c.g_ready.at(t + 1))
                    act.activation(bv[:, t], bv[:, t], ACT.Exp).then_inc(c.h_ready.sem, 1)
                    act.wait_ge(c.e_ready.sem, c.e_ready.at(t + 1))
                    for x, to in enumerate((IT, JT, GT)):
                        act.copy(to[:, t * P:(t + 1) * P], c.ps[:, t % 2, x * P:(x + 1) * P]).then_inc(c.act_done.sem, 1)
                act.wait_ge(c.act_done.sem, c.act_done.at(3 * NCH))

            @block.gpsimd
            def _(pool):
                for t in range(NCH):
                    for side in range(2):
                        idx = tf[:, t % 2].rearrange("p (h s) m -> p h s m", s=2)[:, :, side, :]
                        view = hot[:, 2 * (t % 2) + side, :, :].rearrange("p (h k) m -> p h k m", k=K16)
                        pool.wait_ge(c.a_ready.sem, c.a_ready.at(2 * t + side + 1))
                        pool.tensor_tensor(view, view, idx.unsqueeze(2).broadcast_to([P, 8, K16, K16]), ALU.mult
                                           ).then_inc(c.b_ready.sem, 1)

            @block.vector
            def _(dve):
                ch = Chain(c.dve_chain, dve)

                def gates(t):
                    dve.wait_ge(c.h_ready.sem, c.h_ready.at(t + 1))
                    ch.link(dve.tensor_reduce(rs[:], bv[:, t], AX.X, ALU.add))
                    ch.link(dve.reciprocal(rs[:], rs[:]))
                    if t:
                        dve.wait_ge(c.e_ready.sem, c.e_ready.at(t))
                    ch.link(dve.tensor_tensor(IJG[:, 2, :].rearrange("p (h k) -> p h k", k=K16), bv[:, t],
                                              rs[:].unsqueeze(2).broadcast_to([P, 8, K16]), ALU.mult))
                    for side in range(2):
                        dve.wait_ge(c.b_ready.sem, c.b_ready.at(2 * t + side + 1))
                        ch.link(dve.tensor_reduce(IJG[:, side, :], hot[:, 2 * (t % 2) + side, :, :], AX.X, ALU.add))
                    dve.sem_inc(c.d_ready.sem, 1)
                for t in range(NCH):
                    ch.link(dve.tensor_copy(tf[:, t % 2], ti[:, t, :, :]))
                    ch.link(dve.tensor_copy(top[:], bv[:, t, :, 0]))
                    dve.tensor_tensor(bv[:, t], bv[:, t], top[:].unsqueeze(2).broadcast_to([P, 8, K16]), ALU.subtract
                                      ).then_inc(c.g_ready.sem, 1)
                    place = bc[:, t].rearrange("p h k -> p (h k)")
                    steps = [lambda s: dve.tensor_scalar(half[:, s, :], place, (4, 15)[s], None,
                                                         (ALU.logical_shift_right, ALU.bitwise_and)[s]),
                             lambda s: dve.tensor_copy(hf[:, s, :], half[:, s, :]),
                             lambda s: dve.tensor_tensor(hot[:, 2 * (t % 2) + s, :, :], iota[:, 0:K16].unsqueeze(1)
                                                         .broadcast_to([P, P, K16]), hf[:, s, :].unsqueeze(2)
                                                         .broadcast_to([P, P, K16]), ALU.is_equal)]
                    Lanes(ch, 2).run(steps)
                    dve.sem_inc(c.a_ready.sem, 2)
                    if t:
                        gates(t - 1)
                gates(NCH - 1)
                ch.close()
        for t, n in ((c.a_ready, 8), (c.b_ready, 8), (c.d_ready, 4), (c.e_ready, 4), (c.g_ready, 4), (c.h_ready, 4),
                     (c.act_done, 12)):
            t.close(n)


def peer_gates(c, IT, JT, GT):
    nc = c.nc
    SUB, SLOTS = 4, 4
    groups = P // SUB
    with ExitStack() as ctx:
        iota = c.sb(ctx, "iota", [P, P])
        hot_i = c.sb(ctx, "hot_i", [P, SLOTS, SUB, P])
        hot_j = c.sb(ctx, "gate_j", [P, SLOTS, SUB, P])
        stage = c.sb(ctx, "gate_stage", [P, P, P])
        more = c.sb(ctx, "gate_stage_more", [P, PARTS])
        wide = lambda x: x.rearrange("p (i t) -> p i t", t=P)
        part = PARTS // P
        places = ([(0, stage[:])],
                  [(n * part, wide(x)) for n, x in enumerate((c.ring[:], c.w_hi[:].bitcast(F32),
                                                              c.w_lo[:].bitcast(F32), more[:]))])
        stored = (c.stored, c.h_ready)
        load(c, [(iota[:], c.const("iota"))])
        total = NCH * groups

        def copies(t):
            return sum(groups * len(places[u % 2]) for u in range(t))
        with nc.Block() as block:
            @block.vector
            def _(dve):
                with dve.Fori(0, total // SLOTS) as p:
                    for r in range(SLOTS):
                        g = p * SLOTS + r
                        dve.wait_ge(c.b_ready.sem, c.b_ready.at(1) + g)
                        for hot, index, made in ((hot_j, JT, c.a_ready), (hot_i, IT, c.dve_done)):
                            dve.tensor_tensor(hot[:, r, :, :], iota[:].unsqueeze(1).broadcast_to([P, SUB, P]),
                                              index[:, bass.ds(g * SUB, SUB)].unsqueeze(2).broadcast_to([P, SUB, P]),
                                              ALU.is_equal).then_inc(made.sem, 1)

            @block.gpsimd
            def _(pool):
                with pool.Fori(0, total // SLOTS) as p:
                    for r in range(SLOTS):
                        g = p * SLOTS + r
                        pool.wait_ge(c.a_ready.sem, c.a_ready.at(1) + g)
                        pool.tensor_tensor(hot_j[:, r, :, :], hot_j[:, r, :, :],
                                           GT[:, bass.ds(g * SUB, SUB)].unsqueeze(2).broadcast_to([P, SUB, P]),
                                           ALU.mult).then_inc(c.pool_done.sem, 1)

            @block.tensor
            def _(pe):
                pe.sem_inc(c.b_ready.sem, SLOTS)
                with pe.Fori(0, total // SLOTS) as p:
                    for r in range(SLOTS):
                        pe.wait_ge(c.dve_done.sem, c.dve_done.at(1) + p * SLOTS + r)
                        pe.wait_ge(c.pool_done.sem, c.pool_done.at(1) + p * SLOTS + r)
                        pe.wait_ge(c.bank_free.sem, c.bank_free.at(1) + p * SLOTS + r)
                        for s in range(SUB):
                            mm = pe.matmul(c.ps[:, r, s * P:(s + 1) * P], hot_j[:, r, s, :], hot_i[:, r, s, :],
                                           start=True, stop=True)
                        mm.then_inc(c.b_ready.sem, 1)

            @block.scalar
            def _(act):
                act.sem_inc(c.bank_free.sem, SLOTS)
                for t in range(NCH):
                    if t >= 2:
                        act.wait_ge(stored[t % 2].sem, stored[t % 2].at(16 * len(places[t % 2])))
                    with act.Fori(0, groups // SLOTS) as p:
                        for r in range(SLOTS):
                            act.wait_ge(c.b_ready.sem, c.b_ready.at(1 + SLOTS + t * groups) + p * SLOTS + r)
                            for i0, place in places[t % 2]:
                                n = place.shape[1]
                                ins = act.copy(place[:, :, bass.ds((p * SLOTS + r) * SUB, SUB)].rearrange("p i t -> p t i"),
                                               c.ps[:, r, :].rearrange("p (t i) -> p t i", i=P)[:, :, i0:i0 + n])
                                ins.then_inc(c.act_done.sem, 1)
                            act.wait_ge(c.act_done.sem, c.act_done.at(copies(t)) + (p * SLOTS + r + 1) * len(places[t % 2]))
                            act.sem_inc(c.bank_free.sem, 1)

            @block.sync
            def _(sp):
                for t in range(NCH):
                    sp.wait_ge(c.bank_free.sem, c.bank_free.at(SLOTS + groups * (t + 1)))
                    for i0, place in places[t % 2]:
                        sp.dma_start(c.dram["gates"][:, t, i0:i0 + place.shape[1], :], place
                                     ).then_inc(stored[t % 2].sem, 16)
                for s in range(2):
                    sp.wait_ge(stored[s].sem, stored[s].at(16 * NCH // 2 * len(places[s])))
    n_copies = copies(NCH)
    for t, n in ((c.pool_done, total), (c.a_ready, total), (c.dve_done, total), (c.b_ready, total + SLOTS),
                 (c.bank_free, total + SLOTS), (c.act_done, n_copies),
                 (stored[0], 16 * NCH // 2), (stored[1], 64 * NCH // 2)):
        t.close(n)


def peer_experts(c):
    nc, d = c.nc, c.dram
    groups = P // GI
    BODY = 2 * GI
    with ExitStack() as ctx:
        v_hi = c.sb(ctx, "v_hi", [P, BODY, D], F32R)
        v_lo = c.sb(ctx, "v_lo", [P, BODY, D], F32R)
        w_hi = c.sb(ctx, "weighted_hi", [P, BODY, T], F32R)
        w_lo = c.sb(ctx, "weighted_lo", [P, BODY, T], F32R)
        gs = c.sb(ctx, "gate_slots", [P, 2, T])
        gelu = c.sb(ctx, "gelu", [P, 2, T])
        u_loaded = (c.slot0_loaded, c.slot1_loaded)
        v_loaded = (c.h_ready, c.pool_done)
        g_loaded = (c.loaded, c.pool_chain)
        v_hi_done, v_lo_done, sum_done, sum_free = c.a_ready, c.b_ready, c.d_ready, c.e_ready
        gated, w_hi_done, w_lo_done = c.f_ready, c.g_ready, c.dve_done
        u_raw = lambda r: c.ring[:, r * D:(r + 1) * D]
        v_raw = lambda r: c.ring[:, (2 + r) * D:(3 + r) * D]
        u_half = lambda t, r: t[:, r * D:(r + 1) * D]

        def over_blocks(engine, first, step):
            first(0, 0)
            with engine.Fori(0, P // BODY - 1) as p:
                for i in range(BODY):
                    step(p * BODY + i, i, p * 2 + i // GI, True)
            for i in range(BODY):
                step(P - BODY + i, i, groups - 2 + i // GI, i < BODY - 1)

        with nc.Block() as block:
            @block.sync
            def _(sp):
                def rows(n, r):
                    sp.wait_ge(c.lo_done.sem, c.lo_done.at(1) + n)
                    sp.dma_start(u_raw(r), d["expert_u"][bass.ds(n, 1), :, :].rearrange("a p n -> p (a n)")
                                 ).then_inc(u_loaded[r].sem, 16)
                    sp.wait_ge(v_lo_done.sem, v_lo_done.at(1) + n)
                    sp.dma_start(v_raw(r), d["expert_v"][bass.ds(n, 1), :, :].rearrange("a p n -> p (a n)")
                                 ).then_inc(v_loaded[r].sem, 16)

                def gates(n, r):
                    sp.wait_ge(gated.sem, gated.at(1) + n)
                    sp.dma_start(gs[:, r, :].rearrange("p (n t) -> p n t", t=P),
                                 d["gates"][:, :, bass.ds(n, 1), :].rearrange("p n a t -> p n (a t)")
                                 ).then_inc(g_loaded[r].sem, 16)
                rows(0, 0)
                rows(1, 1)
                gates(0, 0)
                with sp.Fori(1, P // 2) as p:
                    for r in range(2):
                        rows(p * 2 + r, r)
                        gates(p * 2 + r - 1, 1 - r)
                gates(P - 1, 1)

            @block.scalar
            def _(act):
                act.sem_inc(c.act_done.sem, 2)

                def u_high(n, r):
                    act.wait_ge(u_loaded[r].sem, u_loaded[r].at(16 - 8 * r) + n * 8)
                    act.wait_ge(c.mm_done.sem, c.mm_done.at(1) + n)
                    act.copy(u_half(c.w_hi, r), u_raw(r)).then_inc(c.hi_done.sem, 1)

                def step(n, i, g, more):
                    r = i % 2
                    if more:
                        u_high(n + 1, 1 - r)
                    act.wait_ge(v_loaded[r].sem, v_loaded[r].at(16 - 8 * r) + n * 8)
                    act.wait_ge(sum_done.sem, sum_done.at(DT) + g * DT)
                    act.copy(v_hi[:, i, :], v_raw(r)).then_inc(v_hi_done.sem, 1)
                    act.wait_ge(c.mm_done.sem, c.mm_done.at(3) + n)
                    act.wait_ge(gated.sem, gated.at(1) + n)
                    act.activation(gelu[:, r, :], c.ps[:, r, :], ACT.Gelu_apprx_tanh).then_inc(c.act_done.sem, 1)
                over_blocks(act, u_high, step)

            @block.gpsimd
            def _(pool):
                pool.sem_inc(c.lo_done.sem, 2)
                pool.sem_inc(v_lo_done.sem, 2)

                def u_low(n, r):
                    pool.wait_ge(c.hi_done.sem, c.hi_done.at(1) + n)
                    pool.tensor_tensor(u_half(c.w_lo, r), u_raw(r), u_half(c.w_hi, r).bitcast(F32), ALU.subtract
                                       ).then_inc(c.lo_done.sem, 1)

                def step(n, i, g, more):
                    if more:
                        u_low(n + 1, 1 - i % 2)
                    pool.wait_ge(v_hi_done.sem, v_hi_done.at(1) + n)
                    pool.tensor_tensor(v_lo[:, i, :], v_raw(i % 2), v_hi[:, i, :].bitcast(F32), ALU.subtract
                                       ).then_inc(v_lo_done.sem, 1)
                over_blocks(pool, u_low, step)

            @block.tensor
            def _(pe):
                pe.sem_inc(c.mm_done.sem, 2)
                pe.sem_inc(sum_done.sem, 2 * DT)

                def with_u(n, r):
                    pe.wait_ge(c.lo_done.sem, c.lo_done.at(3) + n)
                    pe.wait_ge(c.act_done.sem, c.act_done.at(1) + n)
                    for k in range(DT):
                        at = slice(k * P, (k + 1) * P)
                        mm = passes(pe, c.ps[:, r, :], u_half(c.w_hi, r)[:, at], u_half(c.w_lo, r)[:, at],
                                    c.h_hi[:, k, :], c.h_lo[:, k, :], k == 0, k == DT - 1)
                    mm.then_inc(c.mm_done.sem, 1)

                def step(n, i, g, more):
                    if more:
                        with_u(n + 1, 1 - i % 2)
                    if i % GI < GI - 1:
                        return
                    pe.wait_ge(v_lo_done.sem, v_lo_done.at(2 + GI) + g * GI)
                    for k in range(DT):
                        at = slice(k * P, (k + 1) * P)
                        pe.wait_ge(sum_free.sem, sum_free.at(1 + k) + g * DT)
                        for j in range(GI):
                            if k == 0:
                                pe.wait_ge(w_lo_done.sem, w_lo_done.at(1 + j) + g * GI)
                            slot = i - (GI - 1) + j
                            mm = passes(pe, c.ps[:, 2 + k % 4, :], v_hi[:, slot, at], v_lo[:, slot, at],
                                        w_hi[:, slot, :], w_lo[:, slot, :], j == 0, j == GI - 1)
                        mm.then_inc(sum_done.sem, 1)
                over_blocks(pe, with_u, step)

            @block.vector
            def _(dve):
                dve.sem_inc(gated.sem, 2)
                dve.sem_inc(sum_free.sem, 4)
                with dve.Fori(0, P // BODY) as p:
                    for i in range(BODY):
                        r, n, g = i % 2, p * BODY + i, p * 2 + i // GI
                        dve.wait_ge(c.act_done.sem, c.act_done.at(3) + n)
                        dve.wait_ge(g_loaded[r].sem, g_loaded[r].at(16 - 8 * r) + n * 8)
                        dve.tensor_tensor(gelu[:, r, :], gelu[:, r, :], gs[:, r, :], ALU.mult
                                          ).then_inc(c.i_ready.sem, 1)
                        dve.wait_ge(c.i_ready.sem, c.i_ready.at(1) + n)
                        dve.wait_ge(sum_done.sem, sum_done.at(DT) + g * DT)
                        dve.tensor_copy(w_hi[:, i, :], gelu[:, r, :]).then_inc(w_hi_done.sem, 1)
                        dve.wait_ge(w_hi_done.sem, w_hi_done.at(1) + n)
                        dve.tensor_tensor(w_lo[:, i, :], gelu[:, r, :], w_hi[:, i, :].bitcast(F32), ALU.subtract
                                          ).then_inc(w_lo_done.sem, 1)
                        dve.wait_ge(w_lo_done.sem, w_lo_done.at(1) + n)
                        dve.sem_inc(gated.sem, 1)
                        if i % GI < GI - 1:
                            continue
                        for k in range(DT):
                            dve.wait_ge(sum_done.sem, sum_done.at(2 * DT + 1 + k) + g * DT)
                            dve.tensor_tensor(c.xT[:, k, :], c.xT[:, k, :], c.ps[:, 2 + k % 4, :], ALU.add
                                              ).then_inc(sum_free.sem, 1)
                dve.wait_ge(sum_free.sem, sum_free.at(4 + groups * DT))
    for t, n in ((u_loaded[0], 8 * P), (u_loaded[1], 8 * P), (g_loaded[0], 8 * P), (g_loaded[1], 8 * P),
                 (v_loaded[0], 8 * P), (v_loaded[1], 8 * P), (c.hi_done, P), (c.lo_done, P + 2),
                 (v_hi_done, P), (v_lo_done, P + 2), (gated, P + 2), (c.i_ready, P), (w_hi_done, P), (w_lo_done, P),
                 (c.act_done, P + 2), (c.mm_done, P + 2), (sum_done, (groups + 2) * DT),
                 (sum_free, groups * DT + 4)):
        t.close(n)


def peer(c):
    x, hh, hl = (lambda k: c.xT[:, k, :]), (lambda k: c.h_hi[:, k, :]), (lambda k: c.h_lo[:, k, :])
    norm(c, 1, DT, x, None, D, weight=lambda k: c.col("norm_ffn_w_2", k), halves=(hh, hl),
         then=first_pieces(c.dram["w_peer_q"]))
    with ExitStack() as ctx:
        IT = c.sb(ctx, "index_i", [P, T])
        JT = c.sb(ctx, "index_j", [P, T])
        GT = c.sb(ctx, "gate", [P, T])
        peer_choose(c, hh, hl, IT, JT, GT)
        peer_gates(c, IT, JT, GT)
    peer_experts(c)


def build(nc, dram, out):
    with ExitStack() as ctx:
        c = Core(nc, ctx, dram)
        start(c, dram["x"])
        even_layer(c)
        swiglu(c, 0)
        mla(c)
        swiglu(c, 1)
        mix2(c)
        peer(c)
        x = lambda k: c.xT[:, k, :]
        norm(c, 1, DT, x, x, D, weight=lambda k: c.col("final_norm_w_2", k))
        with nc.Block() as block:
            @block.sync
            def _(sp):
                sp.dma_start(out, c.xT[:]).then_inc(c.stored.sem, 16)
                sp.wait_ge(c.stored.sem, c.stored.at(16))


def tiles_of(w):
    k, n = w.shape
    return np.ascontiguousarray(w.reshape(k // P, P, n // P, P).transpose(2, 1, 0, 3)).reshape(n // P, P, k)


def wide_tiles_of(w):
    k, n = w.shape
    return np.ascontiguousarray(w.reshape(k // P, P, n // T, T).transpose(2, 1, 0, 3)).reshape(n // T, P, k * 4)


def column(v):
    return v.reshape(-1, P).T


def layout(i):
    out = {}
    out["x"] = i["x"][0].T.reshape(DT, P, T).transpose(1, 0, 2)
    w = i["w_in_even"][0]
    dt_w, gk_w = w[:, 2560:2576], w[:, 5648:5664]
    out["w_small"] = tiles_of(np.concatenate([dt_w, dt_w, gk_w, gk_w] * 2, axis=1))
    out["w_ssd"] = tiles_of(w[:, 0:2560])
    out["w_gla"] = tiles_of(np.concatenate([w[:, 2576:3600], w[:, 4624:5648]], axis=1))
    out["w_v_even"] = wide_tiles_of(w[:, 3600:4624])
    out["gla_gk_w2"] = i["gla_gk_w2"][0]
    out["w_out_even"] = tiles_of(i["w_out_even"][0][0:D])
    out["w_out_even2"] = tiles_of(i["w_out_even"][0][D:2 * D])
    gu = [[tiles_of(i[n][l]) for n in ("w_gate", "w_up")] for l in range(2)]
    out["w_gate_up"] = np.stack([np.concatenate(p, axis=2) for p in gu])
    for l in range(2):
        out[f"w_down{l}"] = tiles_of(i["w_down"][l])
    dq = i["w_dqkv"][0]
    out["w_dqkv"] = tiles_of(np.concatenate([dq[:, 0:640]] + 4 * [dq[:, 640:672]], axis=1))
    uq = i["w_uq"][0].reshape(384, 16, 96)
    out["w_uq"] = tiles_of(np.concatenate([uq[:, :, 0:64].reshape(384, 1024), uq[:, :, 64:96].reshape(384, 512)], axis=1))
    ukv = i["w_ukv"][0].reshape(256, 16, 128)
    out["w_uk"] = tiles_of(ukv[:, :, 0:64].reshape(256, 1024))
    out["w_uv"] = wide_tiles_of(ukv[:, :, 64:128].reshape(256, 1024))
    out["w_o"] = tiles_of(i["w_o_mla"][0])
    w = i["w_in_2"][0]
    out["w_hg"] = tiles_of(np.concatenate([w[:, 0:2048], w[:, 3072:4096]], axis=1))
    out["w_hg_v"] = wide_tiles_of(w[:, 2048:3072])
    rq, rk = (w[:, a:a + 1024].reshape(D, 4, 256) for a in (4096, 5120))
    out["w_ret"] = tiles_of(np.stack([rq, rk], axis=2).reshape(D, 2048))
    out["w_ret_g"] = tiles_of(w[:, 8192:10240])
    out["w_ret_v"] = wide_tiles_of(w[:, 6144:8192])
    out["w_gates"] = tiles_of(w[:, 10240:12288])
    out["w_branch_hg"] = tiles_of(i["w_branch_hg_2"][0])
    out["w_branch_ret0"] = tiles_of(i["w_branch_ret_2"][0][0:D])
    out["w_branch_ret1"] = tiles_of(i["w_branch_ret_2"][0][D:2 * D])
    out["w_out_2"] = tiles_of(i["w_out_2"][0])
    out["w_peer_q"] = tiles_of(i["peer_w_q_2"][0])
    out["peer_keys"] = i["peer_sub_keys_2"][0].transpose(3, 0, 1, 2).reshape(P, 2048)
    out["expert_u"] = tiles_of(i["expert_u_2"][0].T)
    out["expert_v"] = i["expert_v_2"][0].reshape(P, P, D)
    cols = {
        "mix_norm_even": column(i["mix_norm_even"][0]),
        "conv_w": i["conv_w"][0].reshape(4, CONVT, P).transpose(2, 1, 0).reshape(P, 48),
        "conv_b": column(i["conv_b"][0]),
        "dt_bias": np.tile(i["dt_bias"][0], 8)[:, None], "a_log": np.tile(i["a_log"][0], 8)[:, None],
        "d_skip": column(np.repeat(i["d_skip"][0], 64)),
        "ssd_norm": column(i["ssd_norm"][0]), "gla_gk_b": column(i["gla_gk_b"][0]),
        "gla_norm": column(i["gla_norm"][0]), "mix_norm_odd": column(i["mix_norm_odd"][0]),
        "q_lora_norm": column(i["q_lora_norm"][0]), "kv_lora_norm": column(i["kv_lora_norm"][0]),
        "q_nope_norm": np.tile(i["q_nope_norm"][0], 2)[:, None],
        "q_rope_norm": np.tile(i["q_rope_norm"][0], 4)[:, None],
        "k_nope_norm": np.tile(i["k_nope_norm"][0], 2)[:, None],
        "k_rope_norm": np.tile(i["k_rope_norm"][0], 4)[:, None],
        "ffn_norm0": column(i["ffn_norm"][0]), "ffn_norm1": column(i["ffn_norm"][1]),
        "norm_mix_w_2": column(i["norm_mix_w_2"][0]),
        "lb0": column(i["hg_lower_bounds_2"][0]), "lb1": column(i["hg_lower_bounds_2"][1]),
        "hg_norm_w_2": column(i["hg_norm_w_2"][0]), "norm_ffn_w_2": column(i["norm_ffn_w_2"][0]),
        "final_norm_w_2": column(i["final_norm_w_2"]),
    }
    out["cols"] = np.concatenate([cols[k] for k in COL_AT], axis=1)
    out["consts"] = np.concatenate(list(const_table().values()), axis=1)
    out["level_masks"] = level_masks()
    return {k: np.ascontiguousarray(v) for k, v in out.items()}


def kernel(**inputs):
    import concourse.bacc as bacc
    from concourse.bass_utils import run_bass_kernel_spmd

    nc = bacc.Bacc("TRN2", target_bir_lowering=False, num_devices=1)
    arrays = {f"in_{k}": v for k, v in layout({k: np.asarray(v) for k, v in inputs.items()}).items()}
    dram = {k[3:]: nc.dram_tensor(k, v.shape, mybir.dt.from_np(v.dtype), kind="ExternalInput").ap()
            for k, v in arrays.items()}
    dram["gates"] = nc.dram_tensor("gates", [P, NCH, P, P], F32, kind="Internal").ap()
    out = nc.dram_tensor("out", [P, DT, T], F32, kind="ExternalOutput").ap()
    build(nc, dram, out)
    r = run_bass_kernel_spmd(nc, [arrays], core_ids=[0])
    got = r.results[0]["out"]
    return np.ascontiguousarray(got.transpose(1, 0, 2).reshape(D, T).T)[None]
```
